# Optimizing a Trainium2 kernel written in Bass

```python
import jax, jax.numpy as jnp
from jax import lax
import numpy as np

D_MODEL = 1024
BATCH = 1
SEQ = 256
DEPTH = 1

PLE_DIM = 256
GDN_HEADS = 4
GDN_DK = 128
GDN_DV = 128
CONV_WIDTH = 4
MLSTM_HEADS = 4
MLSTM_DQK = 64
MLSTM_DV = 128
CHUNK = 64
D_FF = -(-(8 * D_MODEL) // (3 * 256)) * 256
GDN_QK = GDN_HEADS * GDN_DK
GDN_V = GDN_HEADS * GDN_DV
ML_QK = MLSTM_HEADS * MLSTM_DQK
ML_V = MLSTM_HEADS * MLSTM_DV
IN_SIZES = (GDN_QK, GDN_QK, GDN_V, GDN_V, GDN_HEADS, GDN_HEADS,
            ML_QK, ML_QK, ML_V, ML_V, MLSTM_HEADS, MLSTM_HEADS,
            D_MODEL, D_MODEL)
IN_WIDTH = 2 * GDN_QK + 2 * GDN_V + 2 * GDN_HEADS + 2 * ML_QK + 2 * ML_V + 2 * MLSTM_HEADS + 2 * D_MODEL
CONV_CH = 2 * GDN_QK + GDN_V
NORM_EPS = 1e-6


def _rmsnorm(x, gain):
    xf = x.astype(jnp.float32)
    y = xf * lax.rsqrt(jnp.mean(xf * xf, axis=-1, keepdims=True) + NORM_EPS)
    return (y * gain.astype(jnp.float32)).astype(x.dtype)

def _l2norm(x):
    return x * lax.rsqrt(jnp.sum(x * x, axis=-1, keepdims=True) + NORM_EPS)

def _causal_conv(x, w):
    c = x.shape[-1]
    return lax.conv_general_dilated(x, w[:, None, :].astype(x.dtype), window_strides=(1,),
                                    padding=[(CONV_WIDTH - 1, 0)],
                                    dimension_numbers=('NWC', 'WIO', 'NWC'),
                                    feature_group_count=c)

def _chunk_seq(t):
    b, s, h, d = t.shape
    return t.reshape(b, s // CHUNK, CHUNK, h, d).transpose(1, 0, 3, 2, 4)

def _chunk_gate(t):
    b, s, h = t.shape
    return t.reshape(b, s // CHUNK, CHUNK, h).transpose(1, 0, 3, 2)

def _unchunk(t):
    n, b, h, c, d = t.shape
    return t.transpose(1, 0, 3, 2, 4).reshape(b, n * c, h, d)

def gated_delta_rule(q, k, v, g, beta):
    dk = q.shape[-1]
    dv = v.shape[-1]
    q = _l2norm(q) * (dk ** -0.5)
    k = _l2norm(k)
    qc, kc, vc = _chunk_seq(q), _chunk_seq(k), _chunk_seq(v)
    gc = jnp.cumsum(_chunk_gate(g), axis=-1)
    bc = _chunk_gate(beta)
    incl = jnp.tril(jnp.ones((CHUNK, CHUNK), dtype=bool))
    strict = jnp.tril(jnp.ones((CHUNK, CHUNK), dtype=bool), -1)
    decay = jnp.exp(jnp.where(incl, gc[..., :, None] - gc[..., None, :], -jnp.inf))
    k_beta = kc * bc[..., None]
    m = jnp.where(strict, jnp.einsum('nbhcd,nbhsd->nbhcs', k_beta, kc) * decay, 0.0)
    a = m + jnp.eye(CHUNK, dtype=m.dtype)
    rhs = jnp.concatenate([vc * bc[..., None], k_beta * jnp.exp(gc)[..., None]], axis=-1)
    sol = lax.linalg.triangular_solve(a, rhs, left_side=True, lower=True, unit_diagonal=True)
    u, w = sol[..., :dv], sol[..., dv:]
    attn = jnp.einsum('nbhcd,nbhsd->nbhcs', qc, kc) * decay
    g_last = gc[..., -1]

    def step(state, inp):
        q_i, k_i, u_i, w_i, g_i, gl_i, attn_i = inp
        v_new = u_i - jnp.einsum('bhcd,bhde->bhce', w_i, state)
        o = (jnp.einsum('bhcd,bhde->bhce', q_i * jnp.exp(g_i)[..., None], state)
             + jnp.einsum('bhcs,bhse->bhce', attn_i, v_new))
        k_dec = k_i * jnp.exp(gl_i[..., None] - g_i)[..., None]
        state = state * jnp.exp(gl_i)[..., None, None] + jnp.einsum('bhcd,bhce->bhde', k_dec, v_new)
        return state, o

    init = jnp.zeros(qc.shape[1:3] + (dk, dv), jnp.float32)
    _, out = lax.scan(step, init, (qc, kc, u, w, gc, g_last, attn))
    return _unchunk(out)

def mlstm_chunkwise(q, k, v, i_pre, f_pre):
    dqk = q.shape[-1]
    qc = _chunk_seq(q * (dqk ** -0.5))
    kc, vc = _chunk_seq(k), _chunk_seq(v)
    ic = _chunk_gate(i_pre)
    bc = jnp.cumsum(_chunk_gate(jax.nn.log_sigmoid(f_pre)), axis=-1)
    incl = jnp.tril(jnp.ones((CHUNK, CHUNK), dtype=bool))

    def step(carry, inp):
        c_bar, n_bar, m = carry
        q_i, k_i, v_i, i_i, b_i = inp
        d_log = jnp.where(incl, b_i[..., :, None] - b_i[..., None, :] + i_i[..., None, :], -jnp.inf)
        m_inter = b_i + m[..., None]
        m_t = jnp.maximum(m_inter, jnp.max(d_log, axis=-1))
        w_inter = jnp.exp(m_inter - m_t)
        s = jnp.einsum('bhcd,bhsd->bhcs', q_i, k_i) * jnp.exp(d_log - m_t[..., None])
        num = (w_inter[..., None] * jnp.einsum('bhcd,bhde->bhce', q_i, c_bar)
               + jnp.einsum('bhcs,bhse->bhce', s, v_i))
        den = w_inter * jnp.einsum('bhcd,bhd->bhc', q_i, n_bar) + jnp.sum(s, axis=-1)
        h = num / jnp.maximum(jnp.abs(den), jnp.exp(-m_t))[..., None]
        b_last = b_i[..., -1]
        a_i = b_last[..., None] - b_i + i_i
        m_new = jnp.maximum(b_last + m, jnp.max(a_i, axis=-1))
        scale_prev = jnp.exp(b_last + m - m_new)
        k_w = k_i * jnp.exp(a_i - m_new[..., None])[..., None]
        c_bar = scale_prev[..., None, None] * c_bar + jnp.einsum('bhcd,bhce->bhde', k_w, v_i)
        n_bar = scale_prev[..., None] * n_bar + jnp.sum(k_w, axis=-2)
        return (c_bar, n_bar, m_new), h

    nb, bb, hh = qc.shape[0], qc.shape[1], qc.shape[2]
    init = (jnp.zeros((bb, hh, dqk, vc.shape[-1]), jnp.float32),
            jnp.zeros((bb, hh, dqk), jnp.float32),
            jnp.zeros((bb, hh), jnp.float32))
    _, out = lax.scan(step, init, (qc, kc, vc, ic, bc))
    return _unchunk(out)

def _head_rmsnorm(x, gain):
    return x * lax.rsqrt(jnp.mean(x * x, axis=-1, keepdims=True) + NORM_EPS) * gain.astype(jnp.float32)

def _layer(x, p_i, g_mix, w_in, conv_w, a_log, dt_bias, gdn_norm, ml_i_bias, ml_f_bias, ml_norm,
           w_branch_a, w_branch_b, w_out, g_ffn, w1, w3, w2, g_ple, w_ple_gate, w_ple):
    bsz, seq, _ = x.shape
    dt = x.dtype
    h = _rmsnorm(x, g_mix)
    proj = h @ w_in
    idx = [int(v) for v in np.cumsum(IN_SIZES)[:-1]]
    (gq, gk, gv, gz, gbeta, galpha, mq, mk, mv, mo, mi, mf, gate_a, gate_b) = jnp.split(proj, idx, axis=-1)

    qkv = jax.nn.silu(_causal_conv(jnp.concatenate([gq, gk, gv], axis=-1), conv_w))
    gq, gk, gv = jnp.split(qkv.astype(jnp.float32), [GDN_QK, 2 * GDN_QK], axis=-1)
    beta = jax.nn.sigmoid(gbeta.astype(jnp.float32))
    g = -jnp.exp(a_log.astype(jnp.float32)) * jax.nn.softplus(galpha.astype(jnp.float32) + dt_bias.astype(jnp.float32))
    o_a = gated_delta_rule(gq.reshape(bsz, seq, GDN_HEADS, GDN_DK),
                           gk.reshape(bsz, seq, GDN_HEADS, GDN_DK),
                           gv.reshape(bsz, seq, GDN_HEADS, GDN_DV), g, beta)
    o_a = _head_rmsnorm(o_a, gdn_norm) * jax.nn.silu(gz.astype(jnp.float32)).reshape(bsz, seq, GDN_HEADS, GDN_DV)
    y_a = o_a.reshape(bsz, seq, GDN_V).astype(dt) @ w_branch_a

    o_b = mlstm_chunkwise(mq.astype(jnp.float32).reshape(bsz, seq, MLSTM_HEADS, MLSTM_DQK),
                          mk.astype(jnp.float32).reshape(bsz, seq, MLSTM_HEADS, MLSTM_DQK),
                          mv.astype(jnp.float32).reshape(bsz, seq, MLSTM_HEADS, MLSTM_DV),
                          mi.astype(jnp.float32) + ml_i_bias.astype(jnp.float32),
                          mf.astype(jnp.float32) + ml_f_bias.astype(jnp.float32))
    o_b = _head_rmsnorm(o_b, ml_norm) * jax.nn.sigmoid(mo.astype(jnp.float32)).reshape(bsz, seq, MLSTM_HEADS, MLSTM_DV)
    y_b = o_b.reshape(bsz, seq, ML_V).astype(dt) @ w_branch_b

    mixed = jax.nn.sigmoid(gate_a) * y_a + jax.nn.sigmoid(gate_b) * y_b
    x = x + mixed @ w_out

    h = _rmsnorm(x, g_ffn)
    x = x + (jax.nn.silu(h @ w1) * (h @ w3)) @ w2

    gate = jax.nn.sigmoid(_rmsnorm(x, g_ple) @ w_ple_gate)
    x = x + gate * (p_i @ w_ple)
    return x

def first_inputs(seed: int = 0) -> dict:
    key = jax.random.key(seed)
    ks = jax.random.split(key, 24)
    f32 = jnp.float32
    L, D = DEPTH, D_MODEL

    def nrm(k, shape, scale):
        return jax.random.normal(k, shape, f32) * scale

    def gain(k, shape):
        return 1.0 + 0.05 * jax.random.normal(k, shape, f32)

    dt0 = jnp.exp(jax.random.uniform(ks[5], (L, GDN_HEADS), f32, np.log(1e-3), np.log(1e-1)))
    return {
        'x': jax.random.normal(ks[0], (BATCH, SEQ, D), f32),
        'p': jax.random.normal(ks[1], (DEPTH, BATCH, SEQ, PLE_DIM), f32),
        'g_mix': gain(ks[2], (L, D)),
        'w_in': nrm(ks[3], (L, D, IN_WIDTH), D ** -0.5),
        'conv_w': nrm(ks[4], (L, CONV_WIDTH, CONV_CH), CONV_WIDTH ** -0.5),
        'a_log': jnp.log(jax.random.uniform(ks[6], (L, GDN_HEADS), f32, 1.0, 16.0)),
        'dt_bias': dt0 + jnp.log(-jnp.expm1(-dt0)),
        'gdn_norm': gain(ks[7], (L, GDN_DV)),
        'ml_i_bias': nrm(ks[8], (L, MLSTM_HEADS), 0.1),
        'ml_f_bias': jnp.linspace(3.0, 6.0, MLSTM_HEADS, dtype=f32)[None, :] + nrm(ks[9], (L, MLSTM_HEADS), 0.1),
        'ml_norm': gain(ks[10], (L, MLSTM_HEADS, MLSTM_DV)),
        'w_branch_a': nrm(ks[11], (L, GDN_V, D), GDN_V ** -0.5),
        'w_branch_b': nrm(ks[12], (L, ML_V, D), ML_V ** -0.5),
        'w_out': nrm(ks[13], (L, D, D), D ** -0.5),
        'g_ffn': gain(ks[14], (L, D)),
        'w1': nrm(ks[15], (L, D, D_FF), D ** -0.5),
        'w3': nrm(ks[16], (L, D, D_FF), D ** -0.5),
        'w2': nrm(ks[17], (L, D_FF, D), D_FF ** -0.5),
        'g_ple': gain(ks[18], (L, D)),
        'w_ple_gate': nrm(ks[19], (L, D, D), D ** -0.5),
        'w_ple': nrm(ks[20], (L, PLE_DIM, D), PLE_DIM ** -0.5),
        'g_final': gain(ks[21], (D,)),
    }

def first_block(x, p, g_mix, w_in, conv_w, a_log, dt_bias, gdn_norm, ml_i_bias, ml_f_bias, ml_norm,
              w_branch_a, w_branch_b, w_out, g_ffn, w1, w3, w2, g_ple, w_ple_gate, w_ple, g_final):
    for i in range(DEPTH):
        x = _layer(x, p[i], g_mix[i], w_in[i], conv_w[i], a_log[i], dt_bias[i], gdn_norm[i],
                   ml_i_bias[i], ml_f_bias[i], ml_norm[i], w_branch_a[i], w_branch_b[i], w_out[i],
                   g_ffn[i], w1[i], w3[i], w2[i], g_ple[i], w_ple_gate[i], w_ple[i])
    return _rmsnorm(x, g_final)


DEPTH_2 = 2

N_MIXERS = 2
D_RNN = 128 * round(4 * D_MODEL / (3 * 128))
LRU_BLOCKS = 16
LRU_BLOCK = D_RNN // LRU_BLOCKS
LRU_C = 8.0
FOX_HEADS = 16
FOX_HEAD_DIM = D_MODEL // FOX_HEADS
QUERY_BLOCK = 128
PEER_HEADS = 8
PEER_KEYS = 128
PEER_EXPERTS = PEER_KEYS * PEER_KEYS
PEER_TOPK = 16
PEER_QDIM = 256
PEER_HALF = PEER_QDIM // 2
TOKEN_CHUNK = 128


def rms_norm(x, g):
    xf = x.astype(jnp.float32)
    y = xf * lax.rsqrt(jnp.mean(xf * xf, axis=-1, keepdims=True) + NORM_EPS)
    return (y * g.astype(jnp.float32)).astype(x.dtype)

def ada_modulation(c, w, b):
    mod = jax.nn.silu(c) @ w + b
    shift, scale, gate = jnp.split(mod, 3, axis=-1)
    return shift[:, None, :], scale[:, None, :], gate[:, None, :]

def causal_depthwise_conv(x, w, b):
    y = lax.conv_general_dilated(x, w[:, None, :], window_strides=(1,), padding=[(CONV_WIDTH - 1, 0)], dimension_numbers=('NWC', 'WIO', 'NWC'), feature_group_count=x.shape[-1])
    return y + b

def _linear_recurrence_combine(left, right):
    a_l, b_l = left
    a_r, b_r = right
    return a_l * a_r, a_r * b_l + b_r

def rglru_mixer(h, in_w, conv_w, conv_b, ra_w, ra_b, ri_w, ri_b, lam, out_w):
    B, S, _ = h.shape
    xb, gb = jnp.split(h @ in_w, 2, axis=-1)
    xb = causal_depthwise_conv(xb, conv_w, conv_b)
    xblk = xb.reshape(B, S, LRU_BLOCKS, LRU_BLOCK)
    r = jax.nn.sigmoid(jnp.einsum('bsnc,ncd->bsnd', xblk, ra_w).reshape(B, S, D_RNN) + ra_b)
    i = jax.nn.sigmoid(jnp.einsum('bsnc,ncd->bsnd', xblk, ri_w).reshape(B, S, D_RNN) + ri_b)
    log_a = -LRU_C * jax.nn.softplus(-lam.astype(jnp.float32)) * r.astype(jnp.float32)
    a = jnp.exp(log_a)
    u = jnp.sqrt(-jnp.expm1(2.0 * log_a)) * (i * xb).astype(jnp.float32)
    _, hs = lax.associative_scan(_linear_recurrence_combine, (a, u), axis=1)
    y = hs.astype(h.dtype) * jax.nn.gelu(gb, approximate=False)
    return y @ out_w

def fox_mixer(h, in_w, f_b, q_norm_g, k_norm_g, out_w):
    B, S, D = h.shape
    H, E = FOX_HEADS, FOX_HEAD_DIM
    n_blk = S // QUERY_BLOCK
    q, k, v, f_logit, og = jnp.split(h @ in_w, [D, 2 * D, 3 * D, 3 * D + H], axis=-1)
    q = rms_norm(q.reshape(B, S, H, E), q_norm_g)
    k = rms_norm(k.reshape(B, S, H, E), k_norm_g)
    v = v.reshape(B, S, H, E)
    log_f = jax.nn.log_sigmoid(f_logit.astype(jnp.float32) + f_b.astype(jnp.float32))
    cum = jnp.cumsum(log_f, axis=1).transpose(0, 2, 1)
    q_blocks = q.reshape(B, n_blk, QUERY_BLOCK, H, E).transpose(1, 0, 3, 2, 4)
    cum_blocks = cum.reshape(B, H, n_blk, QUERY_BLOCK).transpose(2, 0, 1, 3)
    pos_blocks = jnp.arange(S, dtype=jnp.int32).reshape(n_blk, QUERY_BLOCK)
    key_pos = jnp.arange(S, dtype=jnp.int32)
    scale = E ** -0.5

    def attend_block(args):
        qb, cq, qpos = args
        s = jnp.einsum('bhqe,bkhe->bhqk', qb, k).astype(jnp.float32) * scale
        s = s + cq[..., None] - cum[:, :, None, :]
        s = jnp.where(qpos[:, None] >= key_pos[None, :], s, -jnp.inf)
        p = jax.nn.softmax(s, axis=-1)
        return jnp.einsum('bhqk,bkhe->bqhe', p.astype(v.dtype), v)

    o = lax.map(attend_block, (q_blocks, cum_blocks, pos_blocks))
    o = o.transpose(1, 0, 2, 3, 4).reshape(B, S, H, E)
    o = o * jax.nn.sigmoid(og).reshape(B, S, H, E)
    return o.reshape(B, S, D) @ out_w

def peer_ffn(h, q_w, subkey1, subkey2, expert_u, expert_v):
    B, S, D = h.shape
    chunks = h.reshape(B * S // TOKEN_CHUNK, TOKEN_CHUNK, D)

    def retrieve_chunk(xc):
        q = (xc @ q_w).reshape(TOKEN_CHUNK, PEER_HEADS, 2, PEER_HALF)
        s1 = jnp.einsum('thd,hnd->thn', q[:, :, 0], subkey1).astype(jnp.float32)
        s2 = jnp.einsum('thd,hnd->thn', q[:, :, 1], subkey2).astype(jnp.float32)
        v1, i1 = lax.top_k(s1, PEER_TOPK)
        v2, i2 = lax.top_k(s2, PEER_TOPK)
        cand = (v1[..., :, None] + v2[..., None, :]).reshape(TOKEN_CHUNK, PEER_HEADS, PEER_TOPK * PEER_TOPK)
        top_s, top_c = lax.top_k(cand, PEER_TOPK)
        e1 = jnp.take_along_axis(i1, top_c // PEER_TOPK, axis=-1)
        e2 = jnp.take_along_axis(i2, top_c % PEER_TOPK, axis=-1)
        expert = e1 * PEER_KEYS + e2
        g = jax.nn.softmax(top_s, axis=-1)
        u = jnp.take(expert_u, expert, axis=0)
        act = jax.nn.gelu(jnp.einsum('thkd,td->thk', u, xc).astype(jnp.float32), approximate=False)
        w = (g * act).astype(xc.dtype)
        return jnp.einsum('thk,thkd->td', w, jnp.take(expert_v, expert, axis=0))

    return lax.map(retrieve_chunk, chunks).reshape(B, S, D)

def _mod_params(nrm):
    return nrm((D_MODEL, 3 * D_MODEL), 0.5 * D_MODEL ** -0.5), nrm((3 * D_MODEL,), 0.02)

def second_inputs(seed: int = 0) -> dict:
    key = jax.random.key(seed)
    ks = iter(jax.random.split(key, 64))

    def nrm(shape, scale):
        return jax.random.normal(next(ks), shape, jnp.float32) * scale

    def gain(n):
        return 1.0 + nrm((n,), 0.05)

    def peer_params():
        return (nrm((D_MODEL, PEER_HEADS * PEER_QDIM), D_MODEL ** -0.5),
                nrm((PEER_HEADS, PEER_KEYS, PEER_HALF), PEER_HALF ** -0.5),
                nrm((PEER_HEADS, PEER_KEYS, PEER_HALF), PEER_HALF ** -0.5),
                nrm((PEER_EXPERTS, D_MODEL), D_MODEL ** -0.5),
                nrm((PEER_EXPERTS, D_MODEL), PEER_HEADS ** -0.5))

    x = nrm((BATCH, SEQ, D_MODEL), 1.0)
    c = nrm((BATCH, D_MODEL), 1.0)
    l0_mix_norm_g = gain(D_MODEL)
    l0_mix_mod_w, l0_mix_mod_b = _mod_params(nrm)
    l0_lru_in_w = nrm((D_MODEL, 2 * D_RNN), D_MODEL ** -0.5)
    l0_lru_conv_w = nrm((CONV_WIDTH, D_RNN), CONV_WIDTH ** -0.5)
    l0_lru_conv_b = nrm((D_RNN,), 0.02)
    l0_lru_ra_w = nrm((LRU_BLOCKS, LRU_BLOCK, LRU_BLOCK), LRU_BLOCK ** -0.5)
    l0_lru_ra_b = nrm((D_RNN,), 0.02)
    l0_lru_ri_w = nrm((LRU_BLOCKS, LRU_BLOCK, LRU_BLOCK), LRU_BLOCK ** -0.5)
    l0_lru_ri_b = nrm((D_RNN,), 0.02)
    a_pow_c = jax.random.uniform(next(ks), (D_RNN,), jnp.float32, minval=0.9, maxval=0.999)
    a0 = a_pow_c ** (1.0 / LRU_C)
    l0_lru_lambda = jnp.log(a0) - jnp.log1p(-a0)
    l0_lru_out_w = nrm((D_RNN, D_MODEL), D_RNN ** -0.5)
    l0_ffn_norm_g = gain(D_MODEL)
    l0_ffn_mod_w, l0_ffn_mod_b = _mod_params(nrm)
    l0_peer_q_w, l0_peer_subkey1, l0_peer_subkey2, l0_peer_u, l0_peer_v = peer_params()
    l1_mix_norm_g = gain(D_MODEL)
    l1_mix_mod_w, l1_mix_mod_b = _mod_params(nrm)
    l1_fox_in_w = nrm((D_MODEL, 4 * D_MODEL + FOX_HEADS), D_MODEL ** -0.5)
    l1_fox_f_b = jax.random.uniform(next(ks), (FOX_HEADS,), jnp.float32, minval=1.0, maxval=6.0)
    l1_fox_q_norm_g = gain(FOX_HEAD_DIM)
    l1_fox_k_norm_g = gain(FOX_HEAD_DIM)
    l1_fox_out_w = nrm((D_MODEL, D_MODEL), D_MODEL ** -0.5)
    l1_ffn_norm_g = gain(D_MODEL)
    l1_ffn_mod_w, l1_ffn_mod_b = _mod_params(nrm)
    l1_peer_q_w, l1_peer_subkey1, l1_peer_subkey2, l1_peer_u, l1_peer_v = peer_params()
    return {'x': x, 'c': c,
            'l0_mix_norm_g': l0_mix_norm_g, 'l0_mix_mod_w': l0_mix_mod_w, 'l0_mix_mod_b': l0_mix_mod_b,
            'l0_lru_in_w': l0_lru_in_w, 'l0_lru_conv_w': l0_lru_conv_w, 'l0_lru_conv_b': l0_lru_conv_b,
            'l0_lru_ra_w': l0_lru_ra_w, 'l0_lru_ra_b': l0_lru_ra_b, 'l0_lru_ri_w': l0_lru_ri_w, 'l0_lru_ri_b': l0_lru_ri_b,
            'l0_lru_lambda': l0_lru_lambda, 'l0_lru_out_w': l0_lru_out_w,
            'l0_ffn_norm_g': l0_ffn_norm_g, 'l0_ffn_mod_w': l0_ffn_mod_w, 'l0_ffn_mod_b': l0_ffn_mod_b,
            'l0_peer_q_w': l0_peer_q_w, 'l0_peer_subkey1': l0_peer_subkey1, 'l0_peer_subkey2': l0_peer_subkey2,
            'l0_peer_u': l0_peer_u, 'l0_peer_v': l0_peer_v,
            'l1_mix_norm_g': l1_mix_norm_g, 'l1_mix_mod_w': l1_mix_mod_w, 'l1_mix_mod_b': l1_mix_mod_b,
            'l1_fox_in_w': l1_fox_in_w, 'l1_fox_f_b': l1_fox_f_b, 'l1_fox_q_norm_g': l1_fox_q_norm_g,
            'l1_fox_k_norm_g': l1_fox_k_norm_g, 'l1_fox_out_w': l1_fox_out_w,
            'l1_ffn_norm_g': l1_ffn_norm_g, 'l1_ffn_mod_w': l1_ffn_mod_w, 'l1_ffn_mod_b': l1_ffn_mod_b,
            'l1_peer_q_w': l1_peer_q_w, 'l1_peer_subkey1': l1_peer_subkey1, 'l1_peer_subkey2': l1_peer_subkey2,
            'l1_peer_u': l1_peer_u, 'l1_peer_v': l1_peer_v}

def second_block(x, c,
              l0_mix_norm_g, l0_mix_mod_w, l0_mix_mod_b,
              l0_lru_in_w, l0_lru_conv_w, l0_lru_conv_b,
              l0_lru_ra_w, l0_lru_ra_b, l0_lru_ri_w, l0_lru_ri_b,
              l0_lru_lambda, l0_lru_out_w,
              l0_ffn_norm_g, l0_ffn_mod_w, l0_ffn_mod_b,
              l0_peer_q_w, l0_peer_subkey1, l0_peer_subkey2, l0_peer_u, l0_peer_v,
              l1_mix_norm_g, l1_mix_mod_w, l1_mix_mod_b,
              l1_fox_in_w, l1_fox_f_b, l1_fox_q_norm_g, l1_fox_k_norm_g, l1_fox_out_w,
              l1_ffn_norm_g, l1_ffn_mod_w, l1_ffn_mod_b,
              l1_peer_q_w, l1_peer_subkey1, l1_peer_subkey2, l1_peer_u, l1_peer_v):
    mix_norms = [(l0_mix_norm_g, l0_mix_mod_w, l0_mix_mod_b), (l1_mix_norm_g, l1_mix_mod_w, l1_mix_mod_b)]
    mixer_params = [(l0_lru_in_w, l0_lru_conv_w, l0_lru_conv_b, l0_lru_ra_w, l0_lru_ra_b, l0_lru_ri_w, l0_lru_ri_b, l0_lru_lambda, l0_lru_out_w),
                    (l1_fox_in_w, l1_fox_f_b, l1_fox_q_norm_g, l1_fox_k_norm_g, l1_fox_out_w)]
    ffn_norms = [(l0_ffn_norm_g, l0_ffn_mod_w, l0_ffn_mod_b), (l1_ffn_norm_g, l1_ffn_mod_w, l1_ffn_mod_b)]
    peer_params = [(l0_peer_q_w, l0_peer_subkey1, l0_peer_subkey2, l0_peer_u, l0_peer_v),
                   (l1_peer_q_w, l1_peer_subkey1, l1_peer_subkey2, l1_peer_u, l1_peer_v)]
    for layer in range(DEPTH_2):
        g, mw, mb = mix_norms[layer]
        shift, scale, gate = ada_modulation(c, mw, mb)
        h = rms_norm(x, g) * (1.0 + scale) + shift
        mixer = rglru_mixer if layer % N_MIXERS == 0 else fox_mixer
        x = x + gate * mixer(h, *mixer_params[layer])
        g, mw, mb = ffn_norms[layer]
        shift, scale, gate = ada_modulation(c, mw, mb)
        h = rms_norm(x, g) * (1.0 + scale) + shift
        x = x + gate * peer_ffn(h, *peer_params[layer])
    return x


def setup_inputs(seed=0):
    out = dict(first_inputs(seed))
    for name, value in second_inputs(seed + 1).items():
        if name != "x":
            out[name + "_2"] = value
    return out


def reference(
    x, p, g_mix, w_in, conv_w, a_log, dt_bias, gdn_norm, ml_i_bias, ml_f_bias, ml_norm,
    w_branch_a, w_branch_b, w_out, g_ffn, w1, w3, w2, g_ple, w_ple_gate, w_ple, g_final, c_2,
    l0_mix_norm_g_2, l0_mix_mod_w_2, l0_mix_mod_b_2, l0_lru_in_w_2, l0_lru_conv_w_2,
    l0_lru_conv_b_2, l0_lru_ra_w_2, l0_lru_ra_b_2, l0_lru_ri_w_2, l0_lru_ri_b_2,
    l0_lru_lambda_2, l0_lru_out_w_2, l0_ffn_norm_g_2, l0_ffn_mod_w_2, l0_ffn_mod_b_2,
    l0_peer_q_w_2, l0_peer_subkey1_2, l0_peer_subkey2_2, l0_peer_u_2, l0_peer_v_2,
    l1_mix_norm_g_2, l1_mix_mod_w_2, l1_mix_mod_b_2, l1_fox_in_w_2, l1_fox_f_b_2,
    l1_fox_q_norm_g_2, l1_fox_k_norm_g_2, l1_fox_out_w_2, l1_ffn_norm_g_2, l1_ffn_mod_w_2,
    l1_ffn_mod_b_2, l1_peer_q_w_2, l1_peer_subkey1_2, l1_peer_subkey2_2, l1_peer_u_2,
    l1_peer_v_2,
):
    x = first_block(
        x, p, g_mix, w_in, conv_w, a_log, dt_bias, gdn_norm, ml_i_bias, ml_f_bias, ml_norm,
        w_branch_a, w_branch_b, w_out, g_ffn, w1, w3, w2, g_ple, w_ple_gate, w_ple, g_final,
    )
    return second_block(
        x, c_2, l0_mix_norm_g_2, l0_mix_mod_w_2, l0_mix_mod_b_2, l0_lru_in_w_2, l0_lru_conv_w_2,
        l0_lru_conv_b_2, l0_lru_ra_w_2, l0_lru_ra_b_2, l0_lru_ri_w_2, l0_lru_ri_b_2,
        l0_lru_lambda_2, l0_lru_out_w_2, l0_ffn_norm_g_2, l0_ffn_mod_w_2, l0_ffn_mod_b_2,
        l0_peer_q_w_2, l0_peer_subkey1_2, l0_peer_subkey2_2, l0_peer_u_2, l0_peer_v_2,
        l1_mix_norm_g_2, l1_mix_mod_w_2, l1_mix_mod_b_2, l1_fox_in_w_2, l1_fox_f_b_2,
        l1_fox_q_norm_g_2, l1_fox_k_norm_g_2, l1_fox_out_w_2, l1_ffn_norm_g_2, l1_ffn_mod_w_2,
        l1_ffn_mod_b_2, l1_peer_q_w_2, l1_peer_subkey1_2, l1_peer_subkey2_2, l1_peer_u_2,
        l1_peer_v_2,
    )


_drawn_inputs = setup_inputs


def setup_inputs(seed=0):
    import zlib

    import numpy as np

    out = dict(_drawn_inputs(seed))
    spreads = {}
    factors = {'gdn_norm': 2.963,
     'ml_i_bias': 64.0,
     'ml_norm': 3.13,
     'g_ple': 5.319,
     'l0_mix_norm_g_2': 3.135,
     'l0_lru_conv_b_2': 2.8,
     'l0_lru_ra_b_2': 8.0,
     'l0_lru_ri_b_2': 8.0,
     'l0_ffn_norm_g_2': 3.676,
     'l0_ffn_mod_b_2': 4.596,
     'l1_mix_norm_g_2': 8.0,
     'l1_mix_mod_b_2': 7.51,
     'l1_fox_q_norm_g_2': 8.0,
     'l1_fox_k_norm_g_2': 8.0,
     'l1_ffn_norm_g_2': 4.329,
     'l1_ffn_mod_b_2': 5.663}
    for name, (base, spread) in spreads.items():
        noise = np.random.default_rng([zlib.crc32(name.encode()), seed]).standard_normal(out[name].shape)
        drawn = base * np.exp(spread * noise) if base else spread * noise
        out[name] = __import__('jax').numpy.asarray(drawn.astype(out[name].dtype))
    for name, factor in factors.items():
        out[name] = (out[name] * factor).astype(out[name].dtype)
    return out
```

```python
from contextlib import ExitStack

import numpy as np

import concourse.bass as bass
from concourse import mybir

F32 = mybir.dt.float32
U32 = mybir.dt.uint32
ACT = mybir.ActivationFunctionType
ALU = mybir.AluOpType
AX = mybir.AxisListType

P = 128
T = 256
TT = T // P
D = 1024
KD = D // P
EPS = 1e-6
BIG = 1e30
LOWEST = -3e38

SLOTS = 6
SLOT = 2048
BANKS = 4

GH = 4
FF = 2816
FFG = FF // P
BLK = 88
NBLK = 16
FH = 16
FE = 64
PH = 8
TOPK = 16
KEYS = 128
LEVELS = 7
MODS = 4

STREAM = [
    ("qkv", 6, 2048, P), ("gz", 2, 2048, P), ("mqk", 2, 2048, P), ("mv", 2, 2048, P), ("mo", 2, 2048, P),
    ("gates", 8, 2048, P), ("mod", 12 * MODS, 2048, P), ("branch_a", 2, 2048, P), ("branch_b", 2, 2048, P),
    ("w_out", 4, 2048, P), ("ffn_up", FFG, 2048, P), ("ffn_down", 16, 1408, P), ("ple_gate", 4, 2048, P),
    ("ple", 1, 2048, P),
    ("lru_in", NBLK, 2 * KD * BLK, P), ("lru_out", KD, 2048, 96),
    ("peer0_q", 8, 2048, P), ("peer0_keys", 1, 2048, P), ("peer0_experts", KEYS, 2048, P),
    ("fox_qk", 8, 2048, P), ("fox_v", 4, 2048, P), ("fox_og", 4, 2048, P), ("fox_out", 4, 2048, P),
    ("peer1_q", 8, 2048, P), ("peer1_keys", 1, 2048, P), ("peer1_experts", KEYS, 2048, P),
]
TILE0 = {}
_n = 0
for _name, _count, _w, _p in STREAM:
    TILE0[_name] = _n
    _n += _count

CONSTS = [("ident", P), ("upper", P), ("ones", P), ("heads", P), ("iota", P), ("mask", 2 * P), ("maskT", P),
          ("level0", P), ("levelsT", LEVELS * P)]
CONST0 = {}
_n = 0
for _name, _w in CONSTS:
    CONST0[_name] = (_n, _n + _w)
    _n += _w
CONSTW = _n

VECS = [("g_mix", 8), ("g_ffn", 8), ("g_ple", 8), ("g_final", 8), ("gdn_norm", 1), ("ml_norm", 4),
        ("conv", 48), ("norms2", 32), ("mod_b", 96), ("c", 8), ("gate_bias", 16), ("a_log", 4),
        ("lru_conv", 64), ("lru_conv_b", 16), ("ra_b", 16), ("ri_b", 16), ("lam", 16),
        ("fox_fb", 16), ("fox_qg", 1), ("fox_kg", 1)]
VEC0 = {}
_n = 0
for _name, _w in VECS:
    VEC0[_name] = (_n, _n + _w)
    _n += _w
VECW = _n


class Signals:

    def __init__(self, nc, ctx):
        self.nc, self.ctx, self.sems = nc, ctx, {}

    def __call__(self, name):
        if name not in self.sems:
            self.sems[name] = self.ctx.enter_context(self.nc.semaphore(name))
        return self.sems[name]


class Steps:

    def __init__(self, eng, sem, own):
        self.eng, self.sem, self.own, self.count, self.last = eng, sem, own, {}, None

    def did(self, ins, name=None):
        if isinstance(name, tuple):
            self.last = name
        else:
            name = name or self.own
            self.count[name] = self.count.get(name, 0) + 1
            self.last = (name, self.count[name])
        ins.then_inc(self.sem(self.last[0]), 1)

    def settle(self):
        self.eng.wait_ge(self.sem(self.last[0]), self.last[1])


def fox_order():
    order = []
    for i in range(FH + 3):
        if i < FH:
            order.append(("scores", i))
        if 0 <= i - 2 < FH:
            order.append(("turn", i - 2))
        if 0 <= i - 3 < FH:
            order.append(("values", i - 3))
    return order


def count_outs():
    at, n = {}, 0

    def stage(name, count):
        nonlocal n
        at[name] = n
        n += count

    stage("norm0", 1)
    stage("small", 1)
    stage("qkv", 12)
    stage("gz", 4)
    stage("mqk", 4)
    stage("mv", 4)
    stage("mo", 4)
    stage("gates", 16)
    stage("branch_a", 8)
    stage("branch_b", 8)
    stage("w_out", 8)
    stage("norm1", 1)
    stage("ffn_up", 2 * FFG)
    stage("ffn_down", 8)
    stage("norm2", 1)
    stage("ple_gate", 8)
    stage("ple", 8)
    stage("norm3", 1)
    stage("norm4", 1)
    stage("lru", 4 * NBLK)
    stage("lru_out", 8)
    for layer in range(2):
        stage(f"norm{5 + 2 * layer}", 1)
        stage(f"peer{layer}_q", 16)
        stage(f"peer{layer}_scores", 8)
        stage(f"peer{layer}_turn", TT)
        stage(f"peer{layer}_place", T // 4)
        if layer == 0:
            stage("norm6", 1)
            stage("fox_small", 2)
            stage("fox_qk", 16)
            stage("fox_v", 8)
            stage("fox_og", 8)
            stage("fox_squares", 8)
            for kind, h in fox_order():
                if kind != "values":
                    stage(f"fox_{kind}{h}", 1)
            stage("fox_out", 8)
    return at


OUT0 = count_outs()


def lru_out_of(kind, j):
    base = OUT0["lru"]
    if kind in ("x", "g"):
        return base + (2 * j if j == 0 else 2 + 4 * (j - 1)) + (kind == "g")
    return base + (4 * j + 4 if j < NBLK - 1 else 4 * NBLK - 2) + (kind == "ri")


USED0 = {"mod": 0, "ffn_down": 12 * MODS, "peer0_experts": 12 * MODS + 8, "peer1_experts": 12 * MODS + 8 + KEYS}
PER_TILE = {"branch_a": 4, "branch_b": 4, "ple": 8, "lru_out": 1, "peer0_keys": 8, "peer1_keys": 8}


def tile_used(name, i):
    if name in ("mod", "peer0_experts", "peer1_experts"):
        return "tiles_used", USED0[name] + i + 1
    if name == "ffn_down":
        return ("tiles_used", USED0[name] + i // 2 + 1) if i % 2 == 0 else ("outs", OUT0[name] + i // 2 + 1)
    if name == "lru_in":
        return "outs", lru_out_of("g", i) + 1
    stage = name.replace("keys", "scores")
    return "outs", OUT0[stage] + PER_TILE.get(name, 2) * (i + 1)


TILES = [(name, i) for name, count, _, _ in STREAM for i in range(count)]


def build(nc, streams, xT, pT, consts, vecs, small_w, fox_f_w, lru_gate_w, out):
    with ExitStack() as ctx:
        sem = Signals(nc, ctx)

        def sb(name, shape, dt=F32):
            return ctx.enter_context(nc.sbuf_tensor(name, shape, dt))

        ring = sb("ring", [P, SLOTS, SLOT])
        x = sb("x", [P, KD, T])
        h = sb("h", [P, KD, T])
        work = sb("work", [P, KEYS * T])
        scratch = sb("scratch", [P, KD * T])
        con = sb("con", [P, CONSTW])
        vec = sb("vec", [P, VECW])
        wsmall = sb("wsmall", [P, KD, 16])
        wfox = sb("wfox", [P, KD, 16])
        rstd = sb("rstd", [P, T])
        mod = sb("mod", [P, 24 * MODS])
        modg = sb("modg", [P, KD * MODS])
        csilu = sb("csilu", [P, KD])
        lruc = sb("lruc", [P, 6, NBLK])
        mix = sb("mix", [P, 3, T])
        routeT = sb("routeT", [P, 3, T])
        tiny = sb("tiny", [P, 512])

        mm = ctx.enter_context(nc.psum_tensor("mm", [P, BANKS, 512], F32))
        ms = ctx.enter_context(nc.psum_tensor("ms", [P, 4, 512], F32))

        def cst(name):
            return con[:, CONST0[name][0]:CONST0[name][1]]

        def v(name, a=None, b=None, p=P):
            lo, hi = VEC0[name]
            return vec[0:p, lo + (a or 0):(hi if b is None else lo + b)]

        ident, upper, ones, heads64, iota = cst("ident"), cst("upper"), cst("ones"), cst("heads"), cst("iota")

        free = [0]

        def area(n, at=None):
            a = free[0] if at is None else at
            free[0] = a + n
            assert free[0] <= KEYS * T
            return work[:, a:a + n]

        cin = area(12 * (T + 3)).rearrange("p (j t) -> p j t", j=12)
        cv = area(12 * T).rearrange("p (j t) -> p j t", j=12)
        gz = area(GH * T).rearrange("p (j t) -> p j t", j=GH)
        mq = area(2 * T).rearrange("p (j t) -> p j t", j=2)
        mk = area(2 * T).rearrange("p (j t) -> p j t", j=2)
        mv = area(TT * 512).rearrange("p (c f) -> p c f", c=TT)
        mo = area(GH * T).rearrange("p (j t) -> p j t", j=GH)
        gates = area(16 * T).rearrange("p (j t) -> p j t", j=16)
        diag_at = free[0]
        diag = area(16 * P).rearrange("p (j t) -> p j t", j=16)
        vb = area(8 * P, diag_at).rearrange("p (j t) -> p j t", j=8)
        kbg = area(4 * P).rearrange("p (j t) -> p j t", j=4)
        kdec = area(4 * P).rearrange("p (j t) -> p j t", j=4)
        decay = area(8 * P).rearrange("p (j t) -> p j t", j=8)
        decayT = area(8 * P).rearrange("p (j t) -> p j t", j=8)
        grow = area(4 * P).rearrange("p (j t) -> p j t", j=4)
        m_at = free[0]
        M = area(8 * P).rearrange("p (j t) -> p j t", j=8)
        MT = area(8 * P).rearrange("p (j t) -> p j t", j=8)
        attnT = area(8 * P).rearrange("p (j t) -> p j t", j=8)
        x_at = free[0]
        X = area(8 * P).rearrange("p (j t) -> p j t", j=8)
        XT = area(8 * P).rearrange("p (j t) -> p j t", j=8)
        Pm = area(8 * P).rearrange("p (j t) -> p j t", j=8)
        ml_at = free[0]
        Ml = [area(8 * P).rearrange("p (j t) -> p j t", j=8) for _ in range(2)]
        vn = [area(4 * P).rearrange("p (j t) -> p j t", j=4) for _ in range(2)]
        nwT = area(4 * P).rearrange("p (j t) -> p j t", j=4)
        S1 = area(4 * P).rearrange("p (j t) -> p j t", j=4)
        oa = area(GH * T).rearrange("p (j t) -> p j t", j=GH)
        Dlog = area(4 * 384, ml_at).rearrange("p (j t) -> p j t", j=4)
        Em = area(4 * 384, m_at).rearrange("p (j t) -> p j t", j=4)
        ST = area(4 * 384, x_at).rearrange("p (j t) -> p j t", j=4)
        diag2 = area(8 * P, diag_at).rearrange("p (j t) -> p j t", j=8)
        ob = area(GH * T, diag_at + 8 * P).rearrange("p (j t) -> p j t", j=GH)
        ffact = area(FFG * T, 0).rearrange("p (j t) -> p j t", j=FFG)
        up = area(2 * T).rearrange("p (j t) -> p j t", j=2)
        pleg = area(KD * T).rearrange("p (j t) -> p j t", j=KD)
        pTs = area(2 * T).rearrange("p (j t) -> p j t", j=2)
        lx = area(NBLK * (T + 3), 0).rearrange("p (j t) -> p j t", j=NBLK)
        lc = area(NBLK * T).rearrange("p (j t) -> p j t", j=NBLK)
        lg = area(NBLK * T).rearrange("p (j t) -> p j t", j=NBLK)
        lt = area(NBLK * T).rearrange("p (j t) -> p j t", j=NBLK)
        li = area(NBLK * T).rearrange("p (j t) -> p j t", j=NBLK)
        lr = area(NBLK * T).rearrange("p (j t) -> p j t", j=NBLK)
        lgw = area(NBLK * 2 * BLK).rearrange("p (j g d) -> p j g d", j=NBLK, g=2)
        fq = area(KD * T, 0)
        fk = area(KD * T)
        fv = area(TT * D).rearrange("p (c f) -> p c f", c=TT)
        fo = area(KD * T).rearrange("p (j t) -> p j t", j=KD)
        fsq = area(2 * KD * T)
        fd = area(TT * FH * P).rearrange("p (j c t) -> p j c t", j=FH, c=TT)
        fL = area(3 * 384).rearrange("p (j t) -> p j t", j=3)
        fP = area(3 * 384).rearrange("p (j t) -> p j t", j=3)
        fPT = area(3 * 384).rearrange("p (j t) -> p j t", j=3)
        fy = area(KD * T).rearrange("p (j t) -> p j t", j=KD)
        fq3 = fq.rearrange("p (j t) -> p j t", j=KD)
        fk3 = fk.rearrange("p (j t) -> p j t", j=KD)
        eq = area(16 * T, 0).rearrange("p (j t) -> p j t", j=16)
        es = area(TT * 16 * KEYS).rearrange("p (c j n) -> p c j n", c=TT, j=16)
        es2 = area(16 * KEYS).rearrange("p (j n) -> p j n", j=16)
        cand = area(PH * 256).rearrange("p (j n) -> p j n", j=PH)
        cand2 = area(PH * 256).rearrange("p (j n) -> p j n", j=PH)
        hot = area(PH * 256)
        hot2 = area(PH * 256)
        top = area(2 * PH * 16).rearrange("p (s j k) -> p j s k", j=PH, s=2)
        topi_flat = area(2 * PH * 16).bitcast(U32)
        topi = topi_flat.rearrange("p (s j k) -> p j s k", j=PH, s=2)
        topf_flat = area(2 * PH * 16)
        topf = topf_flat.rearrange("p (s j k) -> p j s k", j=PH, s=2)
        best = area(PH * 16).rearrange("p (j k) -> p j k", j=PH)
        besti = area(PH * 16).bitcast(U32)
        part = area(2 * PH * 16).bitcast(U32).rearrange("p (s k) -> p s k", s=2)
        partf = area(2 * PH * 16).rearrange("p (s k) -> p s k", s=2)
        shifted = area(PH * 16).rearrange("p (j k) -> p j k", j=PH)
        expo = area(PH * 16).rearrange("p (j k) -> p j k", j=PH)
        sums = area(PH)
        rsums = area(PH)
        route = area(TT * 3 * P).rearrange("p (c s k) -> p c s k", c=TT, s=3)
        placed = work[:, :].rearrange("p (e t) -> p e t", e=KEYS)
        onehot = scratch[:, :].rearrange("p (b s i n) -> p b s i n", b=2, s=2, i=4)

        def col(a, n):
            return tiny[:, a:a + n]

        pre = col(0, 32).rearrange("p (c j) -> p c j", c=TT)
        zz = col(32, 16).rearrange("p (c j) -> p c j", c=TT)
        nz = col(48, 16).rearrange("p (c j) -> p c j", c=TT)
        en = col(64, 16).rearrange("p (c j) -> p c j", c=TT)
        ln = col(80, 16).rearrange("p (c j) -> p c j", c=TT)
        sp = col(96, 16).rearrange("p (c j) -> p c j", c=TT)
        expa = col(112, 4)
        lgt = col(116, 16).rearrange("p (c j) -> p c j", c=TT)
        beta = col(132, 8).rearrange("p (c j) -> p c j", c=TT)
        cum = col(140, 16).rearrange("p (c j) -> p c j", c=TT)
        gl = col(156, 4)
        ecum = col(160, 4)
        ekd = col(164, 4)
        gdif = col(168, 4)
        ngc = col(172, 8).rearrange("p (c j) -> p c j", c=TT)
        imb = col(180, 8).rearrange("p (c j) -> p c j", c=TT)
        mx = col(188, 8).rearrange("p (c j) -> p c j", c=TT)
        nm = col(196, 8).rearrange("p (c j) -> p c j", c=TT)
        flo = col(204, 8).rearrange("p (c j) -> p c j", c=TT)
        den = col(212, 8).rearrange("p (c j) -> p c j", c=TT)
        nden = col(220, 8).rearrange("p (c j) -> p c j", c=TT)
        rden = col(228, 8).rearrange("p (c j) -> p c j", c=TT)
        ffz = col(256, 32).rearrange("p (c j) -> p c j", c=TT)
        ffn_ = col(288, 32).rearrange("p (c j) -> p c j", c=TT)
        ffe = col(320, 32).rearrange("p (c j) -> p c j", c=TT)
        ffl = col(352, 32).rearrange("p (c j) -> p c j", c=TT)
        ffs = col(384, 32).rearrange("p (c j) -> p c j", c=TT)
        fcum = col(416, 32).rearrange("p (c j) -> p c j", c=TT)
        fmx = col(448, 6).rearrange("p (b c) -> p b c", b=3)
        fnm = col(454, 6).rearrange("p (b c) -> p b c", b=3)
        fsum = col(460, 6).rearrange("p (b c) -> p b c", b=3)
        frs = col(466, 6).rearrange("p (b c) -> p b c", b=3)
        fqg = col(472, 1)

        def tile_ready(eng, n):
            eng.wait_ge(sem(f"slot{n % SLOTS}_loaded"), 16 * (n // SLOTS + 1))

        def out_ready(eng, n):
            eng.wait_ge(sem("outs"), n + 1)

        def out_taken(eng, n):
            eng.wait_ge(sem(f"bank{n % BANKS}_taken"), n // BANKS + 1)

        def taken(n):
            return f"bank{n % BANKS}_taken", n // BANKS + 1

        block = ctx.enter_context(nc.Block())

        @block.sync
        def _(sp_):
            sp_.dma_start(x[:, :, :], xT).then_inc(sem("x_loaded"), 16)
            sp_.dma_start(vec[:, :], vecs).then_inc(sem("vec_loaded"), 16)
            sp_.dma_start(con[:, :], consts).then_inc(sem("con_loaded"), 16)
            sp_.dma_start(wsmall[:, :, :], small_w).then_inc(sem("wsmall_loaded"), 16)
            sp_.dma_start(wfox[:, :, :], fox_f_w).then_inc(sem("wfox_loaded"), 16)
            for name, count, width, parts in STREAM:
                base, src = TILE0[name], streams[name]

                def load(n, which):
                    sp_.dma_start(ring[0:parts, n % SLOTS, 0:width], which).then_inc(
                        sem(f"slot{n % SLOTS}_loaded"), 16)

                def load_one(i):
                    if base + i >= SLOTS:
                        what, value = tile_used(*TILES[base + i - SLOTS])
                        sp_.wait_ge(sem(what), value)
                    load(base + i, src[i])

                if name not in ("mod", "peer0_experts", "peer1_experts"):
                    for i in range(count):
                        load_one(i)
                    continue
                rounds = count // SLOTS
                for i in range(SLOTS):
                    load_one(i)
                with sp_.Fori(1, rounds) as r:
                    for j in range(SLOTS):
                        sp_.wait_ge(sem("tiles_used"), r * SLOTS + (USED0[name] + j - SLOTS + 1))
                        load(base + j, src[bass.ds(r * SLOTS + j, 1), :, :].rearrange("a p w -> (a p) w"))
                for i in range(rounds * SLOTS, count):
                    load_one(i)
            sp_.wait_ge(sem("x_done"), 8)
            sp_.dma_start(out, x[:, :, :]).then_inc(sem("stored"), 16)
            sp_.wait_ge(sem("stored"), 16)

        @block.tensor
        def _(pe):
            S = Steps(pe, sem, "pe_step")
            mod_tiles = [0]

            def bank(n):
                if n >= BANKS:
                    out_taken(pe, n - BANKS)
                return mm[:, n % BANKS, :]

            def slot(n):
                tile_ready(pe, n)
                return ring[:, n % SLOTS, :]

            def group(dst, pairs, first=True):
                for i, (a, b) in enumerate(pairs):
                    ins = pe.matmul(dst, a, b, start=first and i == 0, stop=i == len(pairs) - 1,
                                    skip_group_check=True)
                return ins

            def norm(i, shifted_):
                n = OUT0[f"norm{i}"]
                pe.wait_ge(sem("norm_squares"), i + 1)
                if i == 0:
                    pe.wait_ge(sem("con_loaded"), 16)
                S.did(group(bank(n)[:, 0:T], [(ones, scratch[:, k * T:(k + 1) * T]) for k in range(KD)]), "outs")
                return i

            def h_ready(i):
                plain = [0, 1, 2]
                if i in plain:
                    pe.wait_ge(sem("h_scaled"), KD * (plain.index(i) + 1))
                else:
                    pe.wait_ge(sem("h_shifted"), KD * (i - 3))

            def dense(stage, tiles, per_tile, pairs_of, m=P, width=T):
                n = OUT0[stage]
                for t in range(tiles):
                    w = slot(TILE0[stage] + t)
                    for b in range(per_tile):
                        dst = bank(n)[0:m, 0:width]
                        S.did(group(dst, pairs_of(w, t, b)), "outs")
                        n += 1

            def by_k(w, t, b, rows=KD, act=None):
                src = h if act is None else act
                return [(w[:, k * 256 + b * P:k * 256 + (b + 1) * P], src[:, k, :]) for k in range(rows)]

            def mods(count):
                for _ in range(count):
                    if mod_tiles[0] == 12 * MODS:
                        return
                    i = mod_tiles[0]
                    w = slot(TILE0["mod"] + i)
                    if i == 0:
                        pe.wait_ge(sem("csilu_ready"), 1)
                        out_taken(pe, OUT0["gates"] + 15)
                        out_taken(pe, OUT0["gates"] + 14)
                        out_taken(pe, OUT0["gates"] + 13)
                        out_taken(pe, OUT0["gates"] + 12)
                    for b in range(2):
                        c = 2 * i + b
                        ins = group(mm[:, MOD_BANK, c:c + 1],
                                    [(w[:, k * 256 + b * P:k * 256 + (b + 1) * P], csilu[:, k:k + 1])
                                     for k in range(KD)])
                    ins.then_inc(sem("tiles_used"), 1)
                    mod_tiles[0] += 1

            MOD_BANK = 3

            norm(0, False)
            h_ready(0)
            n = OUT0["small"]
            pe.wait_ge(sem("wsmall_loaded"), 16)
            dst = bank(n)
            for c in range(TT):
                ins = group(dst[:, 16 * c:16 * (c + 1)],
                            [(h[:, k, c * P:(c + 1) * P], wsmall[:, k, :]) for k in range(KD)])
            S.did(ins, "outs")
            dense("qkv", 6, 2, by_k)
            dense("gz", 2, 2, by_k)
            dense("mqk", 2, 2, by_k)
            dense("mv", 2, 2, lambda w, t, b: [(h[:, k, b * P:(b + 1) * P], w[:, k * 256:(k + 1) * 256])
                                               for k in range(KD)])
            dense("mo", 2, 2, by_k)
            dense("gates", 8, 2, by_k)

            pe.wait_ge(sem("qk_squares"), 1)
            for j in range(4):
                ins = pe.matmul(ms[:, j, :], ones, scratch[:, j * 512:(j + 1) * 512], start=True, stop=True)
            S.did(ins, "qk_sums")
            mods(1)
            pe.wait_ge(sem("log_decays"), 1)
            for c in range(TT):
                ins = pe.matmul(mm[:, 0, 8 * c:8 * c + 8], upper, lgt[:, c, :], start=True, stop=True,
                                skip_group_check=True)
            pe.matmul(mm[:, 0, 12:16], ones, lgt[:, 0, 4:8], start=False, stop=True, skip_group_check=True)
            ins = pe.matmul(mm[:, 0, 16:20], ones, lgt[:, 0, 0:4], start=True, stop=True, skip_group_check=True)
            S.did(ins, "cum_ready")
            mods(1)
            pe.wait_ge(sem("diag_ready"), 1)
            pe.wait_ge(sem("qk_sums_taken"), 1)
            for j in range(2):
                ins = pe.matmul(ms[:, j, :], ones, diag[:, 4 * j:4 * j + 4, :].rearrange("p j t -> p (j t)"), start=True, stop=True)
            S.did(ins, "rows_ready")
            mods(2)
            pe.wait_ge(sem("qk_normal"), 1)
            pe.wait_ge(sem("cum_taken"), 1)
            for u in range(8):
                hd, c = u // 2, u % 2
                ins = pe.matmul(mm[:, u // 4, (u % 4) * P:(u % 4 + 1) * P], cv[:, 4 + hd, c * P:(c + 1) * P],
                                cv[:, 4 + hd, c * P:(c + 1) * P], start=True, stop=True, skip_group_check=True)
            S.did(ins, "kk_ready")
            for u in range(8):
                hd, c = u // 2, u % 2
                ins = pe.matmul(ms[:, 2 + u // 4, (u % 4) * P:(u % 4 + 1) * P], cv[:, 4 + hd, c * P:(c + 1) * P],
                                cv[:, hd, c * P:(c + 1) * P], start=True, stop=True, skip_group_check=True)
            S.did(ins, "kq_ready")
            mods(2)
            pe.wait_ge(sem("rows_taken"), 1)
            for u in range(8):
                hd, c = u // 2, u % 2
                ins = pe.transpose(ms[:, u // 4, (u % 4) * P:(u % 4 + 1) * P], cv[:, 8 + hd, c * P:(c + 1) * P], ident)
            S.did(ins, "v_turned")
            mods(2)
            pe.wait_ge(sem("M_ready"), 1)
            for u in range(8):
                ins = pe.transpose(mm[:, u // 4, (u % 4) * P:(u % 4 + 1) * P], M[:, u, :], ident)
            S.did(ins, "M_turned")
            pe.wait_ge(sem("attnT_ready"), 1)
            for u in range(8):
                hd, c = u % 4, u // 4
                ins = pe.transpose(ms[:, 2 + u // 4, (u % 4) * P:(u % 4 + 1) * P], cv[:, 4 + hd, c * P:(c + 1) * P], ident)
            S.did(ins, "k_turned")
            mods(2)
            pe.wait_ge(sem("tokens_ready"), 1)
            for l in range(1, LEVELS):
                for u in range(2):
                    pe.wait_ge(sem("X_ready"), 2 * (l - 1) + u + 1)
                    pe.wait_ge(sem("corner_ready"), l)
                    for i in range(4 * u, 4 * u + 4):
                        ins = pe.matmul(ms[:, u, (i % 4) * P:(i % 4 + 1) * P], Ml[l % 2][:, i, :], X[:, i, :],
                                        start=True, stop=True, skip_group_check=True)
                    S.did(ins, "MX_ready")
                mods(1)
                for u in range(2):
                    pe.wait_ge(sem("MX_taken"), 2 * (l - 1) + u + 1)
                    for i in range(4 * u, 4 * u + 4):
                        pe.matmul(ms[:, u, (i % 4) * P:(i % 4 + 1) * P], XT[:, i, :], Pm[:, i, :],
                                  start=True, stop=True, skip_group_check=True)
                        ins = pe.matmul(ms[:, 2 + u, (i % 4) * P:(i % 4 + 1) * P], Pm[:, i, :], XT[:, i, :],
                                        start=True, stop=True, skip_group_check=True)
                    S.did(ins, "XMX_ready")
                mods(1)
            pe.wait_ge(sem("X_ready"), 2 * LEVELS)
            for i in range(4):
                ins = pe.matmul(mm[:, 0, i * P:(i + 1) * P], XT[:, 2 * i, :], vb[:, 2 * i, :], start=True, stop=True,
                                skip_group_check=True)
            S.did(ins, "vn0_ready")
            for i in range(4):
                ins = pe.matmul(mm[:, 1, i * P:(i + 1) * P], kbg[:, i, :], XT[:, 2 * i + 1, :], start=True, stop=True,
                                skip_group_check=True)
            S.did(ins, "w_ready")
            mods(1)
            pe.wait_ge(sem("vn0_taken"), 1)
            for i in range(4):
                ins = pe.matmul(mm[:, 2, i * P:(i + 1) * P], kdec[:, i, :], vn[0][:, i, :], start=True, stop=True,
                                skip_group_check=True)
            S.did(ins, "state_ready")
            mods(1)
            pe.wait_ge(sem("state_taken"), 1)
            pe.wait_ge(sem("w_taken"), 1)
            for i in range(4):
                ins = group(mm[:, 0, i * P:(i + 1) * P], [(XT[:, 2 * i + 1, :], vb[:, 2 * i + 1, :]),
                                                          (nwT[:, i, :], S1[:, i, :])])
            S.did(ins, "vn1_ready")
            mods(1)
            pe.wait_ge(sem("vn1_taken"), 1)
            for i in range(4):
                dst = ms[:, i // 2, (i % 2) * T:(i % 2) * T + P]
                pe.matmul(dst, vn[0][:, i, :], attnT[:, 2 * i, :], start=True, stop=True, skip_group_check=True)
                dst = ms[:, i // 2, (i % 2) * T + P:(i % 2) * T + 2 * P]
                ins = group(dst, [(vn[1][:, i, :], attnT[:, 2 * i + 1, :]), (S1[:, i, :], grow[:, i, :])])
            S.did(ins, "oa_ready")

            def head_sums(which):
                pe.wait_ge(sem("head_squares"), which + 1)
                for j in range(2):
                    ins = pe.matmul(ms[:, 2 + j, :], ones, scratch[:, j * 512:(j + 1) * 512], start=True, stop=True)
                S.did(ins, "head_sums")

            mods(2)
            head_sums(0)
            mods(1)

            pe.wait_ge(sem("diag2_ready"), 1)
            for j in range(2):
                ins = pe.matmul(mm[:, 1 + j, :], ones, diag2[:, 4 * j:4 * j + 4, :].rearrange("p j t -> p (j t)"), start=True, stop=True)
            S.did(ins, "ml_rows_ready")
            mods(2)
            pe.wait_ge(sem("oa_done"), 1)
            for i in range(4):
                a, o = i // 2, 64 * (i % 2)
                pe.matmul(ms[:, i, 0:P], mq[o:o + 64, a, 0:P], mk[o:o + 64, a, 0:P], start=True, stop=True,
                          skip_group_check=True)
                ins = pe.matmul(ms[:, i, P:3 * P], mq[o:o + 64, a, P:2 * P], mk[o:o + 64, a, :], start=True, stop=True,
                                skip_group_check=True)
            S.did(ins, "ml_qk_ready")
            mods(3)
            pe.wait_ge(sem("ml_scores"), 1)
            for i in range(4):
                if i == 0:
                    pe.wait_ge(sem("ml_rows_taken"), 1)
                if i == 3:
                    pe.wait_ge(sem("ml_turned"), 1)
                for b in range(3):
                    ins = pe.transpose(mm[:, i % 3, b * P:(b + 1) * P], Em[:, i, b * P:(b + 1) * P], ident)
                S.did(ins, "ml_turn")
            mods(2)
            pe.wait_ge(sem("ml_turned"), 4)
            for i in range(4):
                dst = ms[:, i // 2, (i % 2) * T:(i % 2 + 1) * T]
                pe.matmul(dst, mv[:, 0, i * P:(i + 1) * P], ST[:, i, 0:2 * P], start=i % 2 == 0, stop=False,
                          skip_group_check=True)
                ins = pe.matmul(dst[:, P:2 * P], mv[:, 1, i * P:(i + 1) * P], ST[:, i, 2 * P:3 * P], start=False,
                                stop=True, skip_group_check=True)
            S.did(ins, "ob_ready")
            mods(2)
            head_sums(1)
            mods(100)

            def by_k4(act):
                return lambda w, t, b: [(w[:, k * 512 + b * P:k * 512 + (b + 1) * P], act[:, k, :]) for k in range(4)]

            pe.wait_ge(sem("mods_taken"), 1)
            pe.wait_ge(sem("oa_done"), 2)
            dense("branch_a", 2, 4, by_k4(oa))
            pe.wait_ge(sem("ob_done"), 1)
            dense("branch_b", 2, 4, by_k4(ob))
            pe.wait_ge(sem("mixed"), 1)
            dense("w_out", 4, 2, lambda w, t, b: by_k(w, t, b, act=gates))
            norm(1, False)

            h_ready(1)
            dense("ffn_up", FFG, 2, by_k)
            out_taken(pe, OUT0["ffn_up"] + 2 * FFG - 1)
            n = OUT0["ffn_down"]
            for m in range(KD):
                dst = bank(n + m)[:, 0:T]
                for half in range(2):
                    w = slot(TILE0["ffn_down"] + 2 * m + half)
                    for k in range(11):
                        ins = pe.matmul(dst, w[:, k * P:(k + 1) * P], ffact[:, 11 * half + k, :],
                                        start=half == 0 and k == 0, stop=half == 1 and k == 10)
                    S.did(ins, "outs" if half == 1 else "tiles_used")
            norm(2, False)

            h_ready(2)
            dense("ple_gate", 4, 2, by_k)
            pe.wait_ge(sem("p_loaded"), 16)
            dense("ple", 1, 8, lambda w, t, b: [(w[:, k * D + b * P:k * D + (b + 1) * P], pTs[:, k, :])
                                                for k in range(2)])
            norm(3, False)
            norm(4, True)

            h_ready(4)
            pe.wait_ge(sem("lru_gates_loaded"), 16)

            def lru_gates(j):
                pe.wait_ge(sem("lru_conv"), j + 1)
                for g, kind in enumerate(("ra", "ri")):
                    S.did(pe.matmul(bank(lru_out_of(kind, j))[0:BLK, 0:T], lgw[0:BLK, j, g, :], lc[0:BLK, j, :],
                                    start=True, stop=True), "outs")

            for j in range(NBLK):
                w = slot(TILE0["lru_in"] + j)
                for b, kind in enumerate(("x", "g")):
                    S.did(group(bank(lru_out_of(kind, j))[0:BLK, 0:T],
                                [(w[:, (b * KD + k) * BLK:(b * KD + k + 1) * BLK], h[:, k, :]) for k in range(KD)]),
                          "outs")
                if j:
                    lru_gates(j - 1)
            lru_gates(NBLK - 1)
            pe.wait_ge(sem("lru_y"), 1)
            dense("lru_out", KD, 1, lambda w, t, b: [(w[0:BLK, j * P:(j + 1) * P], lt[0:BLK, j, :])
                                                     for j in range(NBLK)])

            def experts(L):
                norm(5 + 2 * L, True)
                h_ready(5 + 2 * L)
                dense(f"peer{L}_q", 8, 2, by_k)
                w = slot(TILE0[f"peer{L}_keys"])
                out_taken(pe, OUT0[f"peer{L}_q"] + 15)
                for c in range(TT):
                    for g in range(4):
                        n = OUT0[f"peer{L}_scores"] + 4 * c + g
                        dst = bank(n)
                        for j in range(4 * g, 4 * g + 4):
                            ins = pe.matmul(dst[:, (j % 4) * P:(j % 4 + 1) * P], eq[:, j, c * P:(c + 1) * P],
                                            w[:, j * P:(j + 1) * P], start=True, stop=True, skip_group_check=True)
                        S.did(ins, "outs")
                for c in range(TT):
                    dst = bank(OUT0[f"peer{L}_turn"] + c)
                    pe.wait_ge(sem("routed"), TT * L + c + 1)
                    for s in range(3):
                        ins = pe.transpose(dst[:, s * P:(s + 1) * P], route[:, c, s, :], ident)
                    S.did(ins, "outs")
                n0 = OUT0[f"peer{L}_place"]

                def place(n, wait_taken, wait_hot, b):
                    pe.wait_ge(sem(taken(n)[0]), wait_taken)
                    pe.wait_ge(sem("onehots"), wait_hot)
                    for i in range(4):
                        ins = pe.matmul(mm[:, n % BANKS, i * P:(i + 1) * P], onehot[:, b, 0, i, :],
                                        onehot[:, b, 1, i, :], start=True, stop=True, skip_group_check=True)
                    ins.then_inc(sem("outs"), 1)

                with pe.Fori(0, T // 16) as r:
                    for j in range(4):
                        place(n0 + j, r + (n0 + j) // BANKS, r * 4 + (T // 4 * L + j + 1), j % 2)
                for j in range(4):
                    out_taken(pe, n0 + T // 4 - 4 + j)

                t0 = TILE0[f"peer{L}_experts"]

                def hidden(j, wait_slot, wait_free):
                    pe.wait_ge(sem(f"slot{(t0 + j) % SLOTS}_loaded"), wait_slot)
                    if wait_free is not None:
                        pe.wait_ge(sem("hidden_taken"), wait_free)
                    w = ring[:, (t0 + j) % SLOTS, :]
                    group(mm[:, j % 3, 0:T], [(w[:, k * P:(k + 1) * P], h[:, k, :]) for k in range(KD)]) \
                        .then_inc(sem("hidden_ready"), 1)

                def values(j, wait_mixed, first):
                    pe.wait_ge(sem("weighted"), wait_mixed)
                    w = ring[:, (t0 + j) % SLOTS, :]
                    for m in range(KD):
                        ins = pe.matmul(ms[:, m // 2, (m % 2) * T:(m % 2 + 1) * T], w[:, D + m * P:D + (m + 1) * P],
                                        mix[:, j % 3, :], start=first and m % 2 == 0, stop=False,
                                        skip_group_check=True)
                    ins.then_inc(sem("tiles_used"), 1)

                def step(j, r, first=False):
                    hidden(j, 16 * r + 16 * ((t0 + j) // SLOTS + 1),
                           None if first and j < 3 else r * SLOTS + (KEYS * L + j - 3 + 1))
                    if not (first and j == 0):
                        values(j - 1, r * SLOTS + (KEYS * L + j), first and j == 1)

                for j in range(SLOTS):
                    step(j, 0, True)
                with pe.Fori(1, KEYS // SLOTS) as r:
                    for j in range(SLOTS):
                        step(j, r)
                last = KEYS // SLOTS
                for j in range(KEYS - last * SLOTS):
                    step(j, last)
                values(KEYS - last * SLOTS - 1, KEYS * (L + 1), False)

            experts(0)

            norm(6, True)
            h_ready(6)
            n = OUT0["fox_small"]
            pe.wait_ge(sem("wfox_loaded"), 16)
            dst = bank(n)
            for c in range(TT):
                ins = group(dst[:, 16 * c:16 * (c + 1)],
                            [(h[:, k, c * P:(c + 1) * P], wfox[:, k, :]) for k in range(KD)])
            S.did(ins, "outs")
            n += 1
            pe.wait_ge(sem("fox_logf"), 1)
            dst = bank(n)
            group(dst[:, 0:16], [(upper, ffs[:, 0, :])])
            ins = group(dst[:, 16:32], [(upper, ffs[:, 1, :]), (ones, ffs[:, 0, :])])
            S.did(ins, "outs")
            dense("fox_qk", 8, 2, by_k)
            dense("fox_v", 4, 2, lambda w, t, b: [(h[:, k, b * P:(b + 1) * P], w[:, k * 256:(k + 1) * 256])
                                                  for k in range(KD)])
            dense("fox_og", 4, 2, by_k)
            for j in range(8):
                n = OUT0["fox_squares"] + j
                pe.wait_ge(sem("fox_sq"), j // 4 + 1)
                S.did(pe.matmul(bank(n), heads64, fsq[:, j * 512:(j + 1) * 512], start=True, stop=True), "outs")
            pe.wait_ge(sem("fox_diag"), 1)
            pe.wait_ge(sem("fox_normal"), 2)
            for kind, hd in fox_order():
                a, o = hd // 2, 64 * (hd % 2)
                if kind == "scores":
                    dst = bank(OUT0[f"fox_scores{hd}"])
                    group(dst[:, 0:P], [(fq3[o:o + 64, a, 0:P], fk3[o:o + 64, a, 0:P]), (ones, fd[:, hd, 0, :])])
                    ins = group(dst[:, P:3 * P], [(fq3[o:o + 64, a, P:2 * P], fk3[o:o + 64, a, :]),
                                                  (ones, fd[:, hd, :, :].rearrange("p c t -> p (c t)"))])
                    S.did(ins, "outs")
                elif kind == "turn":
                    dst = bank(OUT0[f"fox_turn{hd}"])
                    pe.wait_ge(sem("fox_probs"), hd + 1)
                    for b in range(3):
                        ins = pe.transpose(dst[:, b * P:(b + 1) * P], fP[:, hd % 3, b * P:(b + 1) * P], ident)
                    S.did(ins, "outs")
                else:
                    out_taken(pe, OUT0[f"fox_turn{hd}"])
                    if a >= 4:
                        pe.wait_ge(sem("fox_y"), a - 3)
                    dst = ms[o:o + 64, a % 4, 0:T]
                    pe.matmul(dst, fv[:, 0, hd * FE:(hd + 1) * FE], fPT[:, hd % 3, 0:2 * P], start=True, stop=False,
                              skip_group_check=True)
                    S.did(pe.matmul(dst[:, P:2 * P], fv[:, 1, hd * FE:(hd + 1) * FE], fPT[:, hd % 3, 2 * P:3 * P],
                                    start=False, stop=True, skip_group_check=True), "fox_pv")
            pe.wait_ge(sem("fox_y"), KD)
            dense("fox_out", 4, 2, lambda w, t, b: by_k(w, t, b, act=fy))
            experts(1)

        @block.scalar
        def _(act):
            S = Steps(act, sem, "act_step")
            def squares(i):
                if i == 0:
                    act.wait_ge(sem("x_loaded"), 16)
                else:
                    act.wait_ge(sem("x_done"), i)
                if i >= 1:
                    out_ready(act, OUT0[f"norm{i - 1}"])
                S.did(act.activation(scratch[:, :], x[:, :, :].rearrange("p k t -> p (k t)"), ACT.Square),
                      "norm_squares")

            def root(i):
                act.wait_ge(sem("norm_inverse"), i + 1)
                S.did(act.activation(rstd[:, :], rstd[:, :], ACT.Sqrt), "norm_rstd")

            def shift(i):
                for k in range(KD):
                    act.wait_ge(sem("h_scaled2"), KD * (i - 4) + k + 1)
                    m = (i - 4) * 24 + k
                    S.did(act.activation(h[:, k, :], h[:, k, :], ACT.Identity, bias=mod[:, m:m + 1]), "h_shifted")

            def evacuate(n, dst, func=ACT.Copy, m=P, width=T):
                out_ready(act, n)
                src = mm[0:m, n % BANKS, 0:width]
                if len(dst.shape) == 3:
                    src = src.rearrange("p (j n) -> p j n", n=P)
                S.did(act.activation(dst, src, func), taken(n))

            squares(0)
            root(0)
            act.wait_ge(sem("vec_loaded"), 16)
            S.did(act.activation(expa, v("a_log"), ACT.Exp), "expa_ready")
            act.wait_ge(sem("pre_ready"), 1)
            S.did(act.activation(beta, pre[:, :, 0:4], ACT.Sigmoid), "beta_ready")
            S.did(act.activation(csilu[:, :], v("c"), ACT.Silu), "csilu_ready")
            act.wait_ge(sem("nz_ready"), 1)
            S.did(act.activation(en, nz, ACT.Exp))
            S.settle()
            S.did(act.activation(ln, en, ACT.Ln, bias=1.0), "ln_ready")
            act.wait_ge(sem("pad_zero"), 1)
            for j in range(13):
                if j < 12:
                    evacuate(OUT0["qkv"] + j, cin[:, j, 3:T + 3])
                if j:
                    act.wait_ge(sem("conv_done"), j)
                    S.did(act.activation(cv[:, j - 1, :], cv[:, j - 1, :], ACT.Silu), "qkv_active")
            for j in range(4):
                evacuate(OUT0["gz"] + j, gz[:, j, :], ACT.Silu)
            for j in range(4):
                evacuate(OUT0["mqk"] + j, (mq if j < 2 else mk)[:, j % 2, :])
            for j in range(4):
                evacuate(OUT0["mv"] + j, mv[:, j % 2, (j // 2) * T:(j // 2 + 1) * T])
            for j in range(4):
                evacuate(OUT0["mo"] + j, mo[:, j, :], ACT.Sigmoid)
            for j in range(16):
                evacuate(OUT0["gates"] + j, gates[:, j, :], ACT.Sigmoid)
            act.wait_ge(sem("qk_inverse"), 1)
            S.did(act.activation(scratch[:, :], scratch[:, :], ACT.Sqrt), "qk_rstd")
            act.wait_ge(sem("gdif_ready"), 1)
            act.activation(ecum, cum[:, 1, 0:4], ACT.Exp)
            S.did(act.activation(ekd, gdif, ACT.Exp), "column_decays")
            act.wait_ge(sem("decay_logs"), 1)
            S.did(act.activation(decay, decay, ACT.Exp), "decay_ready")
            S.did(act.activation(decayT, decayT, ACT.Exp, scale=-1.0), "decay_ready")
            act.wait_ge(sem("rows_ready"), 1)
            for i in range(4):
                u = 2 * i + 1
                ins = act.activation(grow[:, i, :], ms[:, u // 4, (u % 4) * P:(u % 4 + 1) * P], ACT.Exp, scale=-1.0)
            S.did(ins, "grow_ready")
            act.wait_ge(sem("oa_ready"), 1)
            halves = ms[:, 0:2, :].rearrange("p b n -> p (b n)")
            act.activation(oa.rearrange("p j t -> p (j t)"), halves, ACT.Copy)
            S.did(act.activation(scratch[:, 0:1024], halves, ACT.Square), "head_squares")
            act.wait_ge(sem("head_inverse"), 1)
            S.did(act.activation(scratch[:, 1024:2048], scratch[:, 1024:2048], ACT.Sqrt), "head_rstd")
            act.wait_ge(sem("ml_nm"), 1)
            act.activation(flo, nm, ACT.Exp)
            for i in range(4):
                act.activation(Em[:, i, 0:P], Dlog[:, i, 0:P], ACT.Exp, bias=nm[:, 0, i:i + 1])
                ins = act.activation(Em[:, i, P:3 * P], Dlog[:, i, P:3 * P], ACT.Exp, bias=nm[:, 1, i:i + 1])
            S.did(ins, "ml_weights")
            for i in range(4):
                act.wait_ge(sem("ml_turn"), i + 1)
                S.did(act.activation(ST[:, i, :], mm[:, i % 3, 0:384], ACT.Copy), "ml_turned")
            act.wait_ge(sem("ob_ready"), 1)
            act.activation(ob.rearrange("p j t -> p (j t)"), halves, ACT.Copy)
            S.did(act.activation(scratch[:, 0:1024], halves, ACT.Square), "head_squares")
            act.wait_ge(sem("head_inverse"), 2)
            S.did(act.activation(scratch[:, 1024:2048], scratch[:, 1024:2048], ACT.Sqrt), "head_rstd")
            act.wait_ge(sem("x_done"), 1)
            act.dma_start(pTs, pT).then_inc(sem("p_loaded"), 16)
            squares(1)
            root(1)
            for j in range(FFG):
                if j >= 2:
                    out_taken(act, OUT0["ffn_up"] + 2 * (j - 2) + 1)
                evacuate(OUT0["ffn_up"] + 2 * j, up[:, j % 2, :], ACT.Silu)
            squares(2)
            root(2)
            for j in range(KD):
                evacuate(OUT0["ple_gate"] + j, pleg[:, j, :], ACT.Sigmoid)
            squares(3)
            root(3)
            act.wait_ge(sem("x_done"), 3)
            act.dma_start(lgw[0:96], lru_gate_w).then_inc(sem("lru_gates_loaded"), 16)
            act.wait_ge(sem("nlam_ready"), 1)
            S.did(act.activation(lruc[:, 1, :], lruc[:, 0, :], ACT.Exp), "lam_exp")
            squares(4)
            root(4)
            shift(4)
            act.wait_ge(sem("lru_pad_zero"), 1)

            def lru_act(j):
                n = lru_out_of("ra", j)
                out_ready(act, n)
                S.did(act.activation(lr[0:BLK, j, :], mm[0:BLK, n % BANKS, 0:T], ACT.Sigmoid,
                                     bias=v("ra_b", j, j + 1, BLK)), taken(n))
                n = lru_out_of("ri", j)
                out_ready(act, n)
                S.did(act.activation(li[0:BLK, j, :], mm[0:BLK, n % BANKS, 0:T], ACT.Sigmoid,
                                     bias=v("ri_b", j, j + 1, BLK)), taken(n))
                out_taken(act, lru_out_of("ra", j))
                S.did(act.activation(lt[0:BLK, j, :], lr[0:BLK, j, :], ACT.Tanh,
                                     scale=lruc[0:BLK, 5, j:j + 1]), "lru_tanh")

            act.wait_ge(sem("lru_rate"), 1)
            for j in range(NBLK):
                evacuate(lru_out_of("x", j), lx[0:BLK, j, 3:T + 3], m=BLK)
                evacuate(lru_out_of("g", j), lg[0:BLK, j, :], m=BLK)
                if j:
                    lru_act(j - 1)
            lru_act(NBLK - 1)
            act.wait_ge(sem("lru_rec"), 1)
            S.did(act.activation(lt[0:BLK], lt[0:BLK], ACT.Sqrt), "lru_root")
            out_taken(act, lru_out_of("g", NBLK - 1))
            S.did(act.activation(lg[0:BLK], lg[0:BLK], ACT.Gelu), "lru_gelu")

            def experts(L):
                squares(5 + 2 * L)
                root(5 + 2 * L)
                shift(5 + 2 * L)
                for j in range(16):
                    evacuate(OUT0[f"peer{L}_q"] + j, eq[:, j, :])
                for c in range(TT):
                    for g in range(4):
                        evacuate(OUT0[f"peer{L}_scores"] + 4 * c + g, es[:, c, 4 * g:4 * g + 4, :], width=512)
                for c in range(TT):
                    act.wait_ge(sem("best_shifted"), TT * L + c + 1)
                    S.did(act.activation(expo, shifted, ACT.Exp), "best_exp")
                for c in range(TT):
                    n = OUT0[f"peer{L}_turn"] + c
                    evacuate(n, routeT[:, :, c * P:(c + 1) * P], width=384)
                n0 = OUT0[f"peer{L}_place"]
                with act.Fori(0, T // 16) as r:
                    for j in range(4):
                        act.wait_ge(sem("outs"), r * 4 + (n0 + j + 1))
                        dst = placed[:, :, bass.ds(r * 16 + 4 * j, 4)].rearrange("p e t -> p t e")
                        act.activation(dst, mm[:, (n0 + j) % BANKS, :].rearrange("p (t e) -> p t e", t=4), ACT.Copy) \
                            .then_inc(sem(taken(n0 + j)[0]), 1)

                def hidden(j, r, first=False):
                    act.wait_ge(sem("hidden_ready"), r * SLOTS + (KEYS * L + j + 1))
                    if not (first and j < 3):
                        act.wait_ge(sem("tiles_used"), r * SLOTS + (USED0[f"peer{L}_experts"] + j - 3 + 1))
                    act.activation(mix[:, j % 3, :], mm[:, j % 3, 0:T], ACT.Gelu).then_inc(sem("hidden_taken"), 1)

                for j in range(SLOTS):
                    hidden(j, 0, True)
                with act.Fori(1, KEYS // SLOTS) as r:
                    for j in range(SLOTS):
                        hidden(j, r)
                for j in range(KEYS - KEYS // SLOTS * SLOTS):
                    hidden(j, KEYS // SLOTS)

            experts(0)

            squares(6)
            root(6)
            shift(6)
            act.wait_ge(sem("fox_nz"), 1)
            S.did(act.activation(ffe, ffn_, ACT.Exp))
            S.settle()
            S.did(act.activation(ffl, ffe, ACT.Ln, bias=1.0), "fox_ln")
            for j in range(16):
                evacuate(OUT0["fox_qk"] + j, (fq3 if j < 8 else fk3)[:, j % 8, :])
            for j in range(8):
                evacuate(OUT0["fox_v"] + j, fv[:, j % 2, (j // 2) * T:(j // 2 + 1) * T])
            for j in range(8):
                evacuate(OUT0["fox_og"] + j, fo[:, j, :], ACT.Sigmoid)
            for j in range(2):
                act.wait_ge(sem("fox_inverse"), j + 1)
                S.did(act.activation(fsq[:, j * 2048:(j + 1) * 2048], fsq[:, j * 2048:(j + 1) * 2048], ACT.Sqrt),
                      "fox_rstd")
            for i in range(FH + 2):
                if i < FH:
                    act.wait_ge(sem("fox_max"), i + 1)
                    if i >= 3:
                        out_ready(act, OUT0[f"fox_turn{i - 3}"])
                    b = i % 3
                    act.activation(fP[:, b, 0:P], fL[:, b, 0:P], ACT.Exp, bias=fnm[:, b, 0:1],
                                   accum_out=fsum[:, b, 0:1])
                    S.did(act.activation(fP[:, b, P:3 * P], fL[:, b, P:3 * P], ACT.Exp, bias=fnm[:, b, 1:2],
                                         accum_out=fsum[:, b, 1:2]), "fox_exp")
                if i >= 2:
                    hd = i - 2
                    if hd >= 3:
                        act.wait_ge(sem("fox_pv"), hd - 2)
                    evacuate(OUT0[f"fox_turn{hd}"], fPT[:, hd % 3, :], width=384)
            experts(1)

        @block.vector
        def _(dve):
            S = Steps(dve, sem, "dve_step")

            def tt(out_, a, b, op, name=None):
                S.did(dve.tensor_tensor(out_, a, b, op), name)

            def ts(out_, a, s1, s2, op0, op1=None, name=None):
                S.did(dve.tensor_scalar(out_, a, s1, s2, op0, *([op1] if op1 is not None else [])), name)

            def stt(out_, a, s, b, op0, op1, name=None, **kw):
                S.did(dve.scalar_tensor_tensor(out=out_, in0=a, scalar=s, in1=b, op0=op0, op1=op1, **kw), name)

            def bank(n, m=P, width=T):
                out_ready(dve, n)
                return mm[0:m, n % BANKS, 0:width]

            def norm(i, gain):
                n = OUT0[f"norm{i}"]
                src = bank(n)
                if i >= 1:
                    S.settle()
                ts(rstd[:, :], src, 1.0 / D, EPS, ALU.mult, ALU.add, taken(n))
                S.settle()
                S.did(dve.reciprocal(rstd[:, :], rstd[:, :]), "norm_inverse")
                dve.wait_ge(sem("norm_rstd"), i + 1)
                if i == 0:
                    dve.wait_ge(sem("vec_loaded"), 16)
                for k in range(KD):
                    name = "h_scaled" if i <= 2 else "x_done" if i == 3 and k == KD - 1 else \
                        None if i == 3 else "h_scaled2"
                    dst = x if i == 3 else h
                    stt(dst[:, k, :], x[:, k, :], gain[:, k:k + 1], rstd[:, :], ALU.mult, ALU.mult, name)

            S.did(dve.memset(cin[:, :, 0:3], 0.0), "pad_zero")
            norm(0, v("g_mix"))

            n = OUT0["small"]
            src = bank(n, width=32).rearrange("p (c j) -> p c j", c=TT)
            tt(pre, src, v("gate_bias").unsqueeze(1).to_broadcast([P, TT, 16]), ALU.add, taken(n))
            S.settle()
            S.did(dve.tensor_copy(zz[:, :, 0:4], pre[:, :, 4:8]), "pre_ready")
            ts(zz[:, :, 4:8], pre[:, :, 12:16], -1.0, None, ALU.mult)
            S.settle()
            ts(nz, zz, -1.0, None, ALU.mult)
            S.settle()
            tt(nz, nz, zz, ALU.min, "nz_ready")
            ts(sp, zz, 0.0, None, ALU.max)
            dve.wait_ge(sem("ln_ready"), 1)
            S.settle()
            tt(sp, sp, ln, ALU.add)
            S.settle()
            ts(lgt, sp, -1.0, None, ALU.mult)
            S.settle()
            dve.wait_ge(sem("expa_ready"), 1)
            tt(lgt[:, :, 0:4], lgt[:, :, 0:4], expa.unsqueeze(1).to_broadcast([P, TT, 4]), ALU.mult, "log_decays")

            for j in range(12):
                out_taken(dve, OUT0["qkv"] + j)
                w = v("conv", 4 * j, 4 * j + 4)
                ts(cv[:, j, :], cin[:, j, 0:T], w[:, 0:1], None, ALU.mult)
                for s in range(1, 4):
                    S.settle()
                    stt(cv[:, j, :], cin[:, j, s:s + T], w[:, s:s + 1], cv[:, j, :], ALU.mult, ALU.add,
                        "conv_done" if s == 3 else None)

            dve.wait_ge(sem("qkv_active"), 8)
            out_ready(dve, OUT0["norm0"])
            qk = cv[:, 0:8, :].rearrange("p j t -> p (j t)")
            tt(scratch[:, :], qk, qk, ALU.mult, "qk_squares")
            dve.wait_ge(sem("qk_sums"), 1)
            S.settle()
            ts(scratch[:, :], ms[:, :, :].rearrange("p b n -> p (b n)"), EPS, None, ALU.add, None, "qk_sums_taken")
            S.settle()
            S.did(dve.reciprocal(scratch[:, :], scratch[:, :]), "qk_inverse")
            dve.wait_ge(sem("cum_ready"), 1)
            S.did(dve.tensor_copy(cum, mm[:, 0, 0:16].rearrange("p (c j) -> p c j", c=TT)))
            S.did(dve.tensor_copy(gl, mm[:, 0, 16:20]), "cum_taken")
            S.settle()
            tt(gdif, gl, cum[:, 0, 0:4], ALU.subtract, "gdif_ready")
            ts(ngc, cum[:, :, 0:4], -1.0, None, ALU.mult)
            tt(imb, pre[:, :, 8:12], cum[:, :, 4:8], ALU.subtract)
            S.settle()
            for u in range(8):
                ts(diag[:, u, :], ident, ngc[:, u % 2, u // 2:u // 2 + 1], None, ALU.mult, None,
                   "diag_ready" if u == 7 else None)
            dve.wait_ge(sem("qk_rstd"), 1)
            stt(qk[:, 0:1024], qk[:, 0:1024], float(P) ** -0.5, scratch[:, 0:1024], ALU.mult, ALU.mult)
            tt(qk[:, 1024:2048], qk[:, 1024:2048], scratch[:, 1024:2048], ALU.mult, "qk_normal")
            dve.wait_ge(sem("rows_ready"), 1)
            for u in range(8):
                r = ms[:, u // 4, (u % 4) * P:(u % 4 + 1) * P]
                g = cum[:, u % 2, u // 2:u // 2 + 1]
                stt(decay[:, u, :], r, g, cst("mask")[:, P:2 * P], ALU.add, ALU.add)
                stt(decayT[:, u, :], r, g, cst("maskT"), ALU.add, ALU.add, "decay_logs" if u == 7 else None)
            dve.wait_ge(sem("grow_ready"), 1)
            tt(grow, grow, cv[:, 0:4, P:T], ALU.mult, "rows_taken")
            dve.wait_ge(sem("decay_ready"), 2)
            dve.wait_ge(sem("kk_ready"), 1)
            dve.wait_ge(sem("beta_ready"), 1)
            for u in range(8):
                stt(M[:, u, :], mm[:, u // 4, (u % 4) * P:(u % 4 + 1) * P], beta[:, u % 2, u // 2:u // 2 + 1],
                    decay[:, u, :], ALU.mult, ALU.mult, "M_ready" if u == 7 else None)
            dve.wait_ge(sem("kq_ready"), 1)
            tt(attnT, ms[:, 2:4, :].rearrange("p b (j t) -> p (b j) t", j=4), decayT, ALU.mult, "attnT_ready")

            def level_mask(l):
                return cst("levelsT")[:, l * P:(l + 1) * P].unsqueeze(1).to_broadcast([P, 8, P])

            identb = ident.unsqueeze(1).to_broadcast([P, 8, P])
            S.settle()
            tt(Pm, M, cst("level0").unsqueeze(1).to_broadcast([P, 8, P]), ALU.mult)
            S.settle()
            tt(X, identb, Pm, ALU.subtract)
            dve.wait_ge(sem("M_turned"), 1)
            S.did(dve.tensor_copy(MT, mm[:, 0:2, :].rearrange("p b (j t) -> p (b j) t", j=4)))
            S.settle()
            tt(Ml[0], MT, level_mask(0), ALU.mult)
            tt(Ml[1], MT, level_mask(1), ALU.mult, "corner_ready")
            dve.wait_ge(sem("v_turned"), 1)
            for u in range(8):
                ts(vb[:, u, :], ms[:, u // 4, (u % 4) * P:(u % 4 + 1) * P], beta[:, u % 2, u // 2:u // 2 + 1], None,
                   ALU.mult)
            dve.wait_ge(sem("k_turned"), 1)
            dve.wait_ge(sem("column_decays"), 1)
            for i in range(4):
                ts(kdec[:, i, :], ms[:, 2, i * P:(i + 1) * P], ekd[:, i:i + 1], None, ALU.mult)
                ts(kbg[:, i, :], ms[:, 3, i * P:(i + 1) * P], beta[:, 1, i:i + 1], ecum[:, i:i + 1], ALU.mult,
                   ALU.mult, "tokens_ready" if i == 3 else None)
            S.settle()
            for u in range(2):
                tt(XT[:, 4 * u:4 * u + 4, :], ident.unsqueeze(1).to_broadcast([P, 4, P]), Ml[0][:, 4 * u:4 * u + 4, :],
                   ALU.subtract, "X_ready")
            for l in range(1, LEVELS):
                for u in range(2):
                    dve.wait_ge(sem("MX_ready"), 2 * (l - 1) + u + 1)
                    S.did(dve.tensor_copy(Pm[:, 4 * u:4 * u + 4, :], ms[:, u, :].rearrange("p (j t) -> p j t", j=4)),
                          "MX_taken")
                if l + 1 < LEVELS:
                    tt(Ml[(l + 1) % 2], MT, level_mask(l + 1), ALU.mult, "corner_ready")
                for u in range(2):
                    sl = slice(4 * u, 4 * u + 4)
                    dve.wait_ge(sem("XMX_ready"), 2 * (l - 1) + u + 1)
                    tt(X[:, sl, :], X[:, sl, :], ms[:, u, :].rearrange("p (j t) -> p j t", j=4), ALU.subtract)
                    tt(XT[:, sl, :], XT[:, sl, :], ms[:, 2 + u, :].rearrange("p (j t) -> p j t", j=4), ALU.subtract,
                       "X_ready")
            dve.wait_ge(sem("vn0_ready"), 1)
            S.did(dve.tensor_copy(vn[0], mm[:, 0, :].rearrange("p (j t) -> p j t", j=4)), "vn0_taken")
            dve.wait_ge(sem("w_ready"), 1)
            ts(nwT, mm[:, 1, :].rearrange("p (j t) -> p j t", j=4), -1.0, None, ALU.mult, None, "w_taken")
            dve.wait_ge(sem("state_ready"), 1)
            S.did(dve.tensor_copy(S1, mm[:, 2, :].rearrange("p (j t) -> p j t", j=4)), "state_taken")
            dve.wait_ge(sem("vn1_ready"), 1)
            S.did(dve.tensor_copy(vn[1], mm[:, 0, :].rearrange("p (j t) -> p j t", j=4)), "vn1_taken")
            for u in range(8):
                ts(diag2[:, u, :], ident, imb[:, u % 2, u // 2:u // 2 + 1], None, ALU.mult, None,
                   "diag2_ready" if u == 7 else None)

            def head_norm(which, o, gain, gate, names):
                dve.wait_ge(sem("head_sums"), which + 1)
                inv = scratch[:, 1024:2048]
                ts(inv, ms[:, 2:4, :].rearrange("p b n -> p (b n)"), 1.0 / P, EPS, ALU.mult, ALU.add)
                S.settle()
                S.did(dve.reciprocal(inv, inv), "head_inverse")
                tt(gate, gate, o, ALU.mult, names[0])
                dve.wait_ge(sem("head_rstd"), which + 1)
                S.settle()
                for i in range(4):
                    stt(o[:, i, :], gate[:, i, :], gain[i], inv[:, i * T:(i + 1) * T], ALU.mult, ALU.mult,
                        names[1] if i == 3 else None)

            head_norm(0, oa, [v("gdn_norm")] * 4, gz, ("oa_done", "oa_done"))

            dve.wait_ge(sem("ml_rows_ready"), 1)
            for i in range(4):
                r = mm[:, 1 + i // 2, (i % 2) * T:(i % 2 + 1) * T]
                stt(Dlog[:, i, 0:P], r[:, 0:P], cum[:, 0, 4 + i:5 + i], cst("mask")[:, P:2 * P], ALU.add, ALU.add)
                stt(Dlog[:, i, P:3 * P], r, cum[:, 1, 4 + i:5 + i], cst("mask"), ALU.add, ALU.add,
                    "ml_rows_taken" if i == 3 else None)
            S.settle()
            S.did(dve.tensor_reduce(mx[:, 0, :], Dlog[:, :, 0:P], AX.X, ALU.max))
            S.did(dve.tensor_reduce(mx[:, 1, :], Dlog[:, :, P:3 * P], AX.X, ALU.max))
            S.settle()
            tt(mx, mx, cum[:, :, 4:8], ALU.max)
            S.settle()
            ts(nm, mx, -1.0, None, ALU.mult, None, "ml_nm")
            dve.wait_ge(sem("ml_weights"), 1)
            dve.wait_ge(sem("ml_qk_ready"), 1)
            for i in range(4):
                stt(Em[:, i, 0:P], ms[:, i, 0:P], 64.0 ** -0.5, Em[:, i, 0:P], ALU.mult, ALU.mult,
                    accum_out=den[:, 0, i:i + 1])
                stt(Em[:, i, P:3 * P], ms[:, i, P:3 * P], 64.0 ** -0.5, Em[:, i, P:3 * P], ALU.mult, ALU.mult,
                    accum_out=den[:, 1, i:i + 1])
            S.settle()
            ts(nden, den, -1.0, None, ALU.mult)
            S.settle()
            tt(nden, nden, den, ALU.max)
            S.settle()
            tt(nden, nden, flo, ALU.max)
            S.settle()
            S.did(dve.reciprocal(rden, nden))
            S.settle()
            for i in range(4):
                ts(Em[:, i, 0:P], Em[:, i, 0:P], rden[:, 0, i:i + 1], None, ALU.mult)
                ts(Em[:, i, P:3 * P], Em[:, i, P:3 * P], rden[:, 1, i:i + 1], None, ALU.mult, None,
                   "ml_scores" if i == 3 else None)
            head_norm(1, ob, [v("ml_norm", i, i + 1) for i in range(4)], mo, (None, "ob_done"))

            dve.wait_ge(sem("tiles_used"), 12 * MODS)
            tt(mod[:, :], mm[:, 3, 0:24 * MODS], v("mod_b"), ALU.add, "mods_taken")
            S.settle()
            mod3 = mod[:, :].rearrange("p (i s) -> p i s", i=MODS)
            ts(modg[:, :].rearrange("p (i s) -> p i s", i=MODS), mod3[:, :, 8:16], 1.0, None, ALU.add)
            S.settle()
            tt(modg[:, :], modg[:, :], v("norms2"), ALU.mult)

            for j in range(8):
                n = OUT0["branch_a"] + j
                tt(gates[:, j, :], bank(n), gates[:, j, :], ALU.mult, taken(n))
            for j in range(8):
                n = OUT0["branch_b"] + j
                tt(gates[:, 8 + j, :], bank(n), gates[:, 8 + j, :], ALU.mult, taken(n))
            S.settle()
            tt(gates[:, 0:8, :], gates[:, 0:8, :], gates[:, 8:16, :], ALU.add, "mixed")

            def residual(stage, gate=None):
                for j in range(KD):
                    n = OUT0[stage] + j
                    src = bank(n)
                    if gate is None:
                        tt(x[:, j, :], src, x[:, j, :], ALU.add, taken(n))
                    else:
                        stt(x[:, j, :], src, gate[:, j:j + 1], x[:, j, :], ALU.mult, ALU.add, taken(n))
                S.settle()
                S.did(dve.memset(tiny[:, 511:512], 0.0), "x_done")

            residual("w_out")
            norm(1, v("g_ffn"))
            for j in range(FFG):
                out_taken(dve, OUT0["ffn_up"] + 2 * j)
                n = OUT0["ffn_up"] + 2 * j + 1
                src = bank(n)
                tt(ffact[:, j, :], src, up[:, j % 2, :], ALU.mult, taken(n))
            residual("ffn_down")
            norm(2, v("g_ple"))
            for j in range(KD):
                n = OUT0["ple"] + j
                out_taken(dve, OUT0["ple_gate"] + j)
                src = bank(n)
                tt(pleg[:, j, :], src, pleg[:, j, :], ALU.mult, taken(n))
            S.settle()
            tt(x[:, :, :], x[:, :, :], pleg, ALU.add, "x_done")
            norm(3, v("g_final"))

            c0, c1, c2, c3, c4, c5 = (lruc[:, i, :] for i in range(6))
            ts(c4, v("lam"), -1.0, None, ALU.mult)
            S.settle()
            tt(c0, c4, v("lam"), ALU.min, "nlam_ready")
            ts(c4, c4, 0.0, None, ALU.max)
            dve.wait_ge(sem("lam_exp"), 1)
            S.settle()
            ts(c2, c1, 2.0, None, ALU.add)
            S.settle()
            S.did(dve.reciprocal(c2, c2))
            S.settle()
            tt(c1, c1, c2, ALU.mult)
            S.settle()
            tt(c2, c1, c1, ALU.mult)
            S.settle()
            ts(c3, c2, 2.0 / 17, 2.0 / 15, ALU.mult, ALU.add)
            for d in (13, 11, 9, 7, 5, 3, 1):
                S.settle()
                tt(c3, c3, c2, ALU.mult)
                S.settle()
                ts(c3, c3, 2.0 / d, None, ALU.add)
            S.settle()
            tt(c3, c3, c1, ALU.mult)
            S.settle()
            tt(c3, c3, c4, ALU.add)
            S.settle()
            ts(c5, c3, 4.0, None, ALU.mult, None, "lru_rate")
            norm(4, modg[:, 0:8])
            S.did(dve.memset(lx[0:BLK, :, 0:3], 0.0), "lru_pad_zero")
            for j in range(NBLK):
                out_taken(dve, lru_out_of("x", j))
                w = v("lru_conv", 4 * j, 4 * j + 4, BLK)
                ts(lc[0:BLK, j, :], lx[0:BLK, j, 0:T], w[:, 0:1], v("lru_conv_b", j, j + 1, BLK), ALU.mult, ALU.add)
                for s in range(1, 4):
                    S.settle()
                    stt(lc[0:BLK, j, :], lx[0:BLK, j, s:s + T], w[:, s:s + 1], lc[0:BLK, j, :], ALU.mult, ALU.add,
                        "lru_conv" if s == 3 else None)
            dve.wait_ge(sem("lru_tanh"), NBLK)
            out_taken(dve, lru_out_of("ri", NBLK - 1))
            S.settle()
            ts(lr[0:BLK], lt[0:BLK], 1.0, None, ALU.add)
            tt(li[0:BLK], li[0:BLK], lc[0:BLK], ALU.mult)
            S.settle()
            S.did(dve.reciprocal(lr[0:BLK], lr[0:BLK]), "lru_rec")
            S.settle()
            stt(li[0:BLK], lr[0:BLK], 2.0, li[0:BLK], ALU.mult, ALU.mult)
            ts(lc[0:BLK], lr[0:BLK], 2.0, -1.0, ALU.mult, ALU.add)
            dve.wait_ge(sem("lru_root"), 1)
            S.settle()
            tt(li[0:BLK], li[0:BLK], lt[0:BLK], ALU.mult)
            S.settle()
            for j in range(NBLK):
                S.did(dve.tensor_tensor_scan(lr[0:BLK, j, :], lc[0:BLK, j, :], li[0:BLK, j, :], 0.0, ALU.mult, ALU.add))
            dve.wait_ge(sem("lru_gelu"), 1)
            S.settle()
            tt(lt[0:BLK], lr[0:BLK], lg[0:BLK], ALU.mult, "lru_y")
            residual("lru_out", mod[:, 16:24])

            def experts(L):
                i = 1 + 2 * L
                norm(5 + 2 * L, modg[:, 8 * i:8 * i + 8])
                for c in range(TT):
                    route_tile(L, c)
                for c in range(TT):
                    out_taken(dve, OUT0[f"peer{L}_turn"] + c)
                def onehots(r, j, b, used):
                    if used is not None:
                        dve.wait_ge(sem("outs"), used)
                    for k in range(4):
                        t = r * 16 + (4 * j + k)
                        dve.tensor_scalar(onehot[:, b, 0, k, :], iota, routeT[:, 0, bass.ds(t, 1)],
                                          routeT[:, 2, bass.ds(t, 1)], ALU.is_equal, ALU.mult)
                        ins = dve.tensor_scalar(onehot[:, b, 1, k, :], iota, routeT[:, 1, bass.ds(t, 1)], None,
                                                ALU.is_equal)
                    ins.then_inc(sem("onehots"), 1)

                n0 = OUT0[f"peer{L}_place"]
                with dve.Fori(0, T // 16) as r:
                    for j in range(4):
                        onehots(r, j, j % 2, r * 4 + (n0 + j - 2 + 1))

                def weigh(j, r):
                    dve.wait_ge(sem("hidden_taken"), r * SLOTS + (KEYS * L + j + 1))
                    g = placed[:, bass.ds(r * SLOTS + j, 1), :].rearrange("p e t -> p (e t)")
                    dve.tensor_tensor(mix[:, j % 3, :], mix[:, j % 3, :], g, ALU.mult).then_inc(sem("weighted"), 1)

                for j in range(4):
                    out_taken(dve, n0 + T // 4 - 4 + j)
                with dve.Fori(0, KEYS // SLOTS) as r:
                    for j in range(SLOTS):
                        weigh(j, r)
                for j in range(KEYS - KEYS // SLOTS * SLOTS):
                    weigh(j, KEYS // SLOTS)
                dve.wait_ge(sem("tiles_used"), USED0[f"peer{L}_experts"] + KEYS)
                for m in range(KD):
                    g = mod[:, 24 * i + 16 + m:24 * i + 17 + m]
                    stt(x[:, m, :], ms[:, m // 2, (m % 2) * T:(m % 2 + 1) * T], g, x[:, m, :], ALU.mult, ALU.add,
                        "x_done" if m == KD - 1 else None)

            def route_tile(L, c):
                for g in range(4):
                    out_taken(dve, OUT0[f"peer{L}_scores"] + 4 * c + g)
                if c or L:
                    S.settle()

                def best16(vals, idx, src, spare, count):
                    for rnd in range(2):
                        s = src if rnd == 0 else spare
                        lo, hi = 8 * rnd, 8 * rnd + 8
                        for j in range(count):
                            S.did(dve.max(vals(j)[:, lo:hi], s(j)))
                        S.settle()
                        for j in range(count):
                            S.did(dve.max_index(idx(j)[:, lo:hi], vals(j)[:, lo:hi], s(j)))
                        if rnd == 0:
                            for j in range(count):
                                S.did(dve.match_replace(spare(j), vals(j)[:, 0:8], src(j), LOWEST))
                            S.settle()
                    S.settle()

                best16(lambda j: top[:, j // 2, j % 2, :], lambda j: topi[:, j // 2, j % 2, :],
                       lambda j: es[:, c, j, :], lambda j: es2[:, j, :], 16)
                S.did(dve.tensor_copy(topf_flat, topi_flat))
                cand4 = cand.rearrange("p j (a b) -> p j a b", a=16)
                for j in range(PH):
                    tt(cand4[:, j], top[:, j, 0, :].unsqueeze(2).to_broadcast([P, 16, 16]),
                       top[:, j, 1, :].unsqueeze(1).to_broadcast([P, 16, 16]), ALU.add)
                S.settle()
                besti3 = besti.rearrange("p (j k) -> p j k", j=PH)
                best16(lambda j: best[:, j, :], lambda j: besti3[:, j, :],
                       lambda j: cand[:, j, :], lambda j: cand2[:, j, :], PH)
                ts(part[:, 0, :], besti, 4, None, ALU.logical_shift_right)
                ts(part[:, 1, :], besti, 15, None, ALU.bitwise_and)
                if c or L:
                    dve.wait_ge(sem("best_exp"), TT * L + c)
                tt(shifted, best, best[:, :, 0:1].to_broadcast([P, PH, 16]), ALU.subtract, "best_shifted")
                S.settle()
                S.did(dve.tensor_copy(partf, part))
                S.settle()
                for s in range(2):
                    hot3 = hot.rearrange("p (q a) -> p q a", a=16)
                    tt(hot3, partf[:, s, :].unsqueeze(2).to_broadcast([P, P, 16]),
                       iota[:, 0:16].unsqueeze(1).to_broadcast([P, P, 16]), ALU.is_equal)
                    S.settle()
                    hot4 = hot.rearrange("p (j k a) -> p j k a", j=PH, k=16)
                    prod = hot2.rearrange("p (j k a) -> p j k a", j=PH, k=16)
                    for j in range(PH):
                        tt(prod[:, j], hot4[:, j], topf[:, j, s, :].unsqueeze(1).to_broadcast([P, 16, 16]), ALU.mult)
                    S.settle()
                    S.did(dve.tensor_reduce(route[:, c, s, :], hot2.rearrange("p (q a) -> p q a", a=16), AX.X,
                                            ALU.add))
                dve.wait_ge(sem("best_exp"), TT * L + c + 1)
                S.did(dve.tensor_reduce(sums, expo, AX.X, ALU.add))
                S.settle()
                S.did(dve.reciprocal(rsums, sums))
                S.settle()
                tt(route[:, c, 2, :].rearrange("p (j k) -> p j k", j=PH), expo,
                   rsums.unsqueeze(2).to_broadcast([P, PH, 16]), ALU.mult, "routed")

            experts(0)

            norm(6, modg[:, 16:24])
            n = OUT0["fox_small"]
            src = bank(n, width=32).rearrange("p (c j) -> p c j", c=TT)
            tt(ffz, src, v("fox_fb").unsqueeze(1).to_broadcast([P, TT, 16]), ALU.add, taken(n))
            S.settle()
            ts(ffs, ffz, -1.0, None, ALU.mult)
            S.settle()
            tt(ffn_, ffs, ffz, ALU.min, "fox_nz")
            ts(ffs, ffs, 0.0, None, ALU.max)
            dve.wait_ge(sem("fox_ln"), 1)
            S.settle()
            tt(ffs, ffs, ffl, ALU.add)
            S.settle()
            S.did(dve.memset(tiny[:, 509:510], 0.0), "fox_logf")
            n += 1
            S.did(dve.tensor_copy(fcum, bank(n, width=32).rearrange("p (c j) -> p c j", c=TT)), taken(n))
            S.settle()
            for hd in range(FH):
                for c in range(TT):
                    ts(fd[:, hd, c, :], ident, fcum[:, c, hd:hd + 1], None, ALU.mult, None,
                       "fox_diag" if hd == FH - 1 and c == TT - 1 else None)
            S.settle()
            ts(fcum, fcum, -1.0, None, ALU.mult)
            ts(fqg, v("fox_qg"), FE ** -0.5, None, ALU.mult)
            for s, f in enumerate((fq, fk)):
                for j in range(KD):
                    out_taken(dve, OUT0["fox_qk"] + 8 * s + j)
                tt(fsq[:, s * 2048:(s + 1) * 2048], f, f, ALU.mult, "fox_sq")
            for s, f in enumerate((fq, fk)):
                sq = fsq[:, s * 2048:(s + 1) * 2048]
                out_ready(dve, OUT0["fox_squares"] + 4 * s + 3)
                S.settle()
                for j in range(4):
                    n = OUT0["fox_squares"] + 4 * s + j
                    ts(sq[:, j * 512:(j + 1) * 512], bank(n, width=512), 1.0 / FE, EPS, ALU.mult, ALU.add, taken(n))
                S.settle()
                S.did(dve.reciprocal(sq, sq), "fox_inverse")
            for s, f in enumerate((fq, fk)):
                dve.wait_ge(sem("fox_rstd"), s + 1)
                stt(f, f, fqg if s == 0 else v("fox_kg"), fsq[:, s * 2048:(s + 1) * 2048], ALU.mult, ALU.mult,
                    "fox_normal")
            for i in range(FH + 4):
                if i < FH:
                    b = i % 3
                    n = OUT0[f"fox_scores{i}"]
                    src = bank(n, width=384)
                    if i >= 3:
                        dve.wait_ge(sem("fox_exp"), i - 2)
                    stt(fL[:, b, 0:P], src[:, 0:P], fcum[:, 0, i:i + 1], cst("mask")[:, P:2 * P], ALU.add, ALU.add)
                    stt(fL[:, b, P:3 * P], src[:, P:3 * P], fcum[:, 1, i:i + 1], cst("mask"), ALU.add, ALU.add, taken(n))
                    S.settle()
                    S.did(dve.tensor_reduce(fmx[:, b, 0:1], fL[:, b, 0:P], AX.X, ALU.max))
                    S.did(dve.tensor_reduce(fmx[:, b, 1:2], fL[:, b, P:3 * P], AX.X, ALU.max))
                    S.settle()
                    ts(fnm[:, b, :], fmx[:, b, :], -1.0, None, ALU.mult, None, "fox_max")
                if 1 <= i <= FH:
                    b = (i - 1) % 3
                    dve.wait_ge(sem("fox_exp"), i)
                    S.did(dve.reciprocal(frs[:, b, :], fsum[:, b, :]))
                    S.settle()
                    ts(fP[:, b, 0:P], fP[:, b, 0:P], frs[:, b, 0:1], None, ALU.mult)
                    ts(fP[:, b, P:3 * P], fP[:, b, P:3 * P], frs[:, b, 1:2], None, ALU.mult, None, "fox_probs")
                if i >= 5 and i % 2 == 1:
                    a = (i - 5) // 2
                    dve.wait_ge(sem("fox_pv"), 2 * a + 2)
                    tt(fy[:, a, :], ms[:, a % 4, 0:T], fo[:, a, :], ALU.mult, "fox_y")
            residual("fox_out", mod[:, 24 * 2 + 16:24 * 2 + 24])
            experts(1)


def host_constants():
    c = np.zeros((P, CONSTW), np.float32)
    i, j = np.arange(P)[:, None], np.arange(P)[None, :]

    def put(name, a):
        c[:, CONST0[name][0]:CONST0[name][1]] = a

    put("ident", i == j)
    put("upper", i <= j)
    put("ones", 1.0)
    put("heads", i // 64 == j // 64)
    put("iota", j + 0 * i)
    put("mask", np.concatenate([np.zeros((P, P)), np.where(j > i, -BIG, 0.0)], 1))
    put("maskT", np.where(j < i, BIG, 0.0))
    levels = []
    for l in range(LEVELS):
        b = 1 << l
        levels.append((i // (2 * b) == j // (2 * b)) & (i % (2 * b) >= b) & (j % (2 * b) < b))
    put("level0", levels[0])
    put("levelsT", np.concatenate([m.T for m in levels], 1))
    return c


def columns(w, rows=P):
    k, n = w.shape
    return w.reshape(k // P, P, n // 256, 256).transpose(2, 1, 0, 3).reshape(n // 256, P, -1)


def kernel(**inputs):
    import concourse.bacc as bacc
    from concourse.bass_utils import run_bass_kernel_spmd

    a = {k: np.asarray(val) for k, val in inputs.items()}
    w_in = a["w_in"][0]
    at = np.cumsum([0, 512, 512, 512, 512, 4, 4, 256, 256, 512, 512, 4, 4, 1024, 1024])
    gq, gk, gv, gz, gb, ga, mq, mk, mv, mo, mi, mf, ta, tb = (w_in[:, s:e] for s, e in zip(at[:-1], at[1:]))

    def rows4(w):
        return w.reshape(4, P, 2, 512).transpose(2, 1, 0, 3).reshape(2, P, 2048)

    s = {}
    s["qkv"] = columns(np.concatenate([gq, gk, gv], 1))
    s["gz"] = columns(gz)
    s["mqk"] = columns(np.concatenate([mq, mk], 1))
    s["mv"] = columns(mv)
    s["mo"] = columns(mo)
    s["gates"] = columns(np.concatenate([ta, tb], 1))
    mods = ["l0_mix", "l0_ffn", "l1_mix", "l1_ffn"]
    s["mod"] = np.concatenate([columns(a[f"{m}_mod_w_2"]) for m in mods], 0)
    s["branch_a"] = rows4(a["w_branch_a"][0])
    s["branch_b"] = rows4(a["w_branch_b"][0])
    s["w_out"] = columns(a["w_out"][0])
    both = np.stack([a["w1"][0].reshape(D, FFG, P), a["w3"][0].reshape(D, FFG, P)], 2).reshape(D, FFG * 256)
    s["ffn_up"] = columns(both)
    s["ffn_down"] = a["w2"][0].reshape(2, 11, P, KD, P).transpose(3, 0, 2, 1, 4).reshape(16, P, 1408)
    s["ple_gate"] = columns(a["w_ple_gate"][0])
    s["ple"] = a["w_ple"][0].reshape(2, P, D).transpose(1, 0, 2).reshape(1, P, 2048)
    s["lru_in"] = a["l0_lru_in_w_2"].reshape(KD, P, 2, NBLK, BLK).transpose(3, 1, 2, 0, 4).reshape(NBLK, P, -1)
    lo = np.zeros((KD, 96, NBLK, P), np.float32)
    lo[:, 0:BLK] = a["l0_lru_out_w_2"].reshape(NBLK, BLK, KD, P).transpose(2, 1, 0, 3)
    s["lru_out"] = lo.reshape(KD, 96, 2048)
    fox = a["l1_fox_in_w_2"]
    s["fox_qk"] = columns(fox[:, 0:2 * D])
    s["fox_v"] = columns(fox[:, 2 * D:3 * D])
    s["fox_og"] = columns(fox[:, 3 * D + FH:])
    s["fox_out"] = columns(a["l1_fox_out_w_2"])
    for L in range(2):
        s[f"peer{L}_q"] = columns(a[f"l{L}_peer_q_w_2"])
        keys = np.stack([a[f"l{L}_peer_subkey1_2"], a[f"l{L}_peer_subkey2_2"]], 1)
        s[f"peer{L}_keys"] = keys.transpose(3, 0, 1, 2).reshape(1, P, 2048)
        u = a[f"l{L}_peer_u_2"].reshape(KEYS, KEYS, KD, P).transpose(1, 3, 2, 0).reshape(KEYS, P, D)
        vv = a[f"l{L}_peer_v_2"].reshape(KEYS, KEYS, D).transpose(1, 0, 2)
        s[f"peer{L}_experts"] = np.concatenate([u, vv], 2)

    def per_channel(w):
        return w.reshape(-1, P).T

    def blocks88(w):
        o = np.zeros((P, NBLK), np.float32)
        o[0:BLK] = w.reshape(NBLK, BLK).T
        return o

    vecs = np.zeros((P, VECW), np.float32)

    def put(name, w):
        vecs[:, VEC0[name][0]:VEC0[name][1]] = w

    put("g_mix", per_channel(a["g_mix"]))
    put("g_ffn", per_channel(a["g_ffn"]))
    put("g_ple", per_channel(a["g_ple"]))
    put("g_final", per_channel(a["g_final"]))
    put("gdn_norm", a["gdn_norm"][0][:, None])
    put("ml_norm", a["ml_norm"][0].T)
    put("conv", a["conv_w"][0].reshape(4, 12, P).transpose(2, 1, 0).reshape(P, 48))
    put("norms2", np.concatenate([per_channel(a[f"{m}_norm_g_2"]) for m in mods], 1))
    put("mod_b", np.concatenate([per_channel(a[f"{m}_mod_b_2"]) for m in mods], 1))
    put("c", per_channel(a["c_2"]))
    zero4 = np.zeros(4, np.float32)
    put("gate_bias", np.concatenate([zero4, a["dt_bias"][0], a["ml_i_bias"][0], a["ml_f_bias"][0]])[None, :])
    put("a_log", a["a_log"][0][None, :])
    lcw = np.zeros((P, NBLK, 4), np.float32)
    lcw[0:BLK] = a["l0_lru_conv_w_2"].reshape(4, NBLK, BLK).transpose(2, 1, 0)
    put("lru_conv", lcw.reshape(P, 64))
    put("lru_conv_b", blocks88(a["l0_lru_conv_b_2"]))
    put("ra_b", blocks88(a["l0_lru_ra_b_2"]))
    put("ri_b", blocks88(a["l0_lru_ri_b_2"]))
    put("lam", blocks88(a["l0_lru_lambda_2"]))
    put("fox_fb", a["l1_fox_f_b_2"][None, :])
    put("fox_qg", np.concatenate([a["l1_fox_q_norm_g_2"]] * 2)[:, None])
    put("fox_kg", np.concatenate([a["l1_fox_k_norm_g_2"]] * 2)[:, None])

    lgw = np.zeros((96, NBLK, 2, BLK), np.float32)
    lgw[0:BLK, :, 0] = a["l0_lru_ra_w_2"].transpose(1, 0, 2)
    lgw[0:BLK, :, 1] = a["l0_lru_ri_w_2"].transpose(1, 0, 2)

    arrays = {f"w_{name}": w for name, w in s.items()}
    arrays["xT"] = a["x"][0].T.reshape(KD, P, T).transpose(1, 0, 2)
    arrays["pT"] = a["p"][0, 0].T.reshape(2, P, T).transpose(1, 0, 2)
    arrays["consts"] = host_constants()
    arrays["vecs"] = vecs
    arrays["small_w"] = np.concatenate([gb, ga, mi, mf], 1).reshape(KD, P, 16).transpose(1, 0, 2)
    arrays["fox_f_w"] = fox[:, 3 * D:3 * D + FH].reshape(KD, P, 16).transpose(1, 0, 2)
    arrays["lru_gate_w"] = lgw
    arrays = {k: np.ascontiguousarray(w) for k, w in arrays.items()}

    nc = bacc.Bacc("TRN2", target_bir_lowering=False, num_devices=1, dynamic_dma_scratch_size=1024)
    dram = {k: nc.dram_tensor(k, list(w.shape), F32, kind="ExternalInput").ap() for k, w in arrays.items()}
    out = nc.dram_tensor("out", [P, KD, T], F32, kind="ExternalOutput").ap()
    build(nc, {name: dram[f"w_{name}"] for name in s}, *(dram[k] for k in (
        "xT", "pT", "consts", "vecs", "small_w", "fox_f_w", "lru_gate_w")), out)
    r = run_bass_kernel_spmd(nc, [arrays], core_ids=[0])
    y = r.results[0]["out"]
    return y.transpose(2, 1, 0).reshape(1, T, D)
```

```python
from contextlib import ExitStack

import numpy as np

import concourse.bass as bass
from concourse import mybir

F32 = mybir.dt.float32
F32R = mybir.dt.float32r
U32 = mybir.dt.uint32
ACT = mybir.ActivationFunctionType
ALU = mybir.AluOpType
AX = mybir.AxisListType

P = 128
T = 256
TT = T // P
D = 1024
KD = D // P
EPS = 1e-6
BIG = 1e30
LOWEST = -3e38

RAW = 4
CUT = 3
SLOT = 1024
UNROLL = 6
LAG = 2
BANKS = 4

GH = 4
FF = 2816
FFG = FF // P
BLK = 88
NBLK = 16
FH = 16
FE = 64
PH = 8
TOPK = 16
KEYS = 128
LEVELS = 7
MODS = 4

STREAM = [
    ("qkv", 12, 1024, P, True), ("gz", 4, 1024, P, True), ("mqk", 4, 1024, P, True), ("mv", 4, 1024, P, True),
    ("mo", 4, 1024, P, True), ("gates", 16, 1024, P, True), ("mod", 24 * MODS, 1024, P, False),
    ("branch_a", 4, 1024, P, True), ("branch_b", 4, 1024, P, True), ("w_out", 8, 1024, P, True),
    ("ffn_up", 2 * FFG, 1024, P, True), ("ffn_down", 24, 1024, P, True), ("ple_gate", 8, 1024, P, True),
    ("ple", 2, 1024, P, False),
    ("lru_in", 2 * NBLK, KD * BLK, P, True), ("lru_out", 2 * KD, 1024, 96, True),
    ("peer0_q", 16, 1024, P, True), ("peer0_keys", 2, 1024, P, False), ("peer0_experts", 2 * KEYS, 1024, P, True),
    ("fox_qk", 16, 1024, P, True), ("fox_v", 8, 1024, P, True), ("fox_og", 8, 1024, P, True),
    ("fox_out", 8, 1024, P, True),
    ("peer1_q", 16, 1024, P, True), ("peer1_keys", 2, 1024, P, False), ("peer1_experts", 2 * KEYS, 1024, P, True),
]
DOWN = (8, 8, 6)
TILE0 = {}
CUT0 = {}
RUN_END = {}
_n = _q = 0
for _name, _count, _w, _p, _cut in STREAM:
    TILE0[_name] = _n
    _n += _count
    if _cut:
        CUT0[_name] = _q
        _q += _count
_end = _q
for _name, _count, _w, _p, _cut in reversed(STREAM):
    if _cut:
        RUN_END[_name] = _end - 1
    elif _name in ("mod", "ple", "peer0_keys", "peer1_keys"):
        _end = min([CUT0[k] for k in CUT0 if TILE0[k] > TILE0[_name]])

CONSTS = [("ident", P), ("upper", P), ("ones", P), ("heads", P), ("iota", P), ("mask", 2 * P),
          ("maskT", P), ("level0", P), ("levelsT", LEVELS * P)]
CONST0 = {}
_n = 0
for _name, _w in CONSTS:
    CONST0[_name] = (_n, _n + _w)
    _n += _w
CONSTW = _n
CON_KEPT = CONST0["maskT"][0]

VECS = [("g_mix", 8), ("g_ffn", 8), ("g_ple", 8), ("g_final", 8), ("gdn_norm", 1), ("ml_norm", 4),
        ("conv", 48), ("norms2", 32), ("mod_b", 96), ("c", 8), ("gate_bias", 16), ("a_log", 4),
        ("lru_conv", 64), ("lru_conv_b", 16), ("ra_b", 16), ("ri_b", 16), ("lam", 16),
        ("fox_fb", 16), ("fox_qg", 1), ("fox_kg", 1)]
VEC0 = {}
_n = 0
for _name, _w in VECS:
    VEC0[_name] = (_n, _n + _w)
    _n += _w
VECW = _n


class Signals:

    def __init__(self, nc, ctx):
        self.nc, self.ctx, self.sems = nc, ctx, {}

    def __call__(self, name):
        if name not in self.sems:
            self.sems[name] = self.ctx.enter_context(self.nc.semaphore(name))
        return self.sems[name]


class Steps:

    def __init__(self, eng, sem, own):
        self.eng, self.sem, self.own, self.count, self.last = eng, sem, own, {}, None

    def did(self, ins, name=None):
        if isinstance(name, tuple):
            self.last = name
        else:
            name = name or self.own
            self.count[name] = self.count.get(name, 0) + 1
            self.last = (name, self.count[name])
        ins.then_inc(self.sem(self.last[0]), 1)

    def settle(self):
        self.eng.wait_ge(self.sem(self.last[0]), self.last[1])


def fox_order():
    order = []
    for i in range(FH + 3):
        if i < FH:
            order.append(("scores", i))
        if 0 <= i - 2 < FH:
            order.append(("turn", i - 2))
        if 0 <= i - 3 < FH:
            order.append(("values", i - 3))
    return order


def count_outs():
    at, n = {}, 0

    def stage(name, count):
        nonlocal n
        at[name] = n
        n += count

    stage("norm0", 1)
    stage("small", 1)
    stage("qkv", 12)
    stage("gz", 4)
    stage("mqk", 4)
    stage("mv", 4)
    stage("mo", 4)
    stage("gates", 16)
    stage("branch_a", 8)
    stage("branch_b", 8)
    stage("w_out", 8)
    stage("norm1", 1)
    stage("ffn_up", 2 * FFG)
    stage("ffn_down", 8)
    stage("norm2", 1)
    stage("ple_gate", 8)
    stage("ple", 8)
    stage("norm3", 1)
    stage("norm4", 1)
    stage("lru", 4 * NBLK)
    stage("lru_out", 8)
    for layer in range(2):
        stage(f"norm{5 + 2 * layer}", 1)
        stage(f"peer{layer}_q", 16)
        stage(f"peer{layer}_scores", 8)
        stage(f"peer{layer}_turn", TT)
        stage(f"peer{layer}_place", T // 4)
        if layer == 0:
            stage("norm6", 1)
            stage("fox_small", 2)
            stage("fox_qk", 16)
            stage("fox_v", 8)
            stage("fox_og", 8)
            stage("fox_squares", 8)
            for kind, h in fox_order():
                if kind != "values":
                    stage(f"fox_{kind}{h}", 1)
            stage("fox_out", 8)
    return at


OUT0 = count_outs()


def lru_out_of(kind, j):
    base = OUT0["lru"]
    if kind in ("x", "g"):
        return base + (2 * j if j == 0 else 2 + 4 * (j - 1)) + (kind == "g")
    return base + (4 * j + 4 if j < NBLK - 1 else 4 * NBLK - 2) + (kind == "ri")


USED0, _n = {}, 0
for _name, _count in (("mv", 2), ("mod", 24 * MODS), ("ffn_down", 2 * KD), ("lru_out", KD), ("peer0_experts", KEYS),
                      ("fox_v", 4), ("peer1_experts", KEYS)):
    USED0[_name] = _n
    _n += _count


def expert_tile(i):
    if i < LAG:
        return "u", i
    if i >= 2 * KEYS - LAG:
        return "v", i - KEYS
    return ("u", LAG + (i - LAG) // 2) if (i - LAG) % 2 == 0 else ("v", (i - LAG) // 2)


def tile_used(name, i):
    if name.endswith("experts"):
        kind, s = expert_tile(i)
        return ("hidden_ready", KEYS * int(name[4]) + s + 1) if kind == "u" else ("tiles_used", USED0[name] + s + 1)
    if name == "mod":
        return "tiles_used", USED0[name] + i + 1
    if name in ("mv", "fox_v"):
        return ("tiles_used", USED0[name] + i // 2 + 1) if i % 2 == 0 else ("outs", OUT0[name] + i + 1)
    if name == "ffn_down":
        m, part_ = i // 3, i % 3
        return ("tiles_used", USED0[name] + 2 * m + part_ + 1) if part_ < 2 else ("outs", OUT0[name] + m + 1)
    if name == "lru_out":
        return ("tiles_used", USED0[name] + i // 2 + 1) if i % 2 == 0 else ("outs", OUT0[name] + i // 2 + 1)
    if name == "lru_in":
        return "outs", lru_out_of("xg"[i % 2], i // 2) + 1
    if name.endswith("keys"):
        return "outs", OUT0[name.replace("keys", "scores")] + 6 + 2 * i
    per_tile = {"branch_a": 2, "branch_b": 2, "ple": 4}.get(name, 1)
    return "outs", OUT0[name] + per_tile * (i + 1)


H_NORMS = (0, 1, 2, 4, 5, 6, 7)


def tile_shape(name, i):
    for name_, _, width, rows, _ in STREAM:
        if name_ == name:
            return rows, P * DOWN[i % 3] if name == "ffn_down" else width


TILES = [(name, i) for name, count, _, _, _ in STREAM for i in range(count)]
CUTS = [(name, i) for name, count, _, _, cut in STREAM if cut for i in range(count)]


def raw_free(n):
    name, i = TILES[n]
    return ("low_done", CUT0[name] + i + 1) if name in CUT0 else tile_used(name, i)


def cut_free(q):
    return tile_used(*CUTS[q])


def build(nc, streams, xT, pT, consts, vecs, small_w, fox_f_w, lru_gate_w, out):
    with ExitStack() as ctx:
        sem = Signals(nc, ctx)

        def sb(name, shape, dt=F32):
            return ctx.enter_context(nc.sbuf_tensor(name, shape, dt))

        ring = sb("ring", [P, RAW, SLOT])
        high = sb("high", [P, CUT, SLOT], F32R)
        low = sb("low", [P, CUT, SLOT], F32R)
        x = sb("x", [P, KD, T])
        hs = sb("hs", [P, 2, KD, T], F32R)
        wts = sb("wts", [P, 3, 2, T], F32R)
        scratch = sb("scratch", [P, KD * T])
        con = sb("con", [P, CON_KEPT])
        vec = sb("vec", [P, VECW])
        wsmall = sb("wsmall", [P, KD, 16])
        wfox = sb("wfox", [P, KD, 16])
        rstd = sb("rstd", [P, T])
        mod = sb("mod", [P, 24 * MODS])
        modg = sb("modg", [P, KD * MODS])
        csilu = sb("csilu", [P, KD])
        lruc = sb("lruc", [P, 6, NBLK])
        routeT = sb("routeT", [P, 3, T])
        tiny = sb("tiny", [P, 512])
        with nc.sbuf_tensor("work", [P, KEYS * T], F32) as work:
            pass
        parts_ = ctx.enter_context(nc.sbuf_tensor("parts", [P, 2 * FFG * T], F32R))

        mm = ctx.enter_context(nc.psum_tensor("mm", [P, BANKS, 512], F32))
        ms = ctx.enter_context(nc.psum_tensor("ms", [P, 4, 512], F32))

        def cst(name):
            a_, b_ = CONST0[name]
            if a_ >= CON_KEPT:
                return masks[:, a_ - CON_KEPT:b_ - CON_KEPT]
            return con[:, a_:b_]

        def v(name, a=None, b=None, p=P):
            lo, hi = VEC0[name]
            return vec[0:p, lo + (a or 0):(hi if b is None else lo + b)]

        ident, upper, ones, heads64, iota = cst("ident"), cst("upper"), cst("ones"), cst("heads"), cst("iota")

        free = [0]

        def area(n, at=None):
            a = free[0] if at is None else at
            free[0] = a + n
            assert free[0] <= KEYS * T
            return work[:, a:a + n]

        def parts(groups, at=None):
            a = free[0] if at is None else at
            free[0] = a + 2 * groups * T
            assert free[0] <= 2 * FFG * T
            return parts_[:, a:a + 2 * groups * T].rearrange("p (s j t) -> p s j t", s=2, j=groups)

        cin = area(12 * (T + 3)).rearrange("p (j t) -> p j t", j=12)
        cv = area(12 * T).rearrange("p (j t) -> p j t", j=12)
        gz = area(GH * T).rearrange("p (j t) -> p j t", j=GH)
        mq = area(2 * T).rearrange("p (j t) -> p j t", j=2)
        mk = area(2 * T).rearrange("p (j t) -> p j t", j=2)
        mv = area(TT * 512).rearrange("p (c f) -> p c f", c=TT)
        mo = area(GH * T).rearrange("p (j t) -> p j t", j=GH)
        gates = area(16 * T).rearrange("p (j t) -> p j t", j=16)
        diag_at = free[0]
        diag = area(16 * P).rearrange("p (j t) -> p j t", j=16)
        vb = area(8 * P, diag_at).rearrange("p (j t) -> p j t", j=8)
        kbg = area(4 * P).rearrange("p (j t) -> p j t", j=4)
        kdec = area(4 * P).rearrange("p (j t) -> p j t", j=4)
        decay = area(8 * P).rearrange("p (j t) -> p j t", j=8)
        decayT = area(8 * P).rearrange("p (j t) -> p j t", j=8)
        grow = area(4 * P).rearrange("p (j t) -> p j t", j=4)
        m_at = free[0]
        M = area(8 * P).rearrange("p (j t) -> p j t", j=8)
        MT = area(8 * P).rearrange("p (j t) -> p j t", j=8)
        attnT = area(8 * P).rearrange("p (j t) -> p j t", j=8)
        x_at = free[0]
        X = area(8 * P).rearrange("p (j t) -> p j t", j=8)
        XT = area(8 * P).rearrange("p (j t) -> p j t", j=8)
        Pm = area(8 * P).rearrange("p (j t) -> p j t", j=8)
        ml_at = free[0]
        Ml = [area(8 * P).rearrange("p (j t) -> p j t", j=8) for _ in range(2)]
        vn = [area(4 * P).rearrange("p (j t) -> p j t", j=4) for _ in range(2)]
        nwT = area(4 * P).rearrange("p (j t) -> p j t", j=4)
        S1 = area(4 * P).rearrange("p (j t) -> p j t", j=4)
        oa = area(GH * T).rearrange("p (j t) -> p j t", j=GH)
        masks = area(CONSTW - CON_KEPT)
        free_ = free[0]
        oas = parts(GH, 0)
        obs = parts(GH)
        mixs = parts(KD)
        free[0] = free_
        Dlog = area(4 * 384, ml_at).rearrange("p (j t) -> p j t", j=4)
        Em = area(4 * 384, m_at).rearrange("p (j t) -> p j t", j=4)
        ST = area(4 * 384, x_at).rearrange("p (j t) -> p j t", j=4)
        diag2 = area(8 * P, diag_at).rearrange("p (j t) -> p j t", j=8)
        ob = area(GH * T, diag_at + 8 * P).rearrange("p (j t) -> p j t", j=GH)
        ffs_ = parts(FFG, 0)
        ffact = area(2 * T).rearrange("p (j t) -> p j t", j=2)
        up = area(2 * T).rearrange("p (j t) -> p j t", j=2)
        pleg = area(KD * T).rearrange("p (j t) -> p j t", j=KD)
        pTs = area(2 * T).rearrange("p (j t) -> p j t", j=2)
        lx = area(NBLK * (T + 3), 0).rearrange("p (j t) -> p j t", j=NBLK)
        lc = area(NBLK * T).rearrange("p (j t) -> p j t", j=NBLK)
        lg = area(NBLK * T).rearrange("p (j t) -> p j t", j=NBLK)
        lt = area(NBLK * T).rearrange("p (j t) -> p j t", j=NBLK)
        li = area(NBLK * T).rearrange("p (j t) -> p j t", j=NBLK)
        lr = area(NBLK * T).rearrange("p (j t) -> p j t", j=NBLK)
        ys = parts(NBLK, 0)
        free[0] = (NBLK * (T + 3)) + 5 * NBLK * T
        lgw = area(NBLK * 2 * BLK).rearrange("p (j g d) -> p j g d", j=NBLK, g=2)
        fys = parts(KD, 0)
        fq = area(KD * T)
        fk = area(KD * T)
        fv = area(TT * D).rearrange("p (c f) -> p c f", c=TT)
        fo = area(KD * T).rearrange("p (j t) -> p j t", j=KD)
        fsq = area(2 * KD * T)
        fd = area(TT * FH * P).rearrange("p (j c t) -> p j c t", j=FH, c=TT)
        fL = area(3 * 384).rearrange("p (j t) -> p j t", j=3)
        fP = area(3 * 384).rearrange("p (j t) -> p j t", j=3)
        fPT = area(3 * 384).rearrange("p (j t) -> p j t", j=3)
        fy = area(2 * T).rearrange("p (j t) -> p j t", j=2)
        fq3 = fq.rearrange("p (j t) -> p j t", j=KD)
        fk3 = fk.rearrange("p (j t) -> p j t", j=KD)
        eq = area(16 * T, 0).rearrange("p (j t) -> p j t", j=16)
        es = area(TT * 16 * KEYS).rearrange("p (c j n) -> p c j n", c=TT, j=16)
        es2 = area(16 * KEYS).rearrange("p (j n) -> p j n", j=16)
        cand = area(PH * 256).rearrange("p (j n) -> p j n", j=PH)
        cand2 = area(PH * 256).rearrange("p (j n) -> p j n", j=PH)
        hot = area(PH * 256)
        hot2 = area(PH * 256)
        top = area(2 * PH * 16).rearrange("p (s j k) -> p j s k", j=PH, s=2)
        topi_flat = area(2 * PH * 16).bitcast(U32)
        topi = topi_flat.rearrange("p (s j k) -> p j s k", j=PH, s=2)
        topf_flat = area(2 * PH * 16)
        topf = topf_flat.rearrange("p (s j k) -> p j s k", j=PH, s=2)
        best = area(PH * 16).rearrange("p (j k) -> p j k", j=PH)
        besti = area(PH * 16).bitcast(U32)
        part = area(2 * PH * 16).bitcast(U32).rearrange("p (s k) -> p s k", s=2)
        partf = area(2 * PH * 16).rearrange("p (s k) -> p s k", s=2)
        shifted = area(PH * 16).rearrange("p (j k) -> p j k", j=PH)
        expo = area(PH * 16).rearrange("p (j k) -> p j k", j=PH)
        sums = area(PH)
        rsums = area(PH)
        route = area(TT * 3 * P).rearrange("p (c s k) -> p c s k", c=TT, s=3)
        placed = work[:, :].rearrange("p (e t) -> p e t", e=KEYS)
        mix = scratch[:, 0:3 * T].rearrange("p (j t) -> p j t", j=3)
        hf = scratch[:, :].rearrange("p (j t) -> p j t", j=KD)
        onehot = scratch[:, :].rearrange("p (b s i n) -> p b s i n", b=2, s=2, i=4)

        def col(a, n):
            return tiny[:, a:a + n]

        pre = col(0, 32).rearrange("p (c j) -> p c j", c=TT)
        zz = col(32, 16).rearrange("p (c j) -> p c j", c=TT)
        nz = col(48, 16).rearrange("p (c j) -> p c j", c=TT)
        en = col(64, 16).rearrange("p (c j) -> p c j", c=TT)
        ln = col(80, 16).rearrange("p (c j) -> p c j", c=TT)
        sp = col(96, 16).rearrange("p (c j) -> p c j", c=TT)
        expa = col(112, 4)
        lgt = col(116, 16).rearrange("p (c j) -> p c j", c=TT)
        beta = col(132, 8).rearrange("p (c j) -> p c j", c=TT)
        cum = col(140, 16).rearrange("p (c j) -> p c j", c=TT)
        gl = col(156, 4)
        ecum = col(160, 4)
        ekd = col(164, 4)
        gdif = col(168, 4)
        ngc = col(172, 8).rearrange("p (c j) -> p c j", c=TT)
        imb = col(180, 8).rearrange("p (c j) -> p c j", c=TT)
        mx = col(188, 8).rearrange("p (c j) -> p c j", c=TT)
        nm = col(196, 8).rearrange("p (c j) -> p c j", c=TT)
        flo = col(204, 8).rearrange("p (c j) -> p c j", c=TT)
        den = col(212, 8).rearrange("p (c j) -> p c j", c=TT)
        nden = col(220, 8).rearrange("p (c j) -> p c j", c=TT)
        rden = col(228, 8).rearrange("p (c j) -> p c j", c=TT)
        ffz = col(256, 32).rearrange("p (c j) -> p c j", c=TT)
        ffn_ = col(288, 32).rearrange("p (c j) -> p c j", c=TT)
        ffe = col(320, 32).rearrange("p (c j) -> p c j", c=TT)
        ffl = col(352, 32).rearrange("p (c j) -> p c j", c=TT)
        ffs = col(384, 32).rearrange("p (c j) -> p c j", c=TT)
        fcum = col(416, 32).rearrange("p (c j) -> p c j", c=TT)
        fmx = col(448, 6).rearrange("p (b c) -> p b c", b=3)
        fnm = col(454, 6).rearrange("p (b c) -> p b c", b=3)
        fsum = col(460, 6).rearrange("p (b c) -> p b c", b=3)
        frs = col(466, 6).rearrange("p (b c) -> p b c", b=3)
        fqg = col(472, 1)

        def tile_ready(eng, n):
            eng.wait_ge(sem(f"slot{n % RAW}_loaded"), 16 * (n // RAW + 1))

        def out_ready(eng, n):
            eng.wait_ge(sem("outs"), n + 1)

        def out_taken(eng, n):
            eng.wait_ge(sem(f"bank{n % BANKS}_taken"), n // BANKS + 1)

        def taken(n):
            return f"bank{n % BANKS}_taken", n // BANKS + 1

        block = ctx.enter_context(nc.Block())

        @block.sync
        def _(sp_):
            sp_.dma_start(x[:, :, :], xT).then_inc(sem("x_loaded"), 16)
            sp_.dma_start(vec[:, :], vecs).then_inc(sem("vec_loaded"), 16)
            sp_.dma_start(con[:, :], consts[:, 0:CON_KEPT]).then_inc(sem("con_loaded"), 16)
            sp_.dma_start(wsmall[:, :, :], small_w).then_inc(sem("wsmall_loaded"), 16)
            sp_.dma_start(wfox[:, :, :], fox_f_w).then_inc(sem("wfox_loaded"), 16)
            sp_.dma_start(masks, consts[:, CON_KEPT:CONSTW]).then_inc(sem("masks_loaded"), 16)
            for name, count, width, parts__, cut in STREAM:
                base, src = TILE0[name], streams[name]

                def load(n, which):
                    w = which.shape[-1]
                    sp_.dma_start(ring[0:parts__, n % RAW, 0:w], which).then_inc(sem(f"slot{n % RAW}_loaded"), 16)

                def load_one(i):
                    if base + i >= RAW:
                        what, value = raw_free(base + i - RAW)
                        sp_.wait_ge(sem(what), value)
                    if name == "ffn_down":
                        m, a_ = i // 3, i % 3 * SLOT
                        load(base + i, src[m][:, a_:a_ + P * DOWN[i % 3]])
                    else:
                        load(base + i, src[i])

                if name != "mod" and not name.endswith("experts"):
                    for i in range(count):
                        load_one(i)
                    continue
                for i in range(RAW):
                    load_one(i)
                what, value = raw_free(base)
                with sp_.Fori(1, count // RAW) as r:
                    for j in range(RAW):
                        sp_.wait_ge(sem(what), r * RAW + (value + j - RAW))
                        load(base + j, src[bass.ds(r * RAW + j, 1), :, :].rearrange("a p w -> (a p) w"))
            sp_.wait_ge(sem("x_done"), 8)
            sp_.dma_start(out, x[:, :, :]).then_inc(sem("stored"), 16)
            sp_.wait_ge(sem("stored"), 16)

        @block.tensor
        def _(pe):
            S = Steps(pe, sem, "pe_step")
            mod_tiles = [0]

            def bank(n):
                if n >= BANKS:
                    out_taken(pe, n - BANKS)
                return mm[:, n % BANKS, :]

            def slot(n):
                tile_ready(pe, n)
                return ring[:, n % RAW, :]

            def parts_of(name, i, width=SLOT):
                q = CUT0[name] + i
                pe.wait_ge(sem("high_done"), q + 1)
                return q, high[:, q % CUT, 0:width], low[:, q % CUT, 0:width]

            def low_ready(q):
                pe.wait_ge(sem("low_done"), q + 1)

            def three_passes(dst, q, ws, acts, first=True, last=True, swap=False):
                rows = len(ws)
                for s_, (a_, b_) in enumerate(((0, 0), (0, 1), (1, 0))):
                    if s_ == 2:
                        low_ready(q)
                    for k in range(rows):
                        l, r_ = ws[k][a_], acts[k][b_]
                        if swap:
                            l, r_ = r_, l
                        ins = pe.matmul(dst, l, r_, start=first and s_ == 0 and k == 0,
                                        stop=last and s_ == 2 and k == rows - 1, skip_group_check=True)
                return ins

            def group(dst, pairs, first=True):
                for i, (a, b) in enumerate(pairs):
                    ins = pe.matmul(dst, a, b, start=first and i == 0, stop=i == len(pairs) - 1,
                                    skip_group_check=True)
                return ins

            def norm(i, shifted_):
                n = OUT0[f"norm{i}"]
                pe.wait_ge(sem("norm_squares"), i + 1)
                if i == 0:
                    pe.wait_ge(sem("con_loaded"), 16)
                S.did(group(bank(n)[:, 0:T], [(ones, scratch[:, k * T:(k + 1) * T]) for k in range(KD)]), "outs")
                return i

            def h_ready(i):
                pe.wait_ge(sem("h_high"), KD * (H_NORMS.index(i) + 1))
                pe.wait_ge(sem("h_low"), KD * (H_NORMS.index(i) + 1))

            def groups_of(act_):
                return [(act_[:, 0, k, :], act_[:, 1, k, :]) for k in range(act_.shape[2])]

            hgroups = groups_of(hs)

            def dense(stage, tiles, acts=None, m=P):
                acts = hgroups if acts is None else acts
                rows = len(acts)
                for t in range(tiles):
                    q, wh, wl = parts_of(stage, t)
                    ws = [(wh[:, k * m:(k + 1) * m], wl[:, k * m:(k + 1) * m]) for k in range(rows)]
                    S.did(three_passes(bank(OUT0[stage] + t)[0:m, 0:T], q, ws, acts), "outs")

            def dense_tokens(stage, pairs):
                for p_ in range(pairs):
                    for half in range(2):
                        q, wh, wl = parts_of(stage, 2 * p_ + half)
                        ws = [(wh[:, k * 256:(k + 1) * 256], wl[:, k * 256:(k + 1) * 256]) for k in range(4)]
                        for c in range(TT):
                            n_ = OUT0[stage] + 2 * p_ + c
                            acts = [(hs[:, 0, 4 * half + k, c * P:(c + 1) * P],
                                     hs[:, 1, 4 * half + k, c * P:(c + 1) * P]) for k in range(4)]
                            dst_ = (bank(n_) if half == 0 else mm[:, n_ % BANKS, :])[:, 0:T]
                            ins_ = three_passes(dst_, q, ws, acts, first=half == 0, last=half == 1, swap=True)
                            if half == 1:
                                S.did(ins_, "outs")
                        if half == 0:
                            ins_.then_inc(sem("tiles_used"), 1)

            def token_gates(dst_, weights):
                for c in range(TT):
                    ins_ = group(dst_[:, 16 * c:16 * (c + 1)],
                                 [(hs[:, s_, k, c * P:(c + 1) * P].bitcast(F32), weights[:, k, :])
                                  for k in range(KD) for s_ in range(2)])
                return ins_

            def mods(count):
                for _ in range(2 * count):
                    if mod_tiles[0] == 24 * MODS:
                        return
                    i = mod_tiles[0]
                    w = slot(TILE0["mod"] + i)
                    if i == 0:
                        pe.wait_ge(sem("csilu_ready"), 1)
                        for j in range(12, 16):
                            out_taken(pe, OUT0["gates"] + j)
                    group(mm[:, MOD_BANK, i:i + 1], [(w[:, k * P:(k + 1) * P], csilu[:, k:k + 1]) for k in range(KD)]) \
                        .then_inc(sem("tiles_used"), 1)
                    mod_tiles[0] += 1

            MOD_BANK = 3

            norm(0, False)
            h_ready(0)
            n = OUT0["small"]
            pe.wait_ge(sem("wsmall_loaded"), 16)
            S.did(token_gates(bank(n), wsmall), "outs")
            dense("qkv", 12)
            dense("gz", 4)
            dense("mqk", 4)
            dense_tokens("mv", 2)
            dense("mo", 4)
            dense("gates", 16)

            pe.wait_ge(sem("qk_squares"), 1)
            for j in range(4):
                ins = pe.matmul(ms[:, j, :], ones, scratch[:, j * 512:(j + 1) * 512], start=True, stop=True)
            S.did(ins, "qk_sums")
            mods(1)
            pe.wait_ge(sem("log_decays"), 1)
            for c in range(TT):
                ins = pe.matmul(mm[:, 0, 8 * c:8 * c + 8], upper, lgt[:, c, :], start=True, stop=True,
                                skip_group_check=True)
            pe.matmul(mm[:, 0, 12:16], ones, lgt[:, 0, 4:8], start=False, stop=True, skip_group_check=True)
            ins = pe.matmul(mm[:, 0, 16:20], ones, lgt[:, 0, 0:4], start=True, stop=True, skip_group_check=True)
            S.did(ins, "cum_ready")
            mods(1)
            pe.wait_ge(sem("diag_ready"), 1)
            pe.wait_ge(sem("qk_sums_taken"), 1)
            for j in range(2):
                ins = pe.matmul(ms[:, j, :], ones, diag[:, 4 * j:4 * j + 4, :].rearrange("p j t -> p (j t)"), start=True, stop=True)
            S.did(ins, "rows_ready")
            mods(2)
            pe.wait_ge(sem("qk_normal"), 1)
            pe.wait_ge(sem("cum_taken"), 1)
            for u in range(8):
                hd, c = u // 2, u % 2
                ins = pe.matmul(mm[:, u // 4, (u % 4) * P:(u % 4 + 1) * P], cv[:, 4 + hd, c * P:(c + 1) * P],
                                cv[:, 4 + hd, c * P:(c + 1) * P], start=True, stop=True, skip_group_check=True)
            S.did(ins, "kk_ready")
            for u in range(8):
                hd, c = u // 2, u % 2
                ins = pe.matmul(ms[:, 2 + u // 4, (u % 4) * P:(u % 4 + 1) * P], cv[:, 4 + hd, c * P:(c + 1) * P],
                                cv[:, hd, c * P:(c + 1) * P], start=True, stop=True, skip_group_check=True)
            S.did(ins, "kq_ready")
            mods(2)
            pe.wait_ge(sem("rows_taken"), 1)
            for u in range(8):
                hd, c = u // 2, u % 2
                ins = pe.transpose(ms[:, u // 4, (u % 4) * P:(u % 4 + 1) * P], cv[:, 8 + hd, c * P:(c + 1) * P], ident)
            S.did(ins, "v_turned")
            mods(2)
            pe.wait_ge(sem("M_ready"), 1)
            for u in range(8):
                ins = pe.transpose(mm[:, u // 4, (u % 4) * P:(u % 4 + 1) * P], M[:, u, :], ident)
            S.did(ins, "M_turned")
            pe.wait_ge(sem("attnT_ready"), 1)
            for u in range(8):
                hd, c = u % 4, u // 4
                ins = pe.transpose(ms[:, 2 + u // 4, (u % 4) * P:(u % 4 + 1) * P], cv[:, 4 + hd, c * P:(c + 1) * P], ident)
            S.did(ins, "k_turned")
            mods(2)
            pe.wait_ge(sem("tokens_ready"), 1)
            for l in range(1, LEVELS):
                for u in range(2):
                    pe.wait_ge(sem("X_ready"), 2 * (l - 1) + u + 1)
                    pe.wait_ge(sem("corner_ready"), l)
                    for i in range(4 * u, 4 * u + 4):
                        ins = pe.matmul(ms[:, u, (i % 4) * P:(i % 4 + 1) * P], Ml[l % 2][:, i, :], X[:, i, :],
                                        start=True, stop=True, skip_group_check=True)
                    S.did(ins, "MX_ready")
                mods(1)
                for u in range(2):
                    pe.wait_ge(sem("MX_taken"), 2 * (l - 1) + u + 1)
                    for i in range(4 * u, 4 * u + 4):
                        pe.matmul(ms[:, u, (i % 4) * P:(i % 4 + 1) * P], XT[:, i, :], Pm[:, i, :],
                                  start=True, stop=True, skip_group_check=True)
                        ins = pe.matmul(ms[:, 2 + u, (i % 4) * P:(i % 4 + 1) * P], Pm[:, i, :], XT[:, i, :],
                                        start=True, stop=True, skip_group_check=True)
                    S.did(ins, "XMX_ready")
                mods(1)
            pe.wait_ge(sem("X_ready"), 2 * LEVELS)
            for i in range(4):
                ins = pe.matmul(mm[:, 0, i * P:(i + 1) * P], XT[:, 2 * i, :], vb[:, 2 * i, :], start=True, stop=True,
                                skip_group_check=True)
            S.did(ins, "vn0_ready")
            for i in range(4):
                ins = pe.matmul(mm[:, 1, i * P:(i + 1) * P], kbg[:, i, :], XT[:, 2 * i + 1, :], start=True, stop=True,
                                skip_group_check=True)
            S.did(ins, "w_ready")
            mods(1)
            pe.wait_ge(sem("vn0_taken"), 1)
            for i in range(4):
                ins = pe.matmul(mm[:, 2, i * P:(i + 1) * P], kdec[:, i, :], vn[0][:, i, :], start=True, stop=True,
                                skip_group_check=True)
            S.did(ins, "state_ready")
            mods(1)
            pe.wait_ge(sem("state_taken"), 1)
            pe.wait_ge(sem("w_taken"), 1)
            for i in range(4):
                ins = group(mm[:, 0, i * P:(i + 1) * P], [(XT[:, 2 * i + 1, :], vb[:, 2 * i + 1, :]),
                                                          (nwT[:, i, :], S1[:, i, :])])
            S.did(ins, "vn1_ready")
            mods(1)
            pe.wait_ge(sem("vn1_taken"), 1)
            for i in range(4):
                dst = ms[:, i // 2, (i % 2) * T:(i % 2) * T + P]
                pe.matmul(dst, vn[0][:, i, :], attnT[:, 2 * i, :], start=True, stop=True, skip_group_check=True)
                dst = ms[:, i // 2, (i % 2) * T + P:(i % 2) * T + 2 * P]
                ins = group(dst, [(vn[1][:, i, :], attnT[:, 2 * i + 1, :]), (S1[:, i, :], grow[:, i, :])])
            S.did(ins, "oa_ready")

            def head_sums(which):
                pe.wait_ge(sem("head_squares"), which + 1)
                for j in range(2):
                    ins = pe.matmul(ms[:, 2 + j, :], ones, scratch[:, j * 512:(j + 1) * 512], start=True, stop=True)
                S.did(ins, "head_sums")

            mods(2)
            head_sums(0)
            mods(1)

            pe.wait_ge(sem("diag2_ready"), 1)
            for j in range(2):
                ins = pe.matmul(mm[:, 1 + j, :], ones, diag2[:, 4 * j:4 * j + 4, :].rearrange("p j t -> p (j t)"), start=True, stop=True)
            S.did(ins, "ml_rows_ready")
            mods(2)
            pe.wait_ge(sem("oa_done"), 1)
            for i in range(4):
                a, o = i // 2, 64 * (i % 2)
                pe.matmul(ms[:, i, 0:P], mq[o:o + 64, a, 0:P], mk[o:o + 64, a, 0:P], start=True, stop=True,
                          skip_group_check=True)
                ins = pe.matmul(ms[:, i, P:3 * P], mq[o:o + 64, a, P:2 * P], mk[o:o + 64, a, :], start=True, stop=True,
                                skip_group_check=True)
            S.did(ins, "ml_qk_ready")
            mods(3)
            pe.wait_ge(sem("ml_scores"), 1)
            for i in range(4):
                if i == 0:
                    pe.wait_ge(sem("ml_rows_taken"), 1)
                if i == 3:
                    pe.wait_ge(sem("ml_turned"), 1)
                for b in range(3):
                    ins = pe.transpose(mm[:, i % 3, b * P:(b + 1) * P], Em[:, i, b * P:(b + 1) * P], ident)
                S.did(ins, "ml_turn")
            mods(2)
            pe.wait_ge(sem("ml_turned"), 4)
            for i in range(4):
                dst = ms[:, i // 2, (i % 2) * T:(i % 2 + 1) * T]
                pe.matmul(dst, mv[:, 0, i * P:(i + 1) * P], ST[:, i, 0:2 * P], start=i % 2 == 0, stop=False,
                          skip_group_check=True)
                ins = pe.matmul(dst[:, P:2 * P], mv[:, 1, i * P:(i + 1) * P], ST[:, i, 2 * P:3 * P], start=False,
                                stop=True, skip_group_check=True)
            S.did(ins, "ob_ready")
            mods(2)
            head_sums(1)
            mods(100)

            def branch(stage, acts):
                for t in range(4):
                    q, wh, wl = parts_of(stage, t)
                    for b in range(2):
                        ws = [(wh[:, k * 256 + b * P:k * 256 + (b + 1) * P], wl[:, k * 256 + b * P:k * 256 + (b + 1) * P])
                              for k in range(4)]
                        S.did(three_passes(bank(OUT0[stage] + 2 * t + b)[:, 0:T], q, ws, acts), "outs")

            pe.wait_ge(sem("mods_taken"), 1)
            pe.wait_ge(sem("oa_done"), 2)
            branch("branch_a", groups_of(oas))
            pe.wait_ge(sem("ob_done"), 1)
            branch("branch_b", groups_of(obs))
            pe.wait_ge(sem("mixed"), KD)
            dense("w_out", 8, groups_of(mixs))
            norm(1, False)

            h_ready(1)
            dense("ffn_up", 2 * FFG)
            pe.wait_ge(sem("ffact_cut"), FFG)
            acts = groups_of(ffs_)
            for m in range(KD):
                dst = bank(OUT0["ffn_down"] + m)[:, 0:T]
                k0 = 0
                for i, rows in enumerate(DOWN):
                    q, wh, wl = parts_of("ffn_down", 3 * m + i)
                    ws = [(wh[:, k * P:(k + 1) * P], wl[:, k * P:(k + 1) * P]) for k in range(rows)]
                    ins = three_passes(dst, q, ws, acts[k0:k0 + rows], first=i == 0, last=i == len(DOWN) - 1)
                    S.did(ins, "outs") if i == len(DOWN) - 1 else ins.then_inc(sem("tiles_used"), 1)
                    k0 += rows
            norm(2, False)

            h_ready(2)
            dense("ple_gate", 8)
            pe.wait_ge(sem("p_loaded"), 16)
            for t in range(2):
                w = slot(TILE0["ple"] + t)
                for b in range(4):
                    S.did(group(bank(OUT0["ple"] + 4 * t + b)[:, 0:T],
                                [(w[:, k * 512 + b * P:k * 512 + (b + 1) * P], pTs[:, k, :]) for k in range(2)]), "outs")
            norm(3, False)
            norm(4, True)

            h_ready(4)
            pe.wait_ge(sem("lru_gates_loaded"), 16)

            def lru_gates(j):
                pe.wait_ge(sem("lru_conv"), j + 1)
                for g, kind in enumerate(("ra", "ri")):
                    S.did(pe.matmul(bank(lru_out_of(kind, j))[0:BLK, 0:T], lgw[0:BLK, j, g, :], lc[0:BLK, j, :],
                                    start=True, stop=True), "outs")

            for j in range(NBLK):
                for b, kind in enumerate(("x", "g")):
                    q, wh, wl = parts_of("lru_in", 2 * j + b)
                    ws = [(wh[:, k * BLK:(k + 1) * BLK], wl[:, k * BLK:(k + 1) * BLK]) for k in range(KD)]
                    S.did(three_passes(bank(lru_out_of(kind, j))[0:BLK, 0:T], q, ws, hgroups), "outs")
                if j:
                    lru_gates(j - 1)
            lru_gates(NBLK - 1)
            pe.wait_ge(sem("lru_y"), NBLK)
            for m in range(KD):
                dst = bank(OUT0["lru_out"] + m)[:, 0:T]
                for half in range(2):
                    q, wh, wl = parts_of("lru_out", 2 * m + half)
                    ws = [(wh[0:BLK, k * P:(k + 1) * P], wl[0:BLK, k * P:(k + 1) * P]) for k in range(8)]
                    acts = [(ys[0:BLK, 0, 8 * half + k, :], ys[0:BLK, 1, 8 * half + k, :]) for k in range(8)]
                    ins = three_passes(dst, q, ws, acts, first=half == 0, last=half == 1)
                    S.did(ins, "outs") if half == 1 else ins.then_inc(sem("tiles_used"), 1)

            def experts(L):
                norm(5 + 2 * L, True)
                h_ready(5 + 2 * L)
                dense(f"peer{L}_q", 16)
                w = [slot(TILE0[f"peer{L}_keys"] + i) for i in range(2)]
                out_taken(pe, OUT0[f"peer{L}_q"] + 15)
                for c in range(TT):
                    for g in range(4):
                        n = OUT0[f"peer{L}_scores"] + 4 * c + g
                        dst = bank(n)
                        for j in range(4 * g, 4 * g + 4):
                            ins = pe.matmul(dst[:, (j % 4) * P:(j % 4 + 1) * P], eq[:, j, c * P:(c + 1) * P],
                                            w[j // 8][:, (j % 8) * P:(j % 8 + 1) * P], start=True, stop=True,
                                            skip_group_check=True)
                        S.did(ins, "outs")
                for c in range(TT):
                    dst = bank(OUT0[f"peer{L}_turn"] + c)
                    pe.wait_ge(sem("routed"), TT * L + c + 1)
                    for s in range(3):
                        ins = pe.transpose(dst[:, s * P:(s + 1) * P], route[:, c, s, :], ident)
                    S.did(ins, "outs")
                n0 = OUT0[f"peer{L}_place"]

                def place(n, wait_taken, wait_hot, b):
                    pe.wait_ge(sem(taken(n)[0]), wait_taken)
                    pe.wait_ge(sem("onehots"), wait_hot)
                    for i in range(4):
                        ins = pe.matmul(mm[:, n % BANKS, i * P:(i + 1) * P], onehot[:, b, 0, i, :],
                                        onehot[:, b, 1, i, :], start=True, stop=True, skip_group_check=True)
                    ins.then_inc(sem("outs"), 1)

                with pe.Fori(0, T // 16) as r:
                    for j in range(4):
                        place(n0 + j, r + (n0 + j) // BANKS, r * 4 + (T // 4 * L + j + 1), j % 2)
                for j in range(4):
                    out_taken(pe, n0 + T // 4 - 4 + j)

                q0 = CUT0[f"peer{L}_experts"]

                def products(dsts, i, r, ws_of, acts_of, first):
                    q = (q0 + i) % CUT
                    pe.wait_ge(sem("high_done"), r * (2 * UNROLL) + (q0 + i + 1))
                    for s_, (a_, b_) in enumerate(((0, 0), (0, 1), (1, 0))):
                        if s_ == 2:
                            pe.wait_ge(sem("low_done"), r * (2 * UNROLL) + (q0 + i + 1))
                        w = (high, low)[a_][:, q, :]
                        for k in range(KD):
                            ins_ = pe.matmul(dsts[k], w[:, k * P:(k + 1) * P], acts_of(b_, k),
                                             start=first(k) and s_ == 0, stop=False, skip_group_check=True)
                    return ins_

                def hidden(j, i, r, wait_free):
                    if wait_free is not None:
                        pe.wait_ge(sem("hidden_taken"), wait_free)
                    products([mm[:, j % 3, 0:T]] * KD, i, r, None, lambda b_, k: hs[:, b_, k, :],
                             lambda k: k == 0).then_inc(sem("hidden_ready"), 1)

                def values(j, i, r, first):
                    pe.wait_ge(sem("weighted"), r * UNROLL + (KEYS * L + j + 1))
                    products([ms[:, m // 2, (m % 2) * T:(m % 2 + 1) * T] for m in range(KD)], i, r, None,
                             lambda b_, k: wts[:, j % 3, b_, :],
                             lambda k: first and k % 2 == 0).then_inc(sem("tiles_used"), 1)

                def step(j, r, first=False):
                    i = j if first and j < LAG else 2 * j - LAG
                    hidden(j, i, r, None if first and j < 3 else r * UNROLL + (KEYS * L + j - 3 + 1))
                    if not (first and j < LAG):
                        values(j - LAG, i + 1, r, first and j == LAG)

                for j in range(UNROLL):
                    step(j, 0, True)
                with pe.Fori(1, KEYS // UNROLL) as r:
                    for j in range(UNROLL):
                        step(j, r)
                last = KEYS // UNROLL
                for j in range(KEYS - last * UNROLL):
                    step(j, last)
                for s_ in range(KEYS - LAG, KEYS):
                    values(s_, KEYS + s_, 0, False)

            experts(0)

            norm(6, True)
            h_ready(6)
            n = OUT0["fox_small"]
            pe.wait_ge(sem("wfox_loaded"), 16)
            S.did(token_gates(bank(n), wfox), "outs")
            n += 1
            pe.wait_ge(sem("fox_logf"), 1)
            dst = bank(n)
            group(dst[:, 0:16], [(upper, ffs[:, 0, :])])
            ins = group(dst[:, 16:32], [(upper, ffs[:, 1, :]), (ones, ffs[:, 0, :])])
            S.did(ins, "outs")
            dense("fox_qk", 16)
            dense_tokens("fox_v", 4)
            dense("fox_og", 8)
            for j in range(8):
                n = OUT0["fox_squares"] + j
                pe.wait_ge(sem("fox_sq"), j // 4 + 1)
                S.did(pe.matmul(bank(n), heads64, fsq[:, j * 512:(j + 1) * 512], start=True, stop=True), "outs")
            pe.wait_ge(sem("fox_diag"), 1)
            pe.wait_ge(sem("fox_normal"), 2)
            for kind, hd in fox_order():
                a, o = hd // 2, 64 * (hd % 2)
                if kind == "scores":
                    dst = bank(OUT0[f"fox_scores{hd}"])
                    group(dst[:, 0:P], [(fq3[o:o + 64, a, 0:P], fk3[o:o + 64, a, 0:P]), (ones, fd[:, hd, 0, :])])
                    ins = group(dst[:, P:3 * P], [(fq3[o:o + 64, a, P:2 * P], fk3[o:o + 64, a, :]),
                                                  (ones, fd[:, hd, :, :].rearrange("p c t -> p (c t)"))])
                    S.did(ins, "outs")
                elif kind == "turn":
                    dst = bank(OUT0[f"fox_turn{hd}"])
                    pe.wait_ge(sem("fox_probs"), hd + 1)
                    for b in range(3):
                        ins = pe.transpose(dst[:, b * P:(b + 1) * P], fP[:, hd % 3, b * P:(b + 1) * P], ident)
                    S.did(ins, "outs")
                else:
                    out_taken(pe, OUT0[f"fox_turn{hd}"])
                    if a >= 4:
                        pe.wait_ge(sem("fox_y"), a - 3)
                    dst = ms[o:o + 64, a % 4, 0:T]
                    pe.matmul(dst, fv[:, 0, hd * FE:(hd + 1) * FE], fPT[:, hd % 3, 0:2 * P], start=True, stop=False,
                              skip_group_check=True)
                    S.did(pe.matmul(dst[:, P:2 * P], fv[:, 1, hd * FE:(hd + 1) * FE], fPT[:, hd % 3, 2 * P:3 * P],
                                    start=False, stop=True, skip_group_check=True), "fox_pv")
            pe.wait_ge(sem("fox_y"), KD)
            dense("fox_out", 8, groups_of(fys))
            experts(1)

        @block.scalar
        def _(act):
            S = Steps(act, sem, "act_step")
            def squares(i):
                if i == 0:
                    act.wait_ge(sem("x_loaded"), 16)
                else:
                    act.wait_ge(sem("x_done"), i)
                if i >= 1:
                    out_ready(act, OUT0[f"norm{i - 1}"])
                S.did(act.activation(scratch[:, :], x[:, :, :].rearrange("p k t -> p (k t)"), ACT.Square),
                      "norm_squares")

            def root(i):
                act.wait_ge(sem("norm_inverse"), i + 1)
                S.did(act.activation(rstd[:, :], rstd[:, :], ACT.Sqrt), "norm_rstd")

            def high_parts(i):
                for k in range(KD):
                    act.wait_ge(sem("h_scaled"), KD * H_NORMS.index(i) + k + 1)
                    if i <= 2:
                        ins = act.activation(hs[:, 0, k, :], hf[:, k, :], ACT.Copy)
                    else:
                        m = (i - 4) * 24 + k
                        ins = act.activation(hs[:, 0, k, :], hf[:, k, :], ACT.Identity, bias=mod[:, m:m + 1])
                    S.did(ins, "h_high")

            cuts_made = [0]

            def ahead(stage, t, more=CUT - 1):
                end = min(CUT0[stage] + t + more, RUN_END[stage])
                while cuts_made[0] <= end:
                    q = cuts_made[0]
                    name, i = CUTS[q]
                    n_ = TILE0[name] + i
                    tile_ready(act, n_)
                    if q >= CUT:
                        what, value = cut_free(q - CUT)
                        act.wait_ge(sem(what), value)
                    rows, width = tile_shape(name, i)
                    act.activation(high[0:rows, q % CUT, 0:width], ring[0:rows, n_ % RAW, 0:width], ACT.Copy) \
                        .then_inc(sem("high_done"), 1)
                    cuts_made[0] += 1

            def evacuate(n, dst, func=ACT.Copy, m=P, width=T):
                out_ready(act, n)
                src = mm[0:m, n % BANKS, 0:width]
                if len(dst.shape) == 3:
                    src = src.rearrange("p (j n) -> p j n", n=P)
                S.did(act.activation(dst, src, func), taken(n))

            squares(0)
            ahead("qkv", 0)
            root(0)
            high_parts(0)
            act.wait_ge(sem("vec_loaded"), 16)
            S.did(act.activation(expa, v("a_log"), ACT.Exp), "expa_ready")
            act.wait_ge(sem("pre_ready"), 1)
            S.did(act.activation(beta, pre[:, :, 0:4], ACT.Sigmoid), "beta_ready")
            S.did(act.activation(csilu[:, :], v("c"), ACT.Silu), "csilu_ready")
            act.wait_ge(sem("nz_ready"), 1)
            S.did(act.activation(en, nz, ACT.Exp))
            S.settle()
            S.did(act.activation(ln, en, ACT.Ln, bias=1.0), "ln_ready")
            act.wait_ge(sem("pad_zero"), 1)
            for j in range(13):
                if j < 12:
                    ahead("qkv", j)
                    evacuate(OUT0["qkv"] + j, cin[:, j, 3:T + 3])
                if j:
                    act.wait_ge(sem("conv_done"), j)
                    S.did(act.activation(cv[:, j - 1, :], cv[:, j - 1, :], ACT.Silu), "qkv_active")
            for j in range(4):
                ahead("gz", j)
                evacuate(OUT0["gz"] + j, gz[:, j, :], ACT.Silu)
            for j in range(4):
                ahead("mqk", j)
                evacuate(OUT0["mqk"] + j, (mq if j < 2 else mk)[:, j % 2, :])
            for j in range(4):
                ahead("mv", j // 2 * 2 + 1)
                evacuate(OUT0["mv"] + j, mv[:, j % 2, (j // 2) * T:(j // 2 + 1) * T])
            for j in range(4):
                ahead("mo", j)
                evacuate(OUT0["mo"] + j, mo[:, j, :], ACT.Sigmoid)
            for j in range(16):
                ahead("gates", j)
                evacuate(OUT0["gates"] + j, gates[:, j, :], ACT.Sigmoid)
            act.wait_ge(sem("qk_inverse"), 1)
            S.did(act.activation(scratch[:, :], scratch[:, :], ACT.Sqrt), "qk_rstd")
            act.wait_ge(sem("gdif_ready"), 1)
            act.activation(ecum, cum[:, 1, 0:4], ACT.Exp)
            S.did(act.activation(ekd, gdif, ACT.Exp), "column_decays")
            act.wait_ge(sem("decay_logs"), 1)
            S.did(act.activation(decay, decay, ACT.Exp), "decay_ready")
            S.did(act.activation(decayT, decayT, ACT.Exp, scale=-1.0), "decay_ready")
            act.wait_ge(sem("rows_ready"), 1)
            for i in range(4):
                u = 2 * i + 1
                ins = act.activation(grow[:, i, :], ms[:, u // 4, (u % 4) * P:(u % 4 + 1) * P], ACT.Exp, scale=-1.0)
            S.did(ins, "grow_ready")
            act.wait_ge(sem("oa_ready"), 1)
            halves = ms[:, 0:2, :].rearrange("p b n -> p (b n)")
            act.activation(oa.rearrange("p j t -> p (j t)"), halves, ACT.Copy)
            S.did(act.activation(scratch[:, 0:1024], halves, ACT.Square), "head_squares")
            act.wait_ge(sem("head_inverse"), 1)
            S.did(act.activation(scratch[:, 1024:2048], scratch[:, 1024:2048], ACT.Sqrt), "head_rstd")
            act.wait_ge(sem("ml_nm"), 1)
            act.activation(flo, nm, ACT.Exp)
            for i in range(4):
                act.activation(Em[:, i, 0:P], Dlog[:, i, 0:P], ACT.Exp, bias=nm[:, 0, i:i + 1])
                ins = act.activation(Em[:, i, P:3 * P], Dlog[:, i, P:3 * P], ACT.Exp, bias=nm[:, 1, i:i + 1])
            S.did(ins, "ml_weights")
            for i in range(4):
                act.wait_ge(sem("ml_turn"), i + 1)
                S.did(act.activation(ST[:, i, :], mm[:, i % 3, 0:384], ACT.Copy), "ml_turned")
            act.wait_ge(sem("ob_ready"), 1)
            act.activation(ob.rearrange("p j t -> p (j t)"), halves, ACT.Copy)
            S.did(act.activation(scratch[:, 0:1024], halves, ACT.Square), "head_squares")
            act.wait_ge(sem("head_inverse"), 2)
            S.did(act.activation(scratch[:, 1024:2048], scratch[:, 1024:2048], ACT.Sqrt), "head_rstd")
            ahead("ffn_up", 0)
            act.wait_ge(sem("x_done"), 1)
            act.dma_start(pTs, pT).then_inc(sem("p_loaded"), 16)
            squares(1)
            root(1)
            high_parts(1)
            for j in range(FFG):
                ahead("ffn_up", 2 * j)
                if j >= 2:
                    out_taken(act, OUT0["ffn_up"] + 2 * (j - 2) + 1)
                evacuate(OUT0["ffn_up"] + 2 * j, up[:, j % 2, :], ACT.Silu)
            ahead("ple_gate", 0)
            squares(2)
            root(2)
            high_parts(2)
            for j in range(KD):
                ahead("ple_gate", j)
                evacuate(OUT0["ple_gate"] + j, pleg[:, j, :], ACT.Sigmoid)
            squares(3)
            root(3)
            ahead("lru_in", 0)
            act.wait_ge(sem("x_done"), 3)
            act.dma_start(lgw[0:96], lru_gate_w).then_inc(sem("lru_gates_loaded"), 16)
            act.wait_ge(sem("nlam_ready"), 1)
            S.did(act.activation(lruc[:, 1, :], lruc[:, 0, :], ACT.Exp), "lam_exp")
            squares(4)
            root(4)
            high_parts(4)
            act.wait_ge(sem("lru_pad_zero"), 1)

            def lru_act(j):
                n = lru_out_of("ra", j)
                out_ready(act, n)
                S.did(act.activation(lr[0:BLK, j, :], mm[0:BLK, n % BANKS, 0:T], ACT.Sigmoid,
                                     bias=v("ra_b", j, j + 1, BLK)), taken(n))
                n = lru_out_of("ri", j)
                out_ready(act, n)
                S.did(act.activation(li[0:BLK, j, :], mm[0:BLK, n % BANKS, 0:T], ACT.Sigmoid,
                                     bias=v("ri_b", j, j + 1, BLK)), taken(n))
                out_taken(act, lru_out_of("ra", j))
                S.did(act.activation(lt[0:BLK, j, :], lr[0:BLK, j, :], ACT.Tanh,
                                     scale=lruc[0:BLK, 5, j:j + 1]), "lru_tanh")

            act.wait_ge(sem("lru_rate"), 1)
            for j in range(NBLK):
                ahead("lru_in", 2 * j)
                evacuate(lru_out_of("x", j), lx[0:BLK, j, 3:T + 3], m=BLK)
                ahead("lru_in", 2 * j + 1)
                evacuate(lru_out_of("g", j), lg[0:BLK, j, :], m=BLK)
                if j:
                    lru_act(j - 1)
            lru_act(NBLK - 1)
            act.wait_ge(sem("lru_rec"), 1)
            S.did(act.activation(lt[0:BLK], lt[0:BLK], ACT.Sqrt), "lru_root")
            out_taken(act, lru_out_of("g", NBLK - 1))
            S.did(act.activation(lg[0:BLK], lg[0:BLK], ACT.Gelu), "lru_gelu")

            def experts(L):
                ahead(f"peer{L}_q", 0)
                squares(5 + 2 * L)
                root(5 + 2 * L)
                high_parts(5 + 2 * L)
                for j in range(16):
                    ahead(f"peer{L}_q", j)
                    evacuate(OUT0[f"peer{L}_q"] + j, eq[:, j, :])
                for c in range(TT):
                    for g in range(4):
                        evacuate(OUT0[f"peer{L}_scores"] + 4 * c + g, es[:, c, 4 * g:4 * g + 4, :], width=512)
                ahead(f"peer{L}_experts", 0)
                for c in range(TT):
                    act.wait_ge(sem("best_shifted"), TT * L + c + 1)
                    S.did(act.activation(expo, shifted, ACT.Exp), "best_exp")
                for c in range(TT):
                    n = OUT0[f"peer{L}_turn"] + c
                    evacuate(n, routeT[:, :, c * P:(c + 1) * P], width=384)
                n0 = OUT0[f"peer{L}_place"]
                with act.Fori(0, T // 16) as r:
                    for j in range(4):
                        act.wait_ge(sem("outs"), r * 4 + (n0 + j + 1))
                        dst = placed[:, :, bass.ds(r * 16 + 4 * j, 4)].rearrange("p e t -> p t e")
                        act.activation(dst, mm[:, (n0 + j) % BANKS, :].rearrange("p (t e) -> p t e", t=4), ACT.Copy) \
                            .then_inc(sem(taken(n0 + j)[0]), 1)

                q0, t0 = CUT0[f"peer{L}_experts"], TILE0[f"peer{L}_experts"]

                def cut_high(i, r):
                    act.wait_ge(sem(f"slot{(t0 + i) % RAW}_loaded"),
                                r * (16 * 2 * UNROLL // RAW) + 16 * ((t0 + i) // RAW + 1))
                    ahead_ = 0 if isinstance(r, int) else UNROLL
                    what, value = cut_free(q0 + i + 2 * ahead_ - CUT)
                    act.wait_ge(sem(what), r * UNROLL + (value - ahead_))
                    act.activation(high[:, (q0 + i) % CUT, :], ring[:, (t0 + i) % RAW, :], ACT.Copy) \
                        .then_inc(sem("high_done"), 1)

                def gelu(j, r, first=False):
                    act.wait_ge(sem("hidden_ready"), r * UNROLL + (KEYS * L + j + 1))
                    if not (first and j < 3):
                        act.wait_ge(sem("weighted"), r * UNROLL + (KEYS * L + j - 3 + 1))
                    act.activation(mix[:, j % 3, :], mm[:, j % 3, 0:T], ACT.Gelu).then_inc(sem("hidden_taken"), 1)

                for j in range(UNROLL):
                    gelu(j, 0, True)
                    for i in ((3,) if j == 0 else (4,) if j == 1 else (2 * j + 1, 2 * j + 2)):
                        cut_high(i, 0)
                with act.Fori(1, KEYS // UNROLL) as r:
                    for j in range(UNROLL):
                        gelu(j, r)
                        cut_high(2 * j + 1, r)
                        cut_high(2 * j + 2, r)
                last = KEYS // UNROLL
                for j in range(KEYS - last * UNROLL):
                    gelu(j, last)
                    for i in (2 * j + 1, 2 * j + 2):
                        if 2 * UNROLL * last + i < 2 * KEYS:
                            cut_high(2 * UNROLL * last + i, 0)
                cuts_made[0] = q0 + 2 * KEYS

            experts(0)

            ahead("fox_qk", 0)
            squares(6)
            root(6)
            high_parts(6)
            act.wait_ge(sem("fox_nz"), 1)
            S.did(act.activation(ffe, ffn_, ACT.Exp))
            S.settle()
            S.did(act.activation(ffl, ffe, ACT.Ln, bias=1.0), "fox_ln")
            for j in range(16):
                ahead("fox_qk", j)
                evacuate(OUT0["fox_qk"] + j, (fq3 if j < 8 else fk3)[:, j % 8, :])
            for j in range(8):
                ahead("fox_v", j // 2 * 2 + 1)
                evacuate(OUT0["fox_v"] + j, fv[:, j % 2, (j // 2) * T:(j // 2 + 1) * T])
            for j in range(8):
                ahead("fox_og", j)
                evacuate(OUT0["fox_og"] + j, fo[:, j, :], ACT.Sigmoid)
            for j in range(2):
                act.wait_ge(sem("fox_inverse"), j + 1)
                S.did(act.activation(fsq[:, j * 2048:(j + 1) * 2048], fsq[:, j * 2048:(j + 1) * 2048], ACT.Sqrt),
                      "fox_rstd")
            for i in range(FH + 2):
                if i < FH:
                    act.wait_ge(sem("fox_max"), i + 1)
                    if i >= 3:
                        out_ready(act, OUT0[f"fox_turn{i - 3}"])
                    b = i % 3
                    act.activation(fP[:, b, 0:P], fL[:, b, 0:P], ACT.Exp, bias=fnm[:, b, 0:1],
                                   accum_out=fsum[:, b, 0:1])
                    S.did(act.activation(fP[:, b, P:3 * P], fL[:, b, P:3 * P], ACT.Exp, bias=fnm[:, b, 1:2],
                                         accum_out=fsum[:, b, 1:2]), "fox_exp")
                if i >= 2:
                    hd = i - 2
                    if hd >= 3:
                        act.wait_ge(sem("fox_pv"), hd - 2)
                    evacuate(OUT0[f"fox_turn{hd}"], fPT[:, hd % 3, :], width=384)
            experts(1)

        @block.gpsimd
        def _(pool):
            def cut_low(rows, width, raw_slot, cut_slot):
                pool.tensor_tensor(low[0:rows, cut_slot, 0:width], ring[0:rows, raw_slot, 0:width],
                                   high[0:rows, cut_slot, 0:width].bitcast(F32), ALU.subtract) \
                    .then_inc(sem("low_done"), 1)

            def cut_one(name, i):
                q, n = CUT0[name] + i, TILE0[name] + i
                pool.wait_ge(sem("high_done"), q + 1)
                cut_low(*tile_shape(name, i), n % RAW, q % CUT)

            for name, count, _, _, is_cut in STREAM:
                if not is_cut:
                    continue
                if not name.endswith("experts"):
                    for i in range(count):
                        cut_one(name, i)
                    continue
                q0, t0, body = CUT0[name], TILE0[name], 2 * UNROLL
                for i in range(body):
                    cut_one(name, i)
                with pool.Fori(1, count // body) as r:
                    for i in range(body):
                        pool.wait_ge(sem("high_done"), r * body + (q0 + i + 1))
                        cut_low(P, SLOT, (t0 + i) % RAW, (q0 + i) % CUT)
                for i in range(count // body * body, count):
                    cut_one(name, i)

        @block.vector
        def _(dve):
            S = Steps(dve, sem, "dve_step")

            def tt(out_, a, b, op, name=None):
                S.did(dve.tensor_tensor(out_, a, b, op), name)

            def ts(out_, a, s1, s2, op0, op1=None, name=None):
                S.did(dve.tensor_scalar(out_, a, s1, s2, op0, *([op1] if op1 is not None else [])), name)

            def stt(out_, a, s, b, op0, op1, name=None, **kw):
                S.did(dve.scalar_tensor_tensor(out=out_, in0=a, scalar=s, in1=b, op0=op0, op1=op1, **kw), name)

            def bank(n, m=P, width=T):
                out_ready(dve, n)
                return mm[0:m, n % BANKS, 0:width]

            def norm(i, gain):
                n = OUT0[f"norm{i}"]
                src = bank(n)
                if i >= 1:
                    S.settle()
                ts(rstd[:, :], src, 1.0 / D, EPS, ALU.mult, ALU.add, taken(n))
                S.settle()
                S.did(dve.reciprocal(rstd[:, :], rstd[:, :]), "norm_inverse")
                dve.wait_ge(sem("norm_rstd"), i + 1)
                if i == 0:
                    dve.wait_ge(sem("vec_loaded"), 16)
                for k in range(KD):
                    dst, name = (x, "x_done" if k == KD - 1 else None) if i == 3 else (hf, "h_scaled")
                    stt(dst[:, k, :], x[:, k, :], gain[:, k:k + 1], rstd[:, :], ALU.mult, ALU.mult, name)
                if i == 3:
                    return
                for k in range(KD):
                    dve.wait_ge(sem("h_high"), KD * H_NORMS.index(i) + k + 1)
                    if k == 0:
                        S.settle()
                    hi_ = hs[:, 0, k, :].bitcast(F32)
                    if i <= 2:
                        tt(hs[:, 1, k, :], hf[:, k, :], hi_, ALU.subtract, "h_low")
                    else:
                        m = (i - 4) * 24 + k
                        stt(hs[:, 1, k, :], hf[:, k, :], mod[:, m:m + 1], hi_, ALU.add, ALU.subtract, "h_low")

            def cut_parts(high_, low_, src, name=None):
                S.settle()
                S.did(dve.tensor_copy(high_, src))
                S.settle()
                tt(low_, src, high_.bitcast(F32), ALU.subtract, name)

            S.did(dve.memset(cin[:, :, 0:3], 0.0), "pad_zero")
            norm(0, v("g_mix"))

            n = OUT0["small"]
            src = bank(n, width=32).rearrange("p (c j) -> p c j", c=TT)
            tt(pre, src, v("gate_bias").unsqueeze(1).to_broadcast([P, TT, 16]), ALU.add, taken(n))
            S.settle()
            S.did(dve.tensor_copy(zz[:, :, 0:4], pre[:, :, 4:8]), "pre_ready")
            ts(zz[:, :, 4:8], pre[:, :, 12:16], -1.0, None, ALU.mult)
            S.settle()
            ts(nz, zz, -1.0, None, ALU.mult)
            S.settle()
            tt(nz, nz, zz, ALU.min, "nz_ready")
            ts(sp, zz, 0.0, None, ALU.max)
            dve.wait_ge(sem("ln_ready"), 1)
            S.settle()
            tt(sp, sp, ln, ALU.add)
            S.settle()
            ts(lgt, sp, -1.0, None, ALU.mult)
            S.settle()
            dve.wait_ge(sem("expa_ready"), 1)
            tt(lgt[:, :, 0:4], lgt[:, :, 0:4], expa.unsqueeze(1).to_broadcast([P, TT, 4]), ALU.mult, "log_decays")

            for j in range(12):
                out_taken(dve, OUT0["qkv"] + j)
                w = v("conv", 4 * j, 4 * j + 4)
                ts(cv[:, j, :], cin[:, j, 0:T], w[:, 0:1], None, ALU.mult)
                for s in range(1, 4):
                    S.settle()
                    stt(cv[:, j, :], cin[:, j, s:s + T], w[:, s:s + 1], cv[:, j, :], ALU.mult, ALU.add,
                        "conv_done" if s == 3 else None)

            dve.wait_ge(sem("qkv_active"), 8)
            out_ready(dve, OUT0["norm0"])
            qk = cv[:, 0:8, :].rearrange("p j t -> p (j t)")
            tt(scratch[:, :], qk, qk, ALU.mult, "qk_squares")
            dve.wait_ge(sem("qk_sums"), 1)
            S.settle()
            ts(scratch[:, :], ms[:, :, :].rearrange("p b n -> p (b n)"), EPS, None, ALU.add, None, "qk_sums_taken")
            S.settle()
            S.did(dve.reciprocal(scratch[:, :], scratch[:, :]), "qk_inverse")
            dve.wait_ge(sem("cum_ready"), 1)
            S.did(dve.tensor_copy(cum, mm[:, 0, 0:16].rearrange("p (c j) -> p c j", c=TT)))
            S.did(dve.tensor_copy(gl, mm[:, 0, 16:20]), "cum_taken")
            S.settle()
            tt(gdif, gl, cum[:, 0, 0:4], ALU.subtract, "gdif_ready")
            ts(ngc, cum[:, :, 0:4], -1.0, None, ALU.mult)
            tt(imb, pre[:, :, 8:12], cum[:, :, 4:8], ALU.subtract)
            S.settle()
            for u in range(8):
                ts(diag[:, u, :], ident, ngc[:, u % 2, u // 2:u // 2 + 1], None, ALU.mult, None,
                   "diag_ready" if u == 7 else None)
            dve.wait_ge(sem("qk_rstd"), 1)
            stt(qk[:, 0:1024], qk[:, 0:1024], float(P) ** -0.5, scratch[:, 0:1024], ALU.mult, ALU.mult)
            tt(qk[:, 1024:2048], qk[:, 1024:2048], scratch[:, 1024:2048], ALU.mult, "qk_normal")
            dve.wait_ge(sem("rows_ready"), 1)
            dve.wait_ge(sem("masks_loaded"), 16)
            for u in range(8):
                r = ms[:, u // 4, (u % 4) * P:(u % 4 + 1) * P]
                g = cum[:, u % 2, u // 2:u // 2 + 1]
                stt(decay[:, u, :], r, g, cst("mask")[:, P:2 * P], ALU.add, ALU.add)
                stt(decayT[:, u, :], r, g, cst("maskT"), ALU.add, ALU.add, "decay_logs" if u == 7 else None)
            dve.wait_ge(sem("grow_ready"), 1)
            tt(grow, grow, cv[:, 0:4, P:T], ALU.mult, "rows_taken")
            dve.wait_ge(sem("decay_ready"), 2)
            dve.wait_ge(sem("kk_ready"), 1)
            dve.wait_ge(sem("beta_ready"), 1)
            for u in range(8):
                stt(M[:, u, :], mm[:, u // 4, (u % 4) * P:(u % 4 + 1) * P], beta[:, u % 2, u // 2:u // 2 + 1],
                    decay[:, u, :], ALU.mult, ALU.mult, "M_ready" if u == 7 else None)
            dve.wait_ge(sem("kq_ready"), 1)
            tt(attnT, ms[:, 2:4, :].rearrange("p b (j t) -> p (b j) t", j=4), decayT, ALU.mult, "attnT_ready")

            def level_mask(l):
                return cst("levelsT")[:, l * P:(l + 1) * P].unsqueeze(1).to_broadcast([P, 8, P])

            identb = ident.unsqueeze(1).to_broadcast([P, 8, P])
            S.settle()
            tt(Pm, M, cst("level0").unsqueeze(1).to_broadcast([P, 8, P]), ALU.mult)
            S.settle()
            tt(X, identb, Pm, ALU.subtract)
            dve.wait_ge(sem("M_turned"), 1)
            S.did(dve.tensor_copy(MT, mm[:, 0:2, :].rearrange("p b (j t) -> p (b j) t", j=4)))
            S.settle()
            tt(Ml[0], MT, level_mask(0), ALU.mult)
            tt(Ml[1], MT, level_mask(1), ALU.mult, "corner_ready")
            dve.wait_ge(sem("v_turned"), 1)
            for u in range(8):
                ts(vb[:, u, :], ms[:, u // 4, (u % 4) * P:(u % 4 + 1) * P], beta[:, u % 2, u // 2:u // 2 + 1], None,
                   ALU.mult)
            dve.wait_ge(sem("k_turned"), 1)
            dve.wait_ge(sem("column_decays"), 1)
            for i in range(4):
                ts(kdec[:, i, :], ms[:, 2, i * P:(i + 1) * P], ekd[:, i:i + 1], None, ALU.mult)
                ts(kbg[:, i, :], ms[:, 3, i * P:(i + 1) * P], beta[:, 1, i:i + 1], ecum[:, i:i + 1], ALU.mult,
                   ALU.mult, "tokens_ready" if i == 3 else None)
            S.settle()
            for u in range(2):
                tt(XT[:, 4 * u:4 * u + 4, :], ident.unsqueeze(1).to_broadcast([P, 4, P]), Ml[0][:, 4 * u:4 * u + 4, :],
                   ALU.subtract, "X_ready")
            for l in range(1, LEVELS):
                for u in range(2):
                    dve.wait_ge(sem("MX_ready"), 2 * (l - 1) + u + 1)
                    S.did(dve.tensor_copy(Pm[:, 4 * u:4 * u + 4, :], ms[:, u, :].rearrange("p (j t) -> p j t", j=4)),
                          "MX_taken")
                if l + 1 < LEVELS:
                    tt(Ml[(l + 1) % 2], MT, level_mask(l + 1), ALU.mult, "corner_ready")
                for u in range(2):
                    sl = slice(4 * u, 4 * u + 4)
                    dve.wait_ge(sem("XMX_ready"), 2 * (l - 1) + u + 1)
                    tt(X[:, sl, :], X[:, sl, :], ms[:, u, :].rearrange("p (j t) -> p j t", j=4), ALU.subtract)
                    tt(XT[:, sl, :], XT[:, sl, :], ms[:, 2 + u, :].rearrange("p (j t) -> p j t", j=4), ALU.subtract,
                       "X_ready")
            dve.wait_ge(sem("vn0_ready"), 1)
            S.did(dve.tensor_copy(vn[0], mm[:, 0, :].rearrange("p (j t) -> p j t", j=4)), "vn0_taken")
            dve.wait_ge(sem("w_ready"), 1)
            ts(nwT, mm[:, 1, :].rearrange("p (j t) -> p j t", j=4), -1.0, None, ALU.mult, None, "w_taken")
            dve.wait_ge(sem("state_ready"), 1)
            S.did(dve.tensor_copy(S1, mm[:, 2, :].rearrange("p (j t) -> p j t", j=4)), "state_taken")
            dve.wait_ge(sem("vn1_ready"), 1)
            S.did(dve.tensor_copy(vn[1], mm[:, 0, :].rearrange("p (j t) -> p j t", j=4)), "vn1_taken")
            for u in range(8):
                ts(diag2[:, u, :], ident, imb[:, u % 2, u // 2:u // 2 + 1], None, ALU.mult, None,
                   "diag2_ready" if u == 7 else None)

            def head_norm(which, o, gain, gate, done, cut_o):
                dve.wait_ge(sem("head_sums"), which + 1)
                inv = scratch[:, 1024:2048]
                ts(inv, ms[:, 2:4, :].rearrange("p b n -> p (b n)"), 1.0 / P, EPS, ALU.mult, ALU.add)
                S.settle()
                S.did(dve.reciprocal(inv, inv), "head_inverse")
                tt(gate, gate, o, ALU.mult, done)
                dve.wait_ge(sem("head_rstd"), which + 1)
                S.settle()
                for i in range(4):
                    stt(o[:, i, :], gate[:, i, :], gain[i], inv[:, i * T:(i + 1) * T], ALU.mult, ALU.mult)
                cut_parts(cut_o[:, 0], cut_o[:, 1], o, done or "ob_done")

            head_norm(0, oa, [v("gdn_norm")] * 4, gz, "oa_done", oas)

            dve.wait_ge(sem("ml_rows_ready"), 1)
            for i in range(4):
                r = mm[:, 1 + i // 2, (i % 2) * T:(i % 2 + 1) * T]
                stt(Dlog[:, i, 0:P], r[:, 0:P], cum[:, 0, 4 + i:5 + i], cst("mask")[:, P:2 * P], ALU.add, ALU.add)
                stt(Dlog[:, i, P:3 * P], r, cum[:, 1, 4 + i:5 + i], cst("mask"), ALU.add, ALU.add,
                    "ml_rows_taken" if i == 3 else None)
            S.settle()
            S.did(dve.tensor_reduce(mx[:, 0, :], Dlog[:, :, 0:P], AX.X, ALU.max))
            S.did(dve.tensor_reduce(mx[:, 1, :], Dlog[:, :, P:3 * P], AX.X, ALU.max))
            S.settle()
            tt(mx, mx, cum[:, :, 4:8], ALU.max)
            S.settle()
            ts(nm, mx, -1.0, None, ALU.mult, None, "ml_nm")
            dve.wait_ge(sem("ml_weights"), 1)
            dve.wait_ge(sem("ml_qk_ready"), 1)
            for i in range(4):
                stt(Em[:, i, 0:P], ms[:, i, 0:P], 64.0 ** -0.5, Em[:, i, 0:P], ALU.mult, ALU.mult,
                    accum_out=den[:, 0, i:i + 1])
                stt(Em[:, i, P:3 * P], ms[:, i, P:3 * P], 64.0 ** -0.5, Em[:, i, P:3 * P], ALU.mult, ALU.mult,
                    accum_out=den[:, 1, i:i + 1])
            S.settle()
            ts(nden, den, -1.0, None, ALU.mult)
            S.settle()
            tt(nden, nden, den, ALU.max)
            S.settle()
            tt(nden, nden, flo, ALU.max)
            S.settle()
            S.did(dve.reciprocal(rden, nden))
            S.settle()
            for i in range(4):
                ts(Em[:, i, 0:P], Em[:, i, 0:P], rden[:, 0, i:i + 1], None, ALU.mult)
                ts(Em[:, i, P:3 * P], Em[:, i, P:3 * P], rden[:, 1, i:i + 1], None, ALU.mult, None,
                   "ml_scores" if i == 3 else None)
            head_norm(1, ob, [v("ml_norm", i, i + 1) for i in range(4)], mo, None, obs)

            dve.wait_ge(sem("tiles_used"), USED0["mod"] + 24 * MODS)
            tt(mod[:, :], mm[:, 3, 0:24 * MODS], v("mod_b"), ALU.add, "mods_taken")
            S.settle()
            mod3 = mod[:, :].rearrange("p (i s) -> p i s", i=MODS)
            ts(modg[:, :].rearrange("p (i s) -> p i s", i=MODS), mod3[:, :, 8:16], 1.0, None, ALU.add)
            S.settle()
            tt(modg[:, :], modg[:, :], v("norms2"), ALU.mult)

            for j in range(8):
                n = OUT0["branch_a"] + j
                tt(gates[:, j, :], bank(n), gates[:, j, :], ALU.mult, taken(n))
            for j in range(8):
                n = OUT0["branch_b"] + j
                tt(gates[:, 8 + j, :], bank(n), gates[:, 8 + j, :], ALU.mult, taken(n))
                S.settle()
                tt(gates[:, j, :], gates[:, j, :], gates[:, 8 + j, :], ALU.add)
                cut_parts(mixs[:, 0, j, :], mixs[:, 1, j, :], gates[:, j, :], "mixed")

            def residual(stage, gate=None):
                for j in range(KD):
                    n = OUT0[stage] + j
                    src = bank(n)
                    if gate is None:
                        tt(x[:, j, :], src, x[:, j, :], ALU.add, taken(n))
                    else:
                        stt(x[:, j, :], src, gate[:, j:j + 1], x[:, j, :], ALU.mult, ALU.add, taken(n))
                S.settle()
                S.did(dve.memset(tiny[:, 511:512], 0.0), "x_done")

            residual("w_out")
            norm(1, v("g_ffn"))
            for j in range(FFG):
                out_taken(dve, OUT0["ffn_up"] + 2 * j)
                n = OUT0["ffn_up"] + 2 * j + 1
                src = bank(n)
                tt(ffact[:, j % 2, :], src, up[:, j % 2, :], ALU.mult, taken(n))
                cut_parts(ffs_[:, 0, j, :], ffs_[:, 1, j, :], ffact[:, j % 2, :], "ffact_cut")
            residual("ffn_down")
            norm(2, v("g_ple"))
            for j in range(KD):
                n = OUT0["ple"] + j
                out_taken(dve, OUT0["ple_gate"] + j)
                src = bank(n)
                tt(pleg[:, j, :], src, pleg[:, j, :], ALU.mult, taken(n))
            S.settle()
            tt(x[:, :, :], x[:, :, :], pleg, ALU.add, "x_done")
            norm(3, v("g_final"))

            c0, c1, c2, c3, c4, c5 = (lruc[:, i, :] for i in range(6))
            ts(c4, v("lam"), -1.0, None, ALU.mult)
            S.settle()
            tt(c0, c4, v("lam"), ALU.min, "nlam_ready")
            ts(c4, c4, 0.0, None, ALU.max)
            dve.wait_ge(sem("lam_exp"), 1)
            S.settle()
            ts(c2, c1, 2.0, None, ALU.add)
            S.settle()
            S.did(dve.reciprocal(c2, c2))
            S.settle()
            tt(c1, c1, c2, ALU.mult)
            S.settle()
            tt(c2, c1, c1, ALU.mult)
            S.settle()
            ts(c3, c2, 2.0 / 17, 2.0 / 15, ALU.mult, ALU.add)
            for d in (13, 11, 9, 7, 5, 3, 1):
                S.settle()
                tt(c3, c3, c2, ALU.mult)
                S.settle()
                ts(c3, c3, 2.0 / d, None, ALU.add)
            S.settle()
            tt(c3, c3, c1, ALU.mult)
            S.settle()
            tt(c3, c3, c4, ALU.add)
            S.settle()
            ts(c5, c3, 4.0, None, ALU.mult, None, "lru_rate")
            norm(4, modg[:, 0:8])
            S.did(dve.memset(lx[0:BLK, :, 0:3], 0.0), "lru_pad_zero")
            for j in range(NBLK):
                out_taken(dve, lru_out_of("x", j))
                w = v("lru_conv", 4 * j, 4 * j + 4, BLK)
                ts(lc[0:BLK, j, :], lx[0:BLK, j, 0:T], w[:, 0:1], v("lru_conv_b", j, j + 1, BLK), ALU.mult, ALU.add)
                for s in range(1, 4):
                    S.settle()
                    stt(lc[0:BLK, j, :], lx[0:BLK, j, s:s + T], w[:, s:s + 1], lc[0:BLK, j, :], ALU.mult, ALU.add,
                        "lru_conv" if s == 3 else None)
            dve.wait_ge(sem("lru_tanh"), NBLK)
            out_taken(dve, lru_out_of("ri", NBLK - 1))
            S.settle()
            ts(lr[0:BLK], lt[0:BLK], 1.0, None, ALU.add)
            tt(li[0:BLK], li[0:BLK], lc[0:BLK], ALU.mult)
            S.settle()
            S.did(dve.reciprocal(lr[0:BLK], lr[0:BLK]), "lru_rec")
            S.settle()
            stt(li[0:BLK], lr[0:BLK], 2.0, li[0:BLK], ALU.mult, ALU.mult)
            ts(lc[0:BLK], lr[0:BLK], 2.0, -1.0, ALU.mult, ALU.add)
            dve.wait_ge(sem("lru_root"), 1)
            S.settle()
            tt(li[0:BLK], li[0:BLK], lt[0:BLK], ALU.mult)
            S.settle()
            for j in range(NBLK):
                S.did(dve.tensor_tensor_scan(lr[0:BLK, j, :], lc[0:BLK, j, :], li[0:BLK, j, :], 0.0, ALU.mult, ALU.add))
            dve.wait_ge(sem("lru_gelu"), 1)
            S.settle()
            for j in range(NBLK):
                tt(lt[0:BLK, j, :], lr[0:BLK, j, :], lg[0:BLK, j, :], ALU.mult)
                cut_parts(ys[0:BLK, 0, j, :], ys[0:BLK, 1, j, :], lt[0:BLK, j, :], "lru_y")
            residual("lru_out", mod[:, 16:24])

            def experts(L):
                i = 1 + 2 * L
                norm(5 + 2 * L, modg[:, 8 * i:8 * i + 8])
                for c in range(TT):
                    route_tile(L, c)
                for c in range(TT):
                    out_taken(dve, OUT0[f"peer{L}_turn"] + c)
                def onehots(r, j, b, used):
                    if used is not None:
                        dve.wait_ge(sem("outs"), used)
                    for k in range(4):
                        t = r * 16 + (4 * j + k)
                        dve.tensor_scalar(onehot[:, b, 0, k, :], iota, routeT[:, 0, bass.ds(t, 1)],
                                          routeT[:, 2, bass.ds(t, 1)], ALU.is_equal, ALU.mult)
                        ins = dve.tensor_scalar(onehot[:, b, 1, k, :], iota, routeT[:, 1, bass.ds(t, 1)], None,
                                                ALU.is_equal)
                    ins.then_inc(sem("onehots"), 1)

                n0 = OUT0[f"peer{L}_place"]
                with dve.Fori(0, T // 16) as r:
                    for j in range(4):
                        onehots(r, j, j % 2, r * 4 + (n0 + j - 2 + 1))

                def weigh(j, r, first=False):
                    s_ = KEYS * L + j + 1
                    dve.wait_ge(sem("hidden_taken"), r * UNROLL + s_)
                    g = placed[:, bass.ds(r * UNROLL + j, 1), :].rearrange("p e t -> p (e t)")
                    dve.tensor_tensor(mix[:, j % 3, :], mix[:, j % 3, :], g, ALU.mult).then_inc(sem("hidden_weighted"), 1)
                    if not (first and j < 3):
                        dve.wait_ge(sem("tiles_used"), r * UNROLL + (USED0[f"peer{L}_experts"] + j - 3 + 1))
                    dve.wait_ge(sem("hidden_weighted"), r * UNROLL + s_)
                    dve.tensor_copy(wts[:, j % 3, 0, :], mix[:, j % 3, :]).then_inc(sem("weighted_high"), 1)
                    dve.wait_ge(sem("weighted_high"), r * UNROLL + s_)
                    dve.tensor_tensor(wts[:, j % 3, 1, :], mix[:, j % 3, :], wts[:, j % 3, 0, :].bitcast(F32),
                                      ALU.subtract).then_inc(sem("weighted"), 1)

                for j in range(4):
                    out_taken(dve, n0 + T // 4 - 4 + j)
                for j in range(UNROLL):
                    weigh(j, 0, True)
                with dve.Fori(1, KEYS // UNROLL) as r:
                    for j in range(UNROLL):
                        weigh(j, r)
                for j in range(KEYS - KEYS // UNROLL * UNROLL):
                    weigh(j, KEYS // UNROLL)
                dve.wait_ge(sem("tiles_used"), USED0[f"peer{L}_experts"] + KEYS)
                for m in range(KD):
                    g = mod[:, 24 * i + 16 + m:24 * i + 17 + m]
                    stt(x[:, m, :], ms[:, m // 2, (m % 2) * T:(m % 2 + 1) * T], g, x[:, m, :], ALU.mult, ALU.add,
                        "x_done" if m == KD - 1 else None)

            def route_tile(L, c):
                for g in range(4):
                    out_taken(dve, OUT0[f"peer{L}_scores"] + 4 * c + g)
                if c or L:
                    S.settle()

                def best16(vals, idx, src, spare, count):
                    for rnd in range(2):
                        s = src if rnd == 0 else spare
                        lo, hi = 8 * rnd, 8 * rnd + 8
                        for j in range(count):
                            S.did(dve.max(vals(j)[:, lo:hi], s(j)))
                        S.settle()
                        for j in range(count):
                            S.did(dve.max_index(idx(j)[:, lo:hi], vals(j)[:, lo:hi], s(j)))
                        if rnd == 0:
                            for j in range(count):
                                S.did(dve.match_replace(spare(j), vals(j)[:, 0:8], src(j), LOWEST))
                            S.settle()
                    S.settle()

                best16(lambda j: top[:, j // 2, j % 2, :], lambda j: topi[:, j // 2, j % 2, :],
                       lambda j: es[:, c, j, :], lambda j: es2[:, j, :], 16)
                S.did(dve.tensor_copy(topf_flat, topi_flat))
                cand4 = cand.rearrange("p j (a b) -> p j a b", a=16)
                for j in range(PH):
                    tt(cand4[:, j], top[:, j, 0, :].unsqueeze(2).to_broadcast([P, 16, 16]),
                       top[:, j, 1, :].unsqueeze(1).to_broadcast([P, 16, 16]), ALU.add)
                S.settle()
                besti3 = besti.rearrange("p (j k) -> p j k", j=PH)
                best16(lambda j: best[:, j, :], lambda j: besti3[:, j, :],
                       lambda j: cand[:, j, :], lambda j: cand2[:, j, :], PH)
                ts(part[:, 0, :], besti, 4, None, ALU.logical_shift_right)
                ts(part[:, 1, :], besti, 15, None, ALU.bitwise_and)
                if c or L:
                    dve.wait_ge(sem("best_exp"), TT * L + c)
                tt(shifted, best, best[:, :, 0:1].to_broadcast([P, PH, 16]), ALU.subtract, "best_shifted")
                S.settle()
                S.did(dve.tensor_copy(partf, part))
                S.settle()
                for s in range(2):
                    hot3 = hot.rearrange("p (q a) -> p q a", a=16)
                    tt(hot3, partf[:, s, :].unsqueeze(2).to_broadcast([P, P, 16]),
                       iota[:, 0:16].unsqueeze(1).to_broadcast([P, P, 16]), ALU.is_equal)
                    S.settle()
                    hot4 = hot.rearrange("p (j k a) -> p j k a", j=PH, k=16)
                    prod = hot2.rearrange("p (j k a) -> p j k a", j=PH, k=16)
                    for j in range(PH):
                        tt(prod[:, j], hot4[:, j], topf[:, j, s, :].unsqueeze(1).to_broadcast([P, 16, 16]), ALU.mult)
                    S.settle()
                    S.did(dve.tensor_reduce(route[:, c, s, :], hot2.rearrange("p (q a) -> p q a", a=16), AX.X,
                                            ALU.add))
                dve.wait_ge(sem("best_exp"), TT * L + c + 1)
                S.did(dve.tensor_reduce(sums, expo, AX.X, ALU.add))
                S.settle()
                S.did(dve.reciprocal(rsums, sums))
                S.settle()
                tt(route[:, c, 2, :].rearrange("p (j k) -> p j k", j=PH), expo,
                   rsums.unsqueeze(2).to_broadcast([P, PH, 16]), ALU.mult, "routed")

            experts(0)

            norm(6, modg[:, 16:24])
            n = OUT0["fox_small"]
            src = bank(n, width=32).rearrange("p (c j) -> p c j", c=TT)
            tt(ffz, src, v("fox_fb").unsqueeze(1).to_broadcast([P, TT, 16]), ALU.add, taken(n))
            S.settle()
            ts(ffs, ffz, -1.0, None, ALU.mult)
            S.settle()
            tt(ffn_, ffs, ffz, ALU.min, "fox_nz")
            ts(ffs, ffs, 0.0, None, ALU.max)
            dve.wait_ge(sem("fox_ln"), 1)
            S.settle()
            tt(ffs, ffs, ffl, ALU.add)
            S.settle()
            S.did(dve.memset(tiny[:, 509:510], 0.0), "fox_logf")
            n += 1
            S.did(dve.tensor_copy(fcum, bank(n, width=32).rearrange("p (c j) -> p c j", c=TT)), taken(n))
            S.settle()
            for hd in range(FH):
                for c in range(TT):
                    ts(fd[:, hd, c, :], ident, fcum[:, c, hd:hd + 1], None, ALU.mult, None,
                       "fox_diag" if hd == FH - 1 and c == TT - 1 else None)
            S.settle()
            ts(fcum, fcum, -1.0, None, ALU.mult)
            ts(fqg, v("fox_qg"), FE ** -0.5, None, ALU.mult)
            for s, f in enumerate((fq, fk)):
                for j in range(KD):
                    out_taken(dve, OUT0["fox_qk"] + 8 * s + j)
                tt(fsq[:, s * 2048:(s + 1) * 2048], f, f, ALU.mult, "fox_sq")
            for s, f in enumerate((fq, fk)):
                sq = fsq[:, s * 2048:(s + 1) * 2048]
                out_ready(dve, OUT0["fox_squares"] + 4 * s + 3)
                S.settle()
                for j in range(4):
                    n = OUT0["fox_squares"] + 4 * s + j
                    ts(sq[:, j * 512:(j + 1) * 512], bank(n, width=512), 1.0 / FE, EPS, ALU.mult, ALU.add, taken(n))
                S.settle()
                S.did(dve.reciprocal(sq, sq), "fox_inverse")
            for s, f in enumerate((fq, fk)):
                dve.wait_ge(sem("fox_rstd"), s + 1)
                stt(f, f, fqg if s == 0 else v("fox_kg"), fsq[:, s * 2048:(s + 1) * 2048], ALU.mult, ALU.mult,
                    "fox_normal")
            for i in range(FH + 4):
                if i < FH:
                    b = i % 3
                    n = OUT0[f"fox_scores{i}"]
                    src = bank(n, width=384)
                    if i >= 3:
                        dve.wait_ge(sem("fox_exp"), i - 2)
                    stt(fL[:, b, 0:P], src[:, 0:P], fcum[:, 0, i:i + 1], cst("mask")[:, P:2 * P], ALU.add, ALU.add)
                    stt(fL[:, b, P:3 * P], src[:, P:3 * P], fcum[:, 1, i:i + 1], cst("mask"), ALU.add, ALU.add, taken(n))
                    S.settle()
                    S.did(dve.tensor_reduce(fmx[:, b, 0:1], fL[:, b, 0:P], AX.X, ALU.max))
                    S.did(dve.tensor_reduce(fmx[:, b, 1:2], fL[:, b, P:3 * P], AX.X, ALU.max))
                    S.settle()
                    ts(fnm[:, b, :], fmx[:, b, :], -1.0, None, ALU.mult, None, "fox_max")
                if 1 <= i <= FH:
                    b = (i - 1) % 3
                    dve.wait_ge(sem("fox_exp"), i)
                    S.did(dve.reciprocal(frs[:, b, :], fsum[:, b, :]))
                    S.settle()
                    ts(fP[:, b, 0:P], fP[:, b, 0:P], frs[:, b, 0:1], None, ALU.mult)
                    ts(fP[:, b, P:3 * P], fP[:, b, P:3 * P], frs[:, b, 1:2], None, ALU.mult, None, "fox_probs")
                if i >= 5 and i % 2 == 1:
                    a = (i - 5) // 2
                    dve.wait_ge(sem("fox_pv"), 2 * a + 2)
                    tt(fy[:, a % 2, :], ms[:, a % 4, 0:T], fo[:, a, :], ALU.mult)
                    cut_parts(fys[:, 0, a, :], fys[:, 1, a, :], fy[:, a % 2, :], "fox_y")
            residual("fox_out", mod[:, 24 * 2 + 16:24 * 2 + 24])
            experts(1)


def host_constants():
    c = np.zeros((P, CONSTW), np.float32)
    i, j = np.arange(P)[:, None], np.arange(P)[None, :]

    def put(name, a):
        c[:, CONST0[name][0]:CONST0[name][1]] = a

    put("ident", i == j)
    put("upper", i <= j)
    put("ones", 1.0)
    put("heads", i // 64 == j // 64)
    put("iota", j + 0 * i)
    put("mask", np.concatenate([np.zeros((P, P)), np.where(j > i, -BIG, 0.0)], 1))
    put("maskT", np.where(j < i, BIG, 0.0))
    levels = []
    for l in range(LEVELS):
        b = 1 << l
        levels.append((i // (2 * b) == j // (2 * b)) & (i % (2 * b) >= b) & (j % (2 * b) < b))
    put("level0", levels[0])
    put("levelsT", np.concatenate([m.T for m in levels], 1))
    return c


def columns(w, groups=KD):
    k, n = w.shape
    wide = SLOT // groups
    return w.reshape(k // P // groups, groups, P, n // wide, wide).transpose(3, 0, 2, 1, 4).reshape(-1, P, SLOT)


def kernel(**inputs):
    import concourse.bacc as bacc
    from concourse.bass_utils import run_bass_kernel_spmd

    a = {k: np.asarray(val) for k, val in inputs.items()}
    w_in = a["w_in"][0]
    at = np.cumsum([0, 512, 512, 512, 512, 4, 4, 256, 256, 512, 512, 4, 4, 1024, 1024])
    gq, gk, gv, gz, gb, ga, mq, mk, mv, mo, mi, mf, ta, tb = (w_in[:, s:e] for s, e in zip(at[:-1], at[1:]))

    s = {}
    s["qkv"] = columns(np.concatenate([gq, gk, gv], 1))
    s["gz"] = columns(gz)
    s["mqk"] = columns(np.concatenate([mq, mk], 1))
    s["mv"] = columns(mv, 4)
    s["mo"] = columns(mo)
    s["gates"] = columns(np.concatenate([ta, tb], 1))
    mods = ["l0_mix", "l0_ffn", "l1_mix", "l1_ffn"]
    s["mod"] = np.concatenate([columns(a[f"{m}_mod_w_2"]) for m in mods], 0)
    s["branch_a"] = columns(a["w_branch_a"][0], 4)
    s["branch_b"] = columns(a["w_branch_b"][0], 4)
    s["w_out"] = columns(a["w_out"][0])
    both = np.stack([a["w1"][0].reshape(D, FFG, P), a["w3"][0].reshape(D, FFG, P)], 2).reshape(D, FFG * 256)
    s["ffn_up"] = columns(both)
    s["ffn_down"] = a["w2"][0].reshape(FFG, P, KD, P).transpose(2, 1, 0, 3).reshape(KD, P, FF)
    s["ple_gate"] = columns(a["w_ple_gate"][0])
    s["ple"] = columns(a["w_ple"][0], 2)
    s["lru_in"] = a["l0_lru_in_w_2"].reshape(KD, P, 2, NBLK, BLK).transpose(3, 2, 1, 0, 4).reshape(2 * NBLK, P, -1)
    lo = np.zeros((KD, 2, 96, 8, P), np.float32)
    lo[:, :, 0:BLK] = a["l0_lru_out_w_2"].reshape(2, 8, BLK, KD, P).transpose(3, 0, 2, 1, 4)
    s["lru_out"] = lo.reshape(2 * KD, 96, SLOT)
    fox = a["l1_fox_in_w_2"]
    s["fox_qk"] = columns(fox[:, 0:2 * D])
    s["fox_v"] = columns(fox[:, 2 * D:3 * D], 4)
    s["fox_og"] = columns(fox[:, 3 * D + FH:])
    s["fox_out"] = columns(a["l1_fox_out_w_2"])
    for L in range(2):
        s[f"peer{L}_q"] = columns(a[f"l{L}_peer_q_w_2"])
        keys = np.stack([a[f"l{L}_peer_subkey1_2"], a[f"l{L}_peer_subkey2_2"]], 1)
        s[f"peer{L}_keys"] = keys.reshape(2, PH // 2, 2, KEYS, P).transpose(0, 4, 1, 2, 3).reshape(2, P, SLOT)
        u = a[f"l{L}_peer_u_2"].reshape(KEYS, KEYS, KD, P).transpose(1, 3, 2, 0).reshape(KEYS, P, D)
        vv = a[f"l{L}_peer_v_2"].reshape(KEYS, KEYS, D).transpose(1, 0, 2)
        kinds = [expert_tile(i) for i in range(2 * KEYS)]
        s[f"peer{L}_experts"] = np.stack([(u if kind == "u" else vv)[step] for kind, step in kinds])

    def per_channel(w):
        return w.reshape(-1, P).T

    def blocks88(w):
        o = np.zeros((P, NBLK), np.float32)
        o[0:BLK] = w.reshape(NBLK, BLK).T
        return o

    vecs = np.zeros((P, VECW), np.float32)

    def put(name, w):
        vecs[:, VEC0[name][0]:VEC0[name][1]] = w

    put("g_mix", per_channel(a["g_mix"]))
    put("g_ffn", per_channel(a["g_ffn"]))
    put("g_ple", per_channel(a["g_ple"]))
    put("g_final", per_channel(a["g_final"]))
    put("gdn_norm", a["gdn_norm"][0][:, None])
    put("ml_norm", a["ml_norm"][0].T)
    put("conv", a["conv_w"][0].reshape(4, 12, P).transpose(2, 1, 0).reshape(P, 48))
    put("norms2", np.concatenate([per_channel(a[f"{m}_norm_g_2"]) for m in mods], 1))
    put("mod_b", np.concatenate([per_channel(a[f"{m}_mod_b_2"]) for m in mods], 1))
    put("c", per_channel(a["c_2"]))
    zero4 = np.zeros(4, np.float32)
    put("gate_bias", np.concatenate([zero4, a["dt_bias"][0], a["ml_i_bias"][0], a["ml_f_bias"][0]])[None, :])
    put("a_log", a["a_log"][0][None, :])
    lcw = np.zeros((P, NBLK, 4), np.float32)
    lcw[0:BLK] = a["l0_lru_conv_w_2"].reshape(4, NBLK, BLK).transpose(2, 1, 0)
    put("lru_conv", lcw.reshape(P, 64))
    put("lru_conv_b", blocks88(a["l0_lru_conv_b_2"]))
    put("ra_b", blocks88(a["l0_lru_ra_b_2"]))
    put("ri_b", blocks88(a["l0_lru_ri_b_2"]))
    put("lam", blocks88(a["l0_lru_lambda_2"]))
    put("fox_fb", a["l1_fox_f_b_2"][None, :])
    put("fox_qg", np.concatenate([a["l1_fox_q_norm_g_2"]] * 2)[:, None])
    put("fox_kg", np.concatenate([a["l1_fox_k_norm_g_2"]] * 2)[:, None])

    lgw = np.zeros((96, NBLK, 2, BLK), np.float32)
    lgw[0:BLK, :, 0] = a["l0_lru_ra_w_2"].transpose(1, 0, 2)
    lgw[0:BLK, :, 1] = a["l0_lru_ri_w_2"].transpose(1, 0, 2)

    arrays = {f"w_{name}": w for name, w in s.items()}
    arrays["xT"] = a["x"][0].T.reshape(KD, P, T).transpose(1, 0, 2)
    arrays["pT"] = a["p"][0, 0].T.reshape(2, P, T).transpose(1, 0, 2)
    arrays["consts"] = host_constants()
    arrays["vecs"] = vecs
    arrays["small_w"] = np.concatenate([gb, ga, mi, mf], 1).reshape(KD, P, 16).transpose(1, 0, 2)
    arrays["fox_f_w"] = fox[:, 3 * D:3 * D + FH].reshape(KD, P, 16).transpose(1, 0, 2)
    arrays["lru_gate_w"] = lgw
    arrays = {k: np.ascontiguousarray(w) for k, w in arrays.items()}

    nc = bacc.Bacc("TRN2", target_bir_lowering=False, num_devices=1, dynamic_dma_scratch_size=1024)
    dram = {k: nc.dram_tensor(k, list(w.shape), F32, kind="ExternalInput").ap() for k, w in arrays.items()}
    out = nc.dram_tensor("out", [P, KD, T], F32, kind="ExternalOutput").ap()
    build(nc, {name: dram[f"w_{name}"] for name in s}, *(dram[k] for k in (
        "xT", "pT", "consts", "vecs", "small_w", "fox_f_w", "lru_gate_w")), out)
    r = run_bass_kernel_spmd(nc, [arrays], core_ids=[0])
    y = r.results[0]["out"]
    return y.transpose(2, 1, 0).reshape(1, T, D)
```

```python
from contextlib import ExitStack

import numpy as np

import concourse.bass as bass
from concourse import mybir

F32 = mybir.dt.float32
F32R = mybir.dt.float32r
U32 = mybir.dt.uint32
ACT = mybir.ActivationFunctionType
ALU = mybir.AluOpType
AX = mybir.AxisListType

P = 128
T = 256
TT = T // P
D = 1024
KD = D // P
EPS = 1e-6
BIG = 1e30
LOWEST = -3e38

RAW = 4
CUT = 3
SLOT = 1024
UNROLL = 6
EARLY = 36
LAG = 2
BANKS = 4

GH = 4
FF = 2816
FFG = FF // P
BLK = 88
NBLK = 16
FH = 16
FE = 64
PH = 8
TOPK = 16
KEYS = 128
MOD_SUMS = 4
SCALED = 6
LEVELS = 7
MODS = 4
EARLY_MODS = 3 * (MODS - 1)

STREAM = [
    ("qkv", 12, 1024, P, True), ("gz", 4, 1024, P, True), ("mqk", 4, 1024, P, True), ("mv", 4, 1024, P, True),
    ("mo", 4, 1024, P, True), ("gates", 16, 1024, P, True), ("mod", 24 * (MODS - 1), 1024, P, False),
    ("branch_a", 4, 1024, P, True), ("branch_b", 4, 1024, P, True), ("w_out", 8, 1024, P, True),
    ("ffn_up", 2 * FFG, 1024, P, True), ("last_mod", 24, 1024, P, False), ("ffn_down", 24, 1024, P, True), ("ple_gate", 8, 1024, P, True),
    ("ple", 2, 1024, P, False),
    ("lru_in", 2 * NBLK, KD * BLK, P, True), ("lru_out", 2 * KD, 1024, 96, True),
    ("peer0_q", 16, 1024, P, True), ("peer0_keys", 2, 1024, P, False), ("peer0_experts", 2 * KEYS, 1024, P, True),
    ("fox_q", 8, 1024, P, True), ("fox_k", 8, 1024, P, True), ("fox_v", 8, 1024, P, True), ("fox_og", 8, 1024, P, True),
    ("fox_out", 8, 1024, P, True),
    ("peer1_q", 16, 1024, P, True), ("peer1_keys", 2, 1024, P, False), ("peer1_experts", 2 * KEYS, 1024, P, True),
]
DOWN = (8, 8, 6)
TILE0 = {}
CUT0 = {}
RUN_END = {}
_n = _q = 0
for _name, _count, _w, _p, _cut in STREAM:
    TILE0[_name] = _n
    _n += _count
    if _cut:
        CUT0[_name] = _q
        _q += _count
_end = _q
for _name, _count, _w, _p, _cut in reversed(STREAM):
    if _cut:
        RUN_END[_name] = _end - 1
    elif _name in ("mod", "ple", "peer0_keys", "peer1_keys"):
        _end = min([CUT0[k] for k in CUT0 if TILE0[k] > TILE0[_name]])

CONSTS = [("ident", P), ("upper", P), ("ones", P), ("heads", P), ("iota", P), ("mask", 2 * P),
          ("maskT", P), ("level0", P), ("levelsT", LEVELS * P)]
CONST0 = {}
_n = 0
for _name, _w in CONSTS:
    CONST0[_name] = (_n, _n + _w)
    _n += _w
CONSTW = _n
CON_KEPT = CONST0["maskT"][0]

VECS = [("g_mix", 8), ("g_ffn", 8), ("g_ple", 8), ("g_final", 8), ("gdn_norm", 1), ("ml_norm", 4),
        ("conv", 48), ("norms2", 32), ("mod_b", 96), ("c", 8), ("gate_bias", 16), ("a_log", 4),
        ("lru_conv", 64), ("lru_conv_b", 16), ("ra_b", 16), ("ri_b", 16), ("lam", 16),
        ("fox_fb", 16), ("fox_qg", 1), ("fox_kg", 1)]
VEC0 = {}
_n = 0
for _name, _w in VECS:
    VEC0[_name] = (_n, _n + _w)
    _n += _w
VECW = _n


class Signals:

    def __init__(self, nc, ctx):
        self.nc, self.ctx, self.sems = nc, ctx, {}

    def __call__(self, name):
        if name not in self.sems:
            self.sems[name] = self.ctx.enter_context(self.nc.semaphore(name))
        return self.sems[name]


class Steps:

    def __init__(self, eng, sem, own):
        self.eng, self.sem, self.own, self.count, self.last = eng, sem, own, {}, None

    def did(self, ins, name=None):
        if isinstance(name, tuple):
            self.last = name
        else:
            name = name or self.own
            self.count[name] = self.count.get(name, 0) + 1
            self.last = (name, self.count[name])
        ins.then_inc(self.sem(self.last[0]), 1)

    def settle(self):
        self.eng.wait_ge(self.sem(self.last[0]), self.last[1])


def fox_order():
    order = []
    for i in range(FH + 3):
        if i < FH:
            order.append(("scores", i))
        if 0 <= i - 2 < FH:
            order.append(("turn", i - 2))
        if 0 <= i - 3 < FH:
            order.append(("values", i - 3))
    return order


def count_outs():
    at, n = {}, 0

    def stage(name, count):
        nonlocal n
        at[name] = n
        n += count

    stage("norm0", 1)
    stage("qkv", 12)
    stage("small", 1)
    stage("gz", 4)
    stage("mqk", 4)
    stage("mv", 4)
    stage("mo", 4)
    stage("gates", 16)
    stage("branch_a", 8)
    stage("branch_b", 8)
    stage("w_out", 8)
    stage("norm1", 1)
    stage("ffn_up", 2 * FFG)
    stage("ffn_down", 8)
    stage("norm2", 1)
    stage("ple_gate", 8)
    stage("ple", 8)
    stage("norm3", 1)
    stage("norm4", 1)
    stage("lru", 4 * NBLK)
    stage("lru_out", 8)
    for layer in range(2):
        stage(f"norm{5 + 2 * layer}", 1)
        stage(f"peer{layer}_q", 16)
        stage(f"peer{layer}_scores", 8)
        stage(f"peer{layer}_turn", TT)
        stage(f"peer{layer}_place", T // 4)
        if layer == 0:
            stage("norm6", 1)
            stage("fox_q", 8)
            stage("fox_small", 1)
            stage("fox_k", 8)
            stage("fox_cum", 1)
            stage("fox_v", 8)
            stage("fox_squares", 8)
            stage("fox_og", 8)
            for kind, h in fox_order():
                if kind != "values":
                    stage(f"fox_{kind}{h}", 1)
            stage("fox_out", 8)
    return at


OUT0 = count_outs()


def lru_out_of(kind, j):
    base = OUT0["lru"]
    if kind in ("x", "g"):
        return base + (2 * j if j == 0 else 2 + 4 * (j - 1)) + (kind == "g")
    return base + (4 * j + 4 if j < NBLK - 1 else 4 * NBLK - 2) + (kind == "ri")


USED0, _n = {}, 0
for _name, _count in (("mv", 2), ("ffn_down", 2 * KD), ("lru_out", KD), ("peer0_experts", KEYS),
                      ("fox_v", 4), ("peer1_experts", KEYS)):
    USED0[_name] = _n
    _n += _count


def expert_tile(i):
    if i < EARLY:
        return "u", i
    if i < 2 * EARLY:
        return "v", i - EARLY
    i -= 2 * EARLY
    if i < LAG:
        return "u", EARLY + i
    if i >= 2 * (KEYS - EARLY) - LAG:
        return "v", EARLY + i - (KEYS - EARLY)
    return ("u", EARLY + LAG + (i - LAG) // 2) if (i - LAG) % 2 == 0 else ("v", EARLY + (i - LAG) // 2)


def tile_used(name, i):
    if name.endswith("experts"):
        kind, s = expert_tile(i)
        return ("hidden_ready", KEYS * int(name[4]) + s + 1) if kind == "u" else ("tiles_used", USED0[name] + s + 1)
    if name == "mod":
        return "mod_scaled", i + 1
    if name == "last_mod":
        return "mod_tiles_added", i + 1
    if name in ("mv", "fox_v"):
        return ("tiles_used", USED0[name] + i // 2 + 1) if i % 2 == 0 else ("outs", OUT0[name] + i + 1)
    if name == "ffn_down":
        m, part_ = i // 3, i % 3
        return ("tiles_used", USED0[name] + 2 * m + part_ + 1) if part_ < 2 else ("outs", OUT0[name] + m + 1)
    if name == "lru_out":
        return ("tiles_used", USED0[name] + i // 2 + 1) if i % 2 == 0 else ("outs", OUT0[name] + i // 2 + 1)
    if name == "lru_in":
        return "outs", lru_out_of("xg"[i % 2], i // 2) + 1
    if name.endswith("keys"):
        return "outs", OUT0[name.replace("keys", "scores")] + 6 + 2 * i
    per_tile = {"branch_a": 2, "branch_b": 2, "ple": 4}.get(name, 1)
    return "outs", OUT0[name] + per_tile * (i + 1)


H_NORMS = (0, 1, 2, 4, 5, 6, 7)


def tile_shape(name, i):
    for name_, _, width, rows, _ in STREAM:
        if name_ == name:
            return rows, P * DOWN[i % 3] if name == "ffn_down" else width


def stage_tiles(name, count):
    if name == "last_mod":
        return []
    if name != "ffn_up":
        return [(name, i) for i in range(count)]
    order = []
    for j in range(FFG):
        order += [(name, 2 * j), (name, 2 * j + 1), ("last_mod", j)]
    return order + [("last_mod", j) for j in range(FFG, 24)]


TILES = [tile for name, count, _, _, _ in STREAM for tile in stage_tiles(name, count)]
TILE_AT = {tile: n for n, tile in enumerate(TILES)}
CUTS = [(name, i) for name, count, _, _, cut in STREAM if cut for i in range(count)]


def raw_free(n):
    name, i = TILES[n]
    return ("low_done", CUT0[name] + i + 1) if name in CUT0 else tile_used(name, i)


def cut_free(q):
    return tile_used(*CUTS[q])


def build(nc, streams, xT, pT, consts, vecs, small_w, fox_f_w, lru_gate_w, out):
    with ExitStack() as ctx:
        sem = Signals(nc, ctx)

        def sb(name, shape, dt=F32):
            return ctx.enter_context(nc.sbuf_tensor(name, shape, dt))

        ring = sb("ring", [P, RAW, SLOT])
        with nc.sbuf_tensor("scaled", [P, SCALED, SLOT], F32) as scaled:
            pass
        high = sb("high", [P, CUT, SLOT], F32R)
        low = sb("low", [P, CUT, SLOT], F32R)
        x = sb("x", [P, KD, T])
        with nc.sbuf_tensor("mod_sums", [P, MOD_SUMS, SLOT], F32) as mod_sums:
            pass
        hs = sb("hs", [P, 2, KD, T], F32R)
        wts = sb("wts", [P, 3, 2, T], F32R)
        scratch = sb("scratch", [P, KD * T])
        con = sb("con", [P, CON_KEPT])
        vec = sb("vec", [P, VECW])
        wsmall = sb("wsmall", [P, KD, 16])
        wfox = sb("wfox", [P, KD, 16])
        rstd = sb("rstd", [P, T])
        mod = sb("mod", [P, 24 * MODS])
        modg = sb("modg", [P, KD * MODS])
        csilu = sb("csilu", [P, KD])
        lruc = sb("lruc", [P, 6, NBLK])
        routeT = sb("routeT", [P, 3, T])
        tiny = sb("tiny", [P, 512])
        with nc.sbuf_tensor("work", [P, KEYS * T], F32) as work:
            pass
        parts_ = ctx.enter_context(nc.sbuf_tensor("parts", [P, 2 * FFG * T], F32R))

        mm = ctx.enter_context(nc.psum_tensor("mm", [P, BANKS, 512], F32))
        ms = ctx.enter_context(nc.psum_tensor("ms", [P, 4, 512], F32))

        def cst(name):
            a_, b_ = CONST0[name]
            if a_ >= CON_KEPT:
                return masks[:, a_ - CON_KEPT:b_ - CON_KEPT]
            return con[:, a_:b_]

        def v(name, a=None, b=None, p=P):
            lo, hi = VEC0[name]
            return vec[0:p, lo + (a or 0):(hi if b is None else lo + b)]

        ident, upper, ones, heads64, iota = cst("ident"), cst("upper"), cst("ones"), cst("heads"), cst("iota")

        free = [0]

        def area(n, at=None):
            a = free[0] if at is None else at
            free[0] = a + n
            assert free[0] <= KEYS * T
            return work[:, a:a + n]

        def parts(groups, at=None):
            a = free[0] if at is None else at
            free[0] = a + 2 * groups * T
            assert free[0] <= 2 * FFG * T
            return parts_[:, a:a + 2 * groups * T].rearrange("p (s j t) -> p s j t", s=2, j=groups)

        cin = area(12 * (T + 3)).rearrange("p (j t) -> p j t", j=12)
        cv = area(12 * T).rearrange("p (j t) -> p j t", j=12)
        gz = area(GH * T).rearrange("p (j t) -> p j t", j=GH)
        mq = area(2 * T).rearrange("p (j t) -> p j t", j=2)
        mk = area(2 * T).rearrange("p (j t) -> p j t", j=2)
        mv = area(TT * 512).rearrange("p (c f) -> p c f", c=TT)
        mo = area(GH * T).rearrange("p (j t) -> p j t", j=GH)
        gates = area(16 * T).rearrange("p (j t) -> p j t", j=16)
        diag_at = free[0]
        diag = area(16 * P).rearrange("p (j t) -> p j t", j=16)
        vb = area(8 * P, diag_at).rearrange("p (j t) -> p j t", j=8)
        kbg = area(4 * P).rearrange("p (j t) -> p j t", j=4)
        kdec = area(4 * P).rearrange("p (j t) -> p j t", j=4)
        decay = area(8 * P).rearrange("p (j t) -> p j t", j=8)
        decayT = area(8 * P).rearrange("p (j t) -> p j t", j=8)
        grow = area(4 * P).rearrange("p (j t) -> p j t", j=4)
        m_at = free[0]
        M = area(8 * P).rearrange("p (j t) -> p j t", j=8)
        MT = area(8 * P).rearrange("p (j t) -> p j t", j=8)
        attnT = area(8 * P).rearrange("p (j t) -> p j t", j=8)
        x_at = free[0]
        X = area(8 * P).rearrange("p (j t) -> p j t", j=8)
        XT = area(8 * P).rearrange("p (j t) -> p j t", j=8)
        Pm = area(8 * P).rearrange("p (j t) -> p j t", j=8)
        ml_at = free[0]
        Ml = [area(8 * P).rearrange("p (j t) -> p j t", j=8) for _ in range(2)]
        vn = [area(4 * P).rearrange("p (j t) -> p j t", j=4) for _ in range(2)]
        nwT = area(4 * P).rearrange("p (j t) -> p j t", j=4)
        S1 = area(4 * P).rearrange("p (j t) -> p j t", j=4)
        oa = area(GH * T).rearrange("p (j t) -> p j t", j=GH)
        masks = area(CONSTW - CON_KEPT)
        free_ = free[0]
        oas = parts(GH, 0)
        obs = parts(GH)
        mixs = parts(KD)
        free[0] = free_
        Dlog = area(4 * 384, ml_at).rearrange("p (j t) -> p j t", j=4)
        Em = area(4 * 384, m_at).rearrange("p (j t) -> p j t", j=4)
        ST = area(4 * 384, x_at).rearrange("p (j t) -> p j t", j=4)
        diag2 = area(8 * P, diag_at).rearrange("p (j t) -> p j t", j=8)
        ob = area(GH * T, diag_at + 8 * P).rearrange("p (j t) -> p j t", j=GH)
        ffs_ = parts(FFG, 0)
        ffact = area(2 * T).rearrange("p (j t) -> p j t", j=2)
        up = area(2 * T).rearrange("p (j t) -> p j t", j=2)
        pleg = area(KD * T).rearrange("p (j t) -> p j t", j=KD)
        last_sums = area(3 * SLOT).rearrange("p (g n) -> p g n", g=3)
        pTs = area(2 * T).rearrange("p (j t) -> p j t", j=2)
        lx = area(NBLK * (T + 3), 0).rearrange("p (j t) -> p j t", j=NBLK)
        lc = area(NBLK * T).rearrange("p (j t) -> p j t", j=NBLK)
        lg = area(NBLK * T).rearrange("p (j t) -> p j t", j=NBLK)
        lt = area(NBLK * T).rearrange("p (j t) -> p j t", j=NBLK)
        li = area(NBLK * T).rearrange("p (j t) -> p j t", j=NBLK)
        lr = area(NBLK * T).rearrange("p (j t) -> p j t", j=NBLK)
        ys = parts(NBLK, 0)
        free[0] = (NBLK * (T + 3)) + 5 * NBLK * T
        lgw = area(NBLK * 2 * BLK).rearrange("p (j g d) -> p j g d", j=NBLK, g=2)
        fys = parts(KD, 0)
        fq = area(KD * T)
        fk = area(KD * T)
        fv = area(TT * D).rearrange("p (c f) -> p c f", c=TT)
        fo = area(KD * T).rearrange("p (j t) -> p j t", j=KD)
        fsq = area(2 * KD * T)
        fd = area(TT * FH * P).rearrange("p (j c t) -> p j c t", j=FH, c=TT)
        fL = area(3 * 384).rearrange("p (j t) -> p j t", j=3)
        fP = area(3 * 384).rearrange("p (j t) -> p j t", j=3)
        fPT = area(3 * 384).rearrange("p (j t) -> p j t", j=3)
        fy = area(2 * T).rearrange("p (j t) -> p j t", j=2)
        fq3 = fq.rearrange("p (j t) -> p j t", j=KD)
        fk3 = fk.rearrange("p (j t) -> p j t", j=KD)
        eq = area(16 * T, EARLY * T).rearrange("p (j t) -> p j t", j=16)
        es = area(TT * 16 * KEYS).rearrange("p (c j n) -> p c j n", c=TT, j=16)
        es2 = area(16 * KEYS).rearrange("p (j n) -> p j n", j=16)
        cand = area(PH * 256).rearrange("p (j n) -> p j n", j=PH)
        cand2 = area(PH * 256).rearrange("p (j n) -> p j n", j=PH)
        hot = area(PH * 256)
        hot2 = area(PH * 256)
        top = area(2 * PH * 16).rearrange("p (s j k) -> p j s k", j=PH, s=2)
        topi_flat = area(2 * PH * 16).bitcast(U32)
        topi = topi_flat.rearrange("p (s j k) -> p j s k", j=PH, s=2)
        topf_flat = area(2 * PH * 16)
        topf = topf_flat.rearrange("p (s j k) -> p j s k", j=PH, s=2)
        best = area(PH * 16).rearrange("p (j k) -> p j k", j=PH)
        besti = area(PH * 16).bitcast(U32)
        part = area(2 * PH * 16).bitcast(U32).rearrange("p (s k) -> p s k", s=2)
        partf = area(2 * PH * 16).rearrange("p (s k) -> p s k", s=2)
        shifted = area(TT * PH * 16).rearrange("p (c j k) -> p c j k", c=TT, j=PH)
        expo = area(TT * PH * 16).rearrange("p (c j k) -> p c j k", c=TT, j=PH)
        sums = area(PH)
        rsums = area(PH)
        route = area(TT * 3 * P).rearrange("p (c s k) -> p c s k", c=TT, s=3)
        placed = work[:, :].rearrange("p (e t) -> p e t", e=KEYS)
        mix = scratch[:, 0:3 * T].rearrange("p (j t) -> p j t", j=3)
        hf = scratch[:, :].rearrange("p (j t) -> p j t", j=KD)
        onehot = scratch[:, :].rearrange("p (b s i n) -> p b s i n", b=2, s=2, i=4)

        def col(a, n):
            return tiny[:, a:a + n]

        pre = col(0, 32).rearrange("p (c j) -> p c j", c=TT)
        zz = col(32, 16).rearrange("p (c j) -> p c j", c=TT)
        nz = col(48, 16).rearrange("p (c j) -> p c j", c=TT)
        en = col(64, 16).rearrange("p (c j) -> p c j", c=TT)
        ln = col(80, 16).rearrange("p (c j) -> p c j", c=TT)
        sp = col(96, 16).rearrange("p (c j) -> p c j", c=TT)
        expa = col(112, 4)
        lgt = col(116, 16).rearrange("p (c j) -> p c j", c=TT)
        beta = col(132, 8).rearrange("p (c j) -> p c j", c=TT)
        cum = col(140, 16).rearrange("p (c j) -> p c j", c=TT)
        gl = col(156, 4)
        ecum = col(160, 4)
        ekd = col(164, 4)
        gdif = col(168, 4)
        ngc = col(172, 8).rearrange("p (c j) -> p c j", c=TT)
        imb = col(180, 8).rearrange("p (c j) -> p c j", c=TT)
        mx = col(188, 8).rearrange("p (c j) -> p c j", c=TT)
        nm = col(196, 8).rearrange("p (c j) -> p c j", c=TT)
        flo = col(204, 8).rearrange("p (c j) -> p c j", c=TT)
        den = col(212, 8).rearrange("p (c j) -> p c j", c=TT)
        nden = col(220, 8).rearrange("p (c j) -> p c j", c=TT)
        rden = col(228, 8).rearrange("p (c j) -> p c j", c=TT)
        ffz = col(256, 32).rearrange("p (c j) -> p c j", c=TT)
        ffn_ = col(288, 32).rearrange("p (c j) -> p c j", c=TT)
        ffe = col(320, 32).rearrange("p (c j) -> p c j", c=TT)
        ffl = col(352, 32).rearrange("p (c j) -> p c j", c=TT)
        ffs = col(384, 32).rearrange("p (c j) -> p c j", c=TT)
        fcum = col(416, 32).rearrange("p (c j) -> p c j", c=TT)
        fmx = col(448, 6).rearrange("p (b c) -> p b c", b=3)
        fnm = col(454, 6).rearrange("p (b c) -> p b c", b=3)
        fsum = col(460, 6).rearrange("p (b c) -> p b c", b=3)
        frs = col(466, 6).rearrange("p (b c) -> p b c", b=3)
        fqg = col(472, 1)

        def tile_ready(eng, n):
            eng.wait_ge(sem(f"slot{n % RAW}_loaded"), 16 * (n // RAW + 1))

        def out_ready(eng, n):
            eng.wait_ge(sem("outs"), n + 1)

        def out_taken(eng, n):
            eng.wait_ge(sem(f"bank{n % BANKS}_taken"), n // BANKS + 1)

        def taken(n):
            return f"bank{n % BANKS}_taken", n // BANKS + 1

        block = ctx.enter_context(nc.Block())

        @block.sync
        def _(sp_):
            sp_.dma_start(x[:, :, :], xT).then_inc(sem("x_loaded"), 16)
            sp_.dma_start(vec[:, :], vecs).then_inc(sem("vec_loaded"), 16)
            sp_.dma_start(con[:, :], consts[:, 0:CON_KEPT]).then_inc(sem("con_loaded"), 16)
            sp_.dma_start(wsmall[:, :, :], small_w).then_inc(sem("wsmall_loaded"), 16)
            sp_.dma_start(wfox[:, :, :], fox_f_w).then_inc(sem("wfox_loaded"), 16)
            sp_.dma_start(masks, consts[:, CON_KEPT:CONSTW]).then_inc(sem("masks_loaded"), 16)
            for name, count, width, parts__, cut in STREAM:
                base = TILE0[name]
                src = streams.get(name)

                def load(n, which):
                    w = which.shape[-1]
                    sp_.dma_start(ring[0:parts__, n % RAW, 0:w], which).then_inc(sem(f"slot{n % RAW}_loaded"), 16)

                def load_one(i, name=name):
                    n = TILE_AT[name, i]
                    if n >= RAW:
                        what, value = raw_free(n - RAW)
                        sp_.wait_ge(sem(what), value)
                    if name == "ffn_down":
                        m, a_ = i // 3, i % 3 * SLOT
                        load(n, src[m][:, a_:a_ + P * DOWN[i % 3]])
                    else:
                        load(n, streams[name][i])

                if name == "ffn_up" or name == "last_mod":
                    for stage_, i in stage_tiles(name, count):
                        load_one(i, stage_)
                    continue
                if name != "mod" and not name.endswith("experts"):
                    for i in range(count):
                        load_one(i)
                    continue
                for i in range(RAW):
                    load_one(i)
                what, value = raw_free(base)
                with sp_.Fori(1, count // RAW) as r:
                    for j in range(RAW):
                        sp_.wait_ge(sem(what), r * RAW + (value + j - RAW))
                        load(base + j, src[bass.ds(r * RAW + j, 1), :, :].rearrange("a p w -> (a p) w"))
            sp_.wait_ge(sem("x_done"), 8)
            sp_.dma_start(out, x[:, :, :]).then_inc(sem("stored"), 16)
            sp_.wait_ge(sem("stored"), 16)

        @block.tensor
        def _(pe):
            S = Steps(pe, sem, "pe_step")
            mods_summed = [0]

            def bank(n):
                if n >= BANKS:
                    out_taken(pe, n - BANKS)
                return mm[:, n % BANKS, :]

            def slot(n):
                tile_ready(pe, n)
                return ring[:, n % RAW, :]

            def parts_of(name, i, width=SLOT):
                q = CUT0[name] + i
                pe.wait_ge(sem("high_done"), q + 1)
                return q, high[:, q % CUT, 0:width], low[:, q % CUT, 0:width]

            def low_ready(q):
                pe.wait_ge(sem("low_done"), q + 1)

            def three_passes(dst, q, ws, acts, first=True, last=True, swap=False):
                rows = len(ws)
                for s_, (a_, b_) in enumerate(((0, 0), (0, 1), (1, 0))):
                    if s_ == 2:
                        low_ready(q)
                    for k in range(rows):
                        l, r_ = ws[k][a_], acts[k][b_]
                        if swap:
                            l, r_ = r_, l
                        ins = pe.matmul(dst, l, r_, start=first and s_ == 0 and k == 0,
                                        stop=last and s_ == 2 and k == rows - 1, skip_group_check=True)
                return ins

            def group(dst, pairs, first=True):
                for i, (a, b) in enumerate(pairs):
                    ins = pe.matmul(dst, a, b, start=first and i == 0, stop=i == len(pairs) - 1,
                                    skip_group_check=True)
                return ins

            def norm(i, shifted_):
                n = OUT0[f"norm{i}"]
                if i == 0:
                    pe.wait_ge(sem("con_loaded"), 16)
                dst_ = bank(n)[:, 0:T]
                for k in range(KD):
                    pe.wait_ge(sem("norm_squares"), KD * i + k + 1)
                    ins = pe.matmul(dst_, ones, hf[:, k, :], start=k == 0, stop=k == KD - 1)
                S.did(ins, "outs")
                return i

            def first_product(dst_, q, ws, i):
                for s_, (a_, b_) in enumerate(((0, 0), (1, 0), (0, 1))):
                    if s_ == 1:
                        low_ready(q)
                    for k in range(KD):
                        if s_ != 1:
                            pe.wait_ge(sem("h_low" if b_ else "h_high"), KD * H_NORMS.index(i) + k + 1)
                        ins_ = pe.matmul(dst_, ws[k][a_], hs[:, b_, k, :], start=s_ == 0 and k == 0,
                                         stop=s_ == 2 and k == KD - 1, skip_group_check=True)
                return ins_

            def groups_of(act_):
                return [(act_[:, 0, k, :], act_[:, 1, k, :]) for k in range(act_.shape[2])]

            hgroups = groups_of(hs)

            def dense(stage, tiles, acts=None, m=P, after_norm=None):
                acts = hgroups if acts is None else acts
                rows = len(acts)
                for t in range(tiles):
                    q, wh, wl = parts_of(stage, t)
                    ws = [(wh[:, k * m:(k + 1) * m], wl[:, k * m:(k + 1) * m]) for k in range(rows)]
                    dst_ = bank(OUT0[stage] + t)[0:m, 0:T]
                    if t == 0 and after_norm is not None:
                        S.did(first_product(dst_, q, ws, after_norm), "outs")
                    else:
                        S.did(three_passes(dst_, q, ws, acts), "outs")

            def dense_tokens(stage, pairs):
                for p_ in range(pairs):
                    for half in range(2):
                        q, wh, wl = parts_of(stage, 2 * p_ + half)
                        ws = [(wh[:, k * 256:(k + 1) * 256], wl[:, k * 256:(k + 1) * 256]) for k in range(4)]
                        for c in range(TT):
                            n_ = OUT0[stage] + 2 * p_ + c
                            acts = [(hs[:, 0, 4 * half + k, c * P:(c + 1) * P],
                                     hs[:, 1, 4 * half + k, c * P:(c + 1) * P]) for k in range(4)]
                            dst_ = (bank(n_) if half == 0 else mm[:, n_ % BANKS, :])[:, 0:T]
                            ins_ = three_passes(dst_, q, ws, acts, first=half == 0, last=half == 1, swap=True)
                            if half == 1:
                                S.did(ins_, "outs")
                        if half == 0:
                            ins_.then_inc(sem("tiles_used"), 1)

            def token_gates(dst_, weights):
                for c in range(TT):
                    ins_ = group(dst_[:, 16 * c:16 * (c + 1)],
                                 [(hs[:, s_, k, c * P:(c + 1) * P].bitcast(F32), weights[:, k, :])
                                  for k in range(KD) for s_ in range(2)])
                return ins_

            def sum_mods(count):
                for _ in range(count):
                    g = mods_summed[0]
                    pe.wait_ge(sem("mod_added"), (KD - 1) * (g + 1))
                    for j in range(KD):
                        ins = pe.matmul(mm[:, MOD_BANK, KD * g + j:KD * g + j + 1],
                                        mod_sums[:, g % MOD_SUMS, j * P:(j + 1) * P], ones[:, 0:1], start=True,
                                        stop=True, skip_group_check=True)
                    ins.then_inc(sem("mods_summed"), 1)
                    mods_summed[0] += 1

            MOD_BANK = 3

            norm(0, False)
            dense("qkv", 12, after_norm=0)
            pe.wait_ge(sem("wsmall_loaded"), 16)
            S.did(token_gates(bank(OUT0["small"]), wsmall), "outs")
            dense("gz", 4)
            dense("mqk", 4)
            dense_tokens("mv", 2)
            dense("mo", 4)
            pe.wait_ge(sem("qk_squares"), 1)
            for j in range(4):
                ins = pe.matmul(ms[:, j, :], ones, scratch[:, j * 512:(j + 1) * 512], start=True, stop=True)
            S.did(ins, "qk_sums")
            dense("gates", 16)

            out_taken(pe, OUT0["gates"] + 15)
            pe.wait_ge(sem("log_decays"), 1)
            for c in range(TT):
                ins = pe.matmul(mm[:, 0, 8 * c:8 * c + 8], upper, lgt[:, c, :], start=True, stop=True,
                                skip_group_check=True)
            pe.matmul(mm[:, 0, 12:16], ones, lgt[:, 0, 4:8], start=False, stop=True, skip_group_check=True)
            ins = pe.matmul(mm[:, 0, 16:20], ones, lgt[:, 0, 0:4], start=True, stop=True, skip_group_check=True)
            S.did(ins, "cum_ready")
            pe.wait_ge(sem("diag_ready"), 1)
            pe.wait_ge(sem("qk_sums_taken"), 1)
            for j in range(2):
                ins = pe.matmul(ms[:, j, :], ones, diag[:, 4 * j:4 * j + 4, :].rearrange("p j t -> p (j t)"), start=True, stop=True)
            S.did(ins, "rows_ready")
            pe.wait_ge(sem("qk_normal"), 1)
            pe.wait_ge(sem("cum_taken"), 1)
            for u in range(8):
                hd, c = u // 2, u % 2
                ins = pe.matmul(mm[:, u // 4, (u % 4) * P:(u % 4 + 1) * P], cv[:, 4 + hd, c * P:(c + 1) * P],
                                cv[:, 4 + hd, c * P:(c + 1) * P], start=True, stop=True, skip_group_check=True)
            S.did(ins, "kk_ready")
            for u in range(8):
                hd, c = u // 2, u % 2
                ins = pe.matmul(ms[:, 2 + u // 4, (u % 4) * P:(u % 4 + 1) * P], cv[:, 4 + hd, c * P:(c + 1) * P],
                                cv[:, hd, c * P:(c + 1) * P], start=True, stop=True, skip_group_check=True)
            S.did(ins, "kq_ready")
            pe.wait_ge(sem("rows_taken"), 1)
            for u in range(8):
                hd, c = u // 2, u % 2
                ins = pe.transpose(ms[:, u // 4, (u % 4) * P:(u % 4 + 1) * P], cv[:, 8 + hd, c * P:(c + 1) * P], ident)
            S.did(ins, "v_turned")
            pe.wait_ge(sem("M_ready"), 1)
            for u in range(8):
                ins = pe.transpose(mm[:, u // 4, (u % 4) * P:(u % 4 + 1) * P], M[:, u, :], ident)
            S.did(ins, "M_turned")
            pe.wait_ge(sem("attnT_ready"), 1)
            for u in range(8):
                hd, c = u % 4, u // 4
                ins = pe.transpose(ms[:, 2 + u // 4, (u % 4) * P:(u % 4 + 1) * P], cv[:, 4 + hd, c * P:(c + 1) * P], ident)
            S.did(ins, "k_turned")
            pe.wait_ge(sem("tokens_ready"), 1)
            for l in range(1, LEVELS):
                for u in range(2):
                    pe.wait_ge(sem("X_ready"), 2 * (l - 1) + u + 1)
                    pe.wait_ge(sem("corner_ready"), l)
                    for i in range(4 * u, 4 * u + 4):
                        ins = pe.matmul(ms[:, u, (i % 4) * P:(i % 4 + 1) * P], Ml[l % 2][:, i, :], X[:, i, :],
                                        start=True, stop=True, skip_group_check=True)
                    S.did(ins, "MX_ready")
                for u in range(2):
                    pe.wait_ge(sem("MX_taken"), 2 * (l - 1) + u + 1)
                    for i in range(4 * u, 4 * u + 4):
                        pe.matmul(ms[:, u, (i % 4) * P:(i % 4 + 1) * P], XT[:, i, :], Pm[:, i, :],
                                  start=True, stop=True, skip_group_check=True)
                        ins = pe.matmul(ms[:, 2 + u, (i % 4) * P:(i % 4 + 1) * P], Pm[:, i, :], XT[:, i, :],
                                        start=True, stop=True, skip_group_check=True)
                    S.did(ins, "XMX_ready")
                if l > 4:
                    sum_mods(1)
            pe.wait_ge(sem("X_ready"), 2 * LEVELS)
            for i in range(4):
                ins = pe.matmul(mm[:, 0, i * P:(i + 1) * P], XT[:, 2 * i, :], vb[:, 2 * i, :], start=True, stop=True,
                                skip_group_check=True)
            S.did(ins, "vn0_ready")
            for i in range(4):
                ins = pe.matmul(mm[:, 1, i * P:(i + 1) * P], kbg[:, i, :], XT[:, 2 * i + 1, :], start=True, stop=True,
                                skip_group_check=True)
            S.did(ins, "w_ready")
            pe.wait_ge(sem("vn0_taken"), 1)
            for i in range(4):
                ins = pe.matmul(mm[:, 2, i * P:(i + 1) * P], kdec[:, i, :], vn[0][:, i, :], start=True, stop=True,
                                skip_group_check=True)
            S.did(ins, "state_ready")
            pe.wait_ge(sem("state_taken"), 1)
            pe.wait_ge(sem("w_taken"), 1)
            for i in range(4):
                ins = group(mm[:, 0, i * P:(i + 1) * P], [(XT[:, 2 * i + 1, :], vb[:, 2 * i + 1, :]),
                                                          (nwT[:, i, :], S1[:, i, :])])
            S.did(ins, "vn1_ready")
            sum_mods(1)
            pe.wait_ge(sem("vn1_taken"), 1)
            for i in range(4):
                dst = ms[:, i // 2, (i % 2) * T:(i % 2) * T + P]
                pe.matmul(dst, vn[0][:, i, :], attnT[:, 2 * i, :], start=True, stop=True, skip_group_check=True)
                dst = ms[:, i // 2, (i % 2) * T + P:(i % 2) * T + 2 * P]
                ins = group(dst, [(vn[1][:, i, :], attnT[:, 2 * i + 1, :]), (S1[:, i, :], grow[:, i, :])])
            S.did(ins, "oa_ready")

            def head_sums(which):
                pe.wait_ge(sem("head_squares"), which + 1)
                for j in range(2):
                    ins = pe.matmul(ms[:, 2 + j, :], ones, scratch[:, j * 512:(j + 1) * 512], start=True, stop=True)
                S.did(ins, "head_sums")

            head_sums(0)
            sum_mods(1)

            pe.wait_ge(sem("diag2_ready"), 1)
            for j in range(2):
                ins = pe.matmul(mm[:, 1 + j, :], ones, diag2[:, 4 * j:4 * j + 4, :].rearrange("p j t -> p (j t)"), start=True, stop=True)
            S.did(ins, "ml_rows_ready")
            pe.wait_ge(sem("oa_done"), 1)
            for i in range(4):
                a, o = i // 2, 64 * (i % 2)
                pe.matmul(ms[:, i, 0:P], mq[o:o + 64, a, 0:P], mk[o:o + 64, a, 0:P], start=True, stop=True,
                          skip_group_check=True)
                ins = pe.matmul(ms[:, i, P:3 * P], mq[o:o + 64, a, P:2 * P], mk[o:o + 64, a, :], start=True, stop=True,
                                skip_group_check=True)
            S.did(ins, "ml_qk_ready")
            sum_mods(1)
            pe.wait_ge(sem("ml_scores"), 1)
            for i in range(4):
                if i == 0:
                    pe.wait_ge(sem("ml_rows_taken"), 1)
                if i == 3:
                    pe.wait_ge(sem("ml_turned"), 1)
                for b in range(3):
                    ins = pe.transpose(mm[:, i % 3, b * P:(b + 1) * P], Em[:, i, b * P:(b + 1) * P], ident)
                S.did(ins, "ml_turn")
            pe.wait_ge(sem("ml_turned"), 4)
            for i in range(4):
                dst = ms[:, i // 2, (i % 2) * T:(i % 2 + 1) * T]
                pe.matmul(dst, mv[:, 0, i * P:(i + 1) * P], ST[:, i, 0:2 * P], start=i % 2 == 0, stop=False,
                          skip_group_check=True)
                ins = pe.matmul(dst[:, P:2 * P], mv[:, 1, i * P:(i + 1) * P], ST[:, i, 2 * P:3 * P], start=False,
                                stop=True, skip_group_check=True)
            S.did(ins, "ob_ready")
            head_sums(1)
            sum_mods(EARLY_MODS - mods_summed[0])

            def branch(stage, acts):
                for t in range(4):
                    q, wh, wl = parts_of(stage, t)
                    for b in range(2):
                        ws = [(wh[:, k * 256 + b * P:k * 256 + (b + 1) * P], wl[:, k * 256 + b * P:k * 256 + (b + 1) * P])
                              for k in range(4)]
                        S.did(three_passes(bank(OUT0[stage] + 2 * t + b)[:, 0:T], q, ws, acts), "outs")

            pe.wait_ge(sem("mods_taken"), 1)
            pe.wait_ge(sem("oa_done"), 2)
            branch("branch_a", groups_of(oas))
            pe.wait_ge(sem("ob_done"), 1)
            branch("branch_b", groups_of(obs))
            pe.wait_ge(sem("mixed"), KD)
            dense("w_out", 8, groups_of(mixs))
            norm(1, False)

            dense("ffn_up", 2 * FFG, after_norm=1)
            pe.wait_ge(sem("ffact_cut"), FFG)
            acts = groups_of(ffs_)
            for m in range(KD):
                dst = bank(OUT0["ffn_down"] + m)[:, 0:T]
                k0 = 0
                for i, rows in enumerate(DOWN):
                    q, wh, wl = parts_of("ffn_down", 3 * m + i)
                    ws = [(wh[:, k * P:(k + 1) * P], wl[:, k * P:(k + 1) * P]) for k in range(rows)]
                    ins = three_passes(dst, q, ws, acts[k0:k0 + rows], first=i == 0, last=i == len(DOWN) - 1)
                    S.did(ins, "outs") if i == len(DOWN) - 1 else ins.then_inc(sem("tiles_used"), 1)
                    k0 += rows
            pe.wait_ge(sem("mod_tiles_added"), 24)
            for i in range(24):
                ins = pe.matmul(ms[:, 0, i:i + 1], last_sums[:, i // KD, i % KD * P:(i % KD + 1) * P], ones[:, 0:1],
                                start=True, stop=True, skip_group_check=True)
            S.did(ins, "last_mod_summed")
            norm(2, False)

            dense("ple_gate", 8, after_norm=2)
            pe.wait_ge(sem("p_loaded"), 16)
            for t in range(2):
                w = slot(TILE0["ple"] + t)
                for b in range(4):
                    S.did(group(bank(OUT0["ple"] + 4 * t + b)[:, 0:T],
                                [(w[:, k * 512 + b * P:k * 512 + (b + 1) * P], pTs[:, k, :]) for k in range(2)]), "outs")
            norm(3, False)
            norm(4, True)

            pe.wait_ge(sem("lru_gates_loaded"), 16)

            def lru_gates(j):
                pe.wait_ge(sem("lru_conv"), j + 1)
                for g, kind in enumerate(("ra", "ri")):
                    S.did(pe.matmul(bank(lru_out_of(kind, j))[0:BLK, 0:T], lgw[0:BLK, j, g, :], lc[0:BLK, j, :],
                                    start=True, stop=True), "outs")

            for j in range(NBLK):
                for b, kind in enumerate(("x", "g")):
                    q, wh, wl = parts_of("lru_in", 2 * j + b)
                    ws = [(wh[:, k * BLK:(k + 1) * BLK], wl[:, k * BLK:(k + 1) * BLK]) for k in range(KD)]
                    dst = bank(lru_out_of(kind, j))[0:BLK, 0:T]
                    if j == 0 and b == 0:
                        S.did(first_product(dst, q, ws, 4), "outs")
                    else:
                        S.did(three_passes(dst, q, ws, hgroups), "outs")
                if j:
                    lru_gates(j - 1)
            lru_gates(NBLK - 1)
            for m in range(KD):
                dst = bank(OUT0["lru_out"] + m)[:, 0:T]
                for half in range(2):
                    if m == 0:
                        pe.wait_ge(sem("lru_y"), 8 * (half + 1))
                    q, wh, wl = parts_of("lru_out", 2 * m + half)
                    ws = [(wh[0:BLK, k * P:(k + 1) * P], wl[0:BLK, k * P:(k + 1) * P]) for k in range(8)]
                    acts = [(ys[0:BLK, 0, 8 * half + k, :], ys[0:BLK, 1, 8 * half + k, :]) for k in range(8)]
                    ins = three_passes(dst, q, ws, acts, first=half == 0, last=half == 1)
                    S.did(ins, "outs") if half == 1 else ins.then_inc(sem("tiles_used"), 1)

            def experts(L):
                norm(5 + 2 * L, True)
                dense(f"peer{L}_q", 16, after_norm=5 + 2 * L)
                w = [slot(TILE0[f"peer{L}_keys"] + i) for i in range(2)]
                out_taken(pe, OUT0[f"peer{L}_q"] + 15)
                for c in range(TT):
                    for g in range(4):
                        n = OUT0[f"peer{L}_scores"] + 4 * c + g
                        dst = bank(n)
                        for j in range(4 * g, 4 * g + 4):
                            ins = pe.matmul(dst[:, (j % 4) * P:(j % 4 + 1) * P], eq[:, j, c * P:(c + 1) * P],
                                            w[j // 8][:, (j % 8) * P:(j % 8 + 1) * P], start=True, stop=True,
                                            skip_group_check=True)
                        S.did(ins, "outs")
                q0 = CUT0[f"peer{L}_experts"]
                body = 2 * UNROLL

                def products(dsts, i, r, acts_of, first):
                    q = (q0 + i) % CUT
                    pe.wait_ge(sem("high_done"), r * body + (q0 + i + 1))
                    for s_, (a_, b_) in enumerate(((0, 0), (0, 1), (1, 0))):
                        if s_ == 2:
                            pe.wait_ge(sem("low_done"), r * body + (q0 + i + 1))
                        w_ = (high, low)[a_][:, q, :]
                        for k in range(KD):
                            ins_ = pe.matmul(dsts[k], w_[:, k * P:(k + 1) * P], acts_of(b_, k),
                                             start=first(k) and s_ == 0, stop=False, skip_group_check=True)
                    return ins_

                def hidden(s_, i, r, steps, first=False):
                    if not first:
                        pe.wait_ge(sem("hidden_taken"), r * steps + (KEYS * L + s_ - 3 + 1))
                    products([mm[:, s_ % 3, 0:T]] * KD, i, r, lambda b_, k: hs[:, b_, k, :],
                             lambda k: k == 0).then_inc(sem("hidden_ready"), 1)

                def values(s_, i, r, steps, first=False):
                    pe.wait_ge(sem("weighted"), r * steps + (KEYS * L + s_ + 1))
                    products([ms[:, m // 2, (m % 2) * T:(m % 2 + 1) * T] for m in range(KD)], i, r,
                             lambda b_, k: wts[:, s_ % 3, b_, :],
                             lambda k: first and k % 2 == 0).then_inc(sem("tiles_used"), 1)

                for j in range(4):
                    out_taken(pe, OUT0[f"peer{L}_scores"] + 4 + j)
                for j in range(body):
                    hidden(j, j, 0, 0, first=j < 3)
                with pe.Fori(1, EARLY // body) as r:
                    for j in range(body):
                        hidden(j, j, r, body)

                pe.wait_ge(sem("hidden_taken"), KEYS * L + EARLY)
                for c in range(TT):
                    dst = bank(OUT0[f"peer{L}_turn"] + c)
                    pe.wait_ge(sem("routed"), TT * L + c + 1)
                    for s in range(3):
                        ins = pe.transpose(dst[:, s * P:(s + 1) * P], route[:, c, s, :], ident)
                    S.did(ins, "outs")
                n0 = OUT0[f"peer{L}_place"]

                def place(n, wait_taken, wait_hot, b):
                    pe.wait_ge(sem(taken(n)[0]), wait_taken)
                    pe.wait_ge(sem("onehots"), wait_hot)
                    for i in range(4):
                        ins = pe.matmul(mm[:, n % BANKS, i * P:(i + 1) * P], onehot[:, b, 0, i, :],
                                        onehot[:, b, 1, i, :], start=True, stop=True, skip_group_check=True)
                    ins.then_inc(sem("outs"), 1)

                with pe.Fori(0, T // 16) as r:
                    for j in range(4):
                        place(n0 + j, r + (n0 + j) // BANKS, r * 4 + (T // 4 * L + j + 1), j % 2)
                for j in range(4):
                    out_taken(pe, n0 + T // 4 - 4 + j)

                for j in range(body):
                    values(j, EARLY + j, 0, 0, first=j == 0)
                with pe.Fori(1, EARLY // body) as r:
                    for j in range(body):
                        values(j, EARLY + j, r, body)

                def step(j, r, first=False):
                    hidden(EARLY + j, 2 * EARLY + (j if first and j < LAG else 2 * j - LAG), r, UNROLL)
                    if not (first and j < LAG):
                        values(EARLY + j - LAG, 2 * EARLY + 2 * j - LAG + 1, r, UNROLL)

                for j in range(UNROLL):
                    step(j, 0, True)
                last = (KEYS - EARLY) // UNROLL
                with pe.Fori(1, last) as r:
                    for j in range(UNROLL):
                        step(j, r)
                for j in range(KEYS - EARLY - last * UNROLL):
                    step(j, last)
                for s_ in range(KEYS - LAG, KEYS):
                    values(s_, KEYS + s_, 0, 0)

            experts(0)

            norm(6, True)
            dense("fox_q", 8, after_norm=6)
            pe.wait_ge(sem("wfox_loaded"), 16)
            S.did(token_gates(bank(OUT0["fox_small"]), wfox), "outs")
            dense("fox_k", 8)
            pe.wait_ge(sem("fox_logf"), 1)
            dst = bank(OUT0["fox_cum"])
            group(dst[:, 0:16], [(upper, ffs[:, 0, :])])
            ins = group(dst[:, 16:32], [(upper, ffs[:, 1, :]), (ones, ffs[:, 0, :])])
            S.did(ins, "outs")
            dense_tokens("fox_v", 4)
            for j in range(8):
                n = OUT0["fox_squares"] + j
                pe.wait_ge(sem("fox_sq"), j // 4 + 1)
                S.did(pe.matmul(bank(n), heads64, fsq[:, j * 512:(j + 1) * 512], start=True, stop=True), "outs")
            dense("fox_og", 8)
            pe.wait_ge(sem("fox_diag"), 1)
            pe.wait_ge(sem("fox_normal"), 2)
            for kind, hd in fox_order():
                a, o = hd // 2, 64 * (hd % 2)
                if kind == "scores":
                    dst = bank(OUT0[f"fox_scores{hd}"])
                    group(dst[:, 0:P], [(fq3[o:o + 64, a, 0:P], fk3[o:o + 64, a, 0:P]), (ones, fd[:, hd, 0, :])])
                    ins = group(dst[:, P:3 * P], [(fq3[o:o + 64, a, P:2 * P], fk3[o:o + 64, a, :]),
                                                  (ones, fd[:, hd, :, :].rearrange("p c t -> p (c t)"))])
                    S.did(ins, "outs")
                elif kind == "turn":
                    dst = bank(OUT0[f"fox_turn{hd}"])
                    pe.wait_ge(sem("fox_probs"), hd + 1)
                    for b in range(3):
                        ins = pe.transpose(dst[:, b * P:(b + 1) * P], fP[:, hd % 3, b * P:(b + 1) * P], ident)
                    S.did(ins, "outs")
                else:
                    out_taken(pe, OUT0[f"fox_turn{hd}"])
                    if a >= 4:
                        pe.wait_ge(sem("fox_y"), a - 3)
                    dst = ms[o:o + 64, a % 4, 0:T]
                    pe.matmul(dst, fv[:, 0, hd * FE:(hd + 1) * FE], fPT[:, hd % 3, 0:2 * P], start=True, stop=False,
                              skip_group_check=True)
                    S.did(pe.matmul(dst[:, P:2 * P], fv[:, 1, hd * FE:(hd + 1) * FE], fPT[:, hd % 3, 2 * P:3 * P],
                                    start=False, stop=True, skip_group_check=True), "fox_pv")
            pe.wait_ge(sem("fox_y"), KD)
            dense("fox_out", 8, groups_of(fys))
            experts(1)

        @block.scalar
        def _(act):
            S = Steps(act, sem, "act_step")
            def squares(i, stage=None):
                if i == 0:
                    act.wait_ge(sem("x_loaded"), 16)
                else:
                    out_ready(act, OUT0[f"norm{i - 1}"])
                    if stage is None:
                        act.wait_ge(sem("x_done"), i)
                for k in range(KD):
                    if stage is not None:
                        out_taken(act, OUT0[stage] + k)
                    S.did(act.activation(hf[:, k, :], x[:, k, :], ACT.Square), "norm_squares")

            def root(i):
                act.wait_ge(sem("norm_inverse"), i + 1)
                S.did(act.activation(rstd[:, :], rstd[:, :], ACT.Sqrt), "norm_rstd")

            def high_parts(i):
                for k in range(KD):
                    act.wait_ge(sem("h_scaled"), KD * H_NORMS.index(i) + k + 1)
                    if i <= 2:
                        ins = act.activation(hs[:, 0, k, :], hf[:, k, :], ACT.Copy)
                    else:
                        m = (i - 4) * 24 + k
                        ins = act.activation(hs[:, 0, k, :], hf[:, k, :], ACT.Identity, bias=mod[:, m:m + 1])
                    S.did(ins, "h_high")

            cuts_made = [0]

            def ahead(stage, t, more=CUT - 1):
                end = min(CUT0[stage] + t + more, RUN_END[stage])
                while cuts_made[0] <= end:
                    q = cuts_made[0]
                    name, i = CUTS[q]
                    n_ = TILE_AT[name, i]
                    tile_ready(act, n_)
                    if q >= CUT:
                        what, value = cut_free(q - CUT)
                        act.wait_ge(sem(what), value)
                    rows, width = tile_shape(name, i)
                    act.activation(high[0:rows, q % CUT, 0:width], ring[0:rows, n_ % RAW, 0:width], ACT.Copy) \
                        .then_inc(sem("high_done"), 1)
                    cuts_made[0] += 1

            def evacuate(n, dst, func=ACT.Copy, m=P, width=T):
                out_ready(act, n)
                src = mm[0:m, n % BANKS, 0:width]
                if len(dst.shape) == 3:
                    src = src.rearrange("p (j n) -> p j n", n=P)
                S.did(act.activation(dst, src, func), taken(n))

            squares(0)
            ahead("qkv", 0)
            root(0)
            high_parts(0)
            act.wait_ge(sem("vec_loaded"), 16)
            S.did(act.activation(expa, v("a_log"), ACT.Exp), "expa_ready")
            act.wait_ge(sem("pad_zero"), 1)
            for j in range(13):
                if j < 12:
                    ahead("qkv", j)
                    evacuate(OUT0["qkv"] + j, cin[:, j, 3:T + 3])
                if j:
                    act.wait_ge(sem("conv_done"), j)
                    S.did(act.activation(cv[:, j - 1, :], cv[:, j - 1, :], ACT.Silu), "qkv_active")
            for j in range(4):
                ahead("gz", j)
                evacuate(OUT0["gz"] + j, gz[:, j, :], ACT.Silu)
            for j in range(4):
                ahead("mqk", j)
                evacuate(OUT0["mqk"] + j, (mq if j < 2 else mk)[:, j % 2, :])
            act.wait_ge(sem("pre_ready"), 1)
            S.did(act.activation(beta, pre[:, :, 0:4], ACT.Sigmoid), "beta_ready")
            S.did(act.activation(csilu[:, :], v("c"), ACT.Silu), "csilu_ready")
            act.wait_ge(sem("nz_ready"), 1)
            S.did(act.activation(en, nz, ACT.Exp))
            S.settle()
            S.did(act.activation(ln, en, ACT.Ln, bias=1.0), "ln_ready")
            for j in range(4):
                ahead("mv", j // 2 * 2 + 1)
                evacuate(OUT0["mv"] + j, mv[:, j % 2, (j // 2) * T:(j // 2 + 1) * T])
            for j in range(4):
                ahead("mo", j)
                evacuate(OUT0["mo"] + j, mo[:, j, :], ACT.Sigmoid)
            for j in range(16):
                ahead("gates", j)
                evacuate(OUT0["gates"] + j, gates[:, j, :], ACT.Sigmoid)
            mods_scaled = [0]

            def scale_mods(count):
                for _ in range(min(count, KD * EARLY_MODS - mods_scaled[0])):
                    i = mods_scaled[0]
                    g, k = i // KD, i % KD
                    tile_ready(act, TILE0["mod"] + i)
                    if i == 0:
                        act.wait_ge(sem("csilu_ready"), 1)
                        out_ready(act, OUT0["gates"] + 15)
                    if k == 0:
                        if g >= MOD_SUMS:
                            act.wait_ge(sem("mods_summed"), g - MOD_SUMS + 1)
                        dst = mod_sums[:, g % MOD_SUMS, :]
                    else:
                        n_ = (KD - 1) * g + k - 1
                        if n_ >= SCALED:
                            act.wait_ge(sem("mod_added"), n_ - SCALED + 1)
                        dst = scaled[:, n_ % SCALED, :]
                    act.activation(dst, ring[:, (TILE0["mod"] + i) % RAW, :], ACT.Copy, scale=csilu[:, k:k + 1]) \
                        .then_inc(sem("mod_scaled"), 1)
                    mods_scaled[0] += 1

            act.wait_ge(sem("qk_inverse"), 1)
            S.did(act.activation(scratch[:, :], scratch[:, :], ACT.Sqrt), "qk_rstd")
            scale_mods(4)
            act.wait_ge(sem("gdif_ready"), 1)
            act.activation(ecum, cum[:, 1, 0:4], ACT.Exp)
            S.did(act.activation(ekd, gdif, ACT.Exp), "column_decays")
            act.wait_ge(sem("decay_logs"), 1)
            S.did(act.activation(decay, decay, ACT.Exp), "decay_ready")
            S.did(act.activation(decayT, decayT, ACT.Exp, scale=-1.0), "decay_ready")
            act.wait_ge(sem("rows_ready"), 1)
            for i in range(4):
                u = 2 * i + 1
                ins = act.activation(grow[:, i, :], ms[:, u // 4, (u % 4) * P:(u % 4 + 1) * P], ACT.Exp, scale=-1.0)
            S.did(ins, "grow_ready")
            scale_mods(40)
            act.wait_ge(sem("oa_ready"), 1)
            halves = ms[:, 0:2, :].rearrange("p b n -> p (b n)")
            act.activation(oa.rearrange("p j t -> p (j t)"), halves, ACT.Copy)
            S.did(act.activation(scratch[:, 0:1024], halves, ACT.Square), "head_squares")
            scale_mods(6)
            act.wait_ge(sem("head_inverse"), 1)
            S.did(act.activation(scratch[:, 1024:2048], scratch[:, 1024:2048], ACT.Sqrt), "head_rstd")
            scale_mods(8)
            act.wait_ge(sem("ml_nm"), 1)
            act.activation(flo, nm, ACT.Exp)
            for i in range(4):
                act.activation(Em[:, i, 0:P], Dlog[:, i, 0:P], ACT.Exp, bias=nm[:, 0, i:i + 1])
                ins = act.activation(Em[:, i, P:3 * P], Dlog[:, i, P:3 * P], ACT.Exp, bias=nm[:, 1, i:i + 1])
            S.did(ins, "ml_weights")
            scale_mods(8)
            for i in range(4):
                act.wait_ge(sem("ml_turn"), i + 1)
                S.did(act.activation(ST[:, i, :], mm[:, i % 3, 0:384], ACT.Copy), "ml_turned")
            act.wait_ge(sem("ob_ready"), 1)
            act.activation(ob.rearrange("p j t -> p (j t)"), halves, ACT.Copy)
            S.did(act.activation(scratch[:, 0:1024], halves, ACT.Square), "head_squares")
            scale_mods(4)
            act.wait_ge(sem("head_inverse"), 2)
            S.did(act.activation(scratch[:, 1024:2048], scratch[:, 1024:2048], ACT.Sqrt), "head_rstd")
            scale_mods(24 * MODS)
            act.wait_ge(sem("mod_added"), EARLY_MODS * (KD - 1))
            ahead("ffn_up", 0)
            act.wait_ge(sem("x_done"), 1)
            act.dma_start(pTs, pT).then_inc(sem("p_loaded"), 16)
            squares(1, "w_out")
            root(1)
            high_parts(1)
            for j in range(FFG):
                ahead("ffn_up", 2 * j)
                if j >= 2:
                    out_taken(act, OUT0["ffn_up"] + 2 * (j - 2) + 1)
                evacuate(OUT0["ffn_up"] + 2 * j, up[:, j % 2, :], ACT.Silu)
            ahead("ple_gate", 0)
            squares(2, "ffn_down")
            root(2)
            high_parts(2)
            for j in range(KD):
                ahead("ple_gate", j)
                evacuate(OUT0["ple_gate"] + j, pleg[:, j, :], ACT.Sigmoid)
            squares(3)
            root(3)
            ahead("lru_in", 0)
            act.wait_ge(sem("x_done"), 3)
            act.dma_start(lgw[0:96], lru_gate_w).then_inc(sem("lru_gates_loaded"), 16)
            act.wait_ge(sem("nlam_ready"), 1)
            S.did(act.activation(lruc[:, 1, :], lruc[:, 0, :], ACT.Exp), "lam_exp")
            squares(4)
            root(4)
            high_parts(4)
            act.wait_ge(sem("lru_pad_zero"), 1)

            def lru_act(j):
                n = lru_out_of("ra", j)
                out_ready(act, n)
                S.did(act.activation(lr[0:BLK, j, :], mm[0:BLK, n % BANKS, 0:T], ACT.Sigmoid,
                                     bias=v("ra_b", j, j + 1, BLK)), taken(n))
                n = lru_out_of("ri", j)
                out_ready(act, n)
                S.did(act.activation(li[0:BLK, j, :], mm[0:BLK, n % BANKS, 0:T], ACT.Sigmoid,
                                     bias=v("ri_b", j, j + 1, BLK)), taken(n))
                out_taken(act, lru_out_of("ra", j))
                S.did(act.activation(lt[0:BLK, j, :], lr[0:BLK, j, :], ACT.Tanh,
                                     scale=lruc[0:BLK, 5, j:j + 1]), "lru_tanh")

            act.wait_ge(sem("lru_rate"), 1)
            for j in range(NBLK):
                ahead("lru_in", 2 * j)
                evacuate(lru_out_of("x", j), lx[0:BLK, j, 3:T + 3], m=BLK)
                ahead("lru_in", 2 * j + 1)
                evacuate(lru_out_of("g", j), lg[0:BLK, j, :], m=BLK)
                if j:
                    lru_act(j - 1)
            lru_act(NBLK - 1)
            ahead("lru_out", 0)
            for j in range(0, NBLK, 4):
                if j == 0:
                    out_taken(act, lru_out_of("g", NBLK - 1))
                    S.did(act.activation(lg[0:BLK], lg[0:BLK], ACT.Gelu), "lru_gelu")
                act.wait_ge(sem("lru_t_read"), j + 4)
                S.did(act.activation(lt[0:BLK, j:j + 4, :], lt[0:BLK, j:j + 4, :], ACT.Sqrt), "lru_root")
            for j in range(NBLK):
                act.wait_ge(sem("lru_product"), j + 1)
                S.did(act.activation(ys[0:BLK, 0, j, :], lt[0:BLK, j, :], ACT.Copy), "lru_high")

            def experts(L):
                ahead(f"peer{L}_q", 0)
                squares(5 + 2 * L, "fox_out" if L else "lru_out")
                root(5 + 2 * L)
                high_parts(5 + 2 * L)
                for j in range(16):
                    ahead(f"peer{L}_q", j)
                    evacuate(OUT0[f"peer{L}_q"] + j, eq[:, j, :])
                for c in range(TT):
                    for g in range(4):
                        evacuate(OUT0[f"peer{L}_scores"] + 4 * c + g, es[:, c, 4 * g:4 * g + 4, :], width=512)
                ahead(f"peer{L}_experts", 0)
                q0, t0 = CUT0[f"peer{L}_experts"], TILE0[f"peer{L}_experts"]
                body = 2 * UNROLL

                def cut_high(i, r, used=None):
                    act.wait_ge(sem(f"slot{(t0 + i) % RAW}_loaded"), r * (16 * body // RAW) + 16 * ((t0 + i) // RAW + 1))
                    if used is not None:
                        act.wait_ge(sem(used[0]), used[1])
                    act.activation(high[:, (q0 + i) % CUT, :], ring[:, (t0 + i) % RAW, :], ACT.Copy) \
                        .then_inc(sem("high_done"), 1)

                def early(j, r):
                    act.wait_ge(sem("hidden_ready"), r * body + (KEYS * L + j + 1))
                    dst = placed[:, bass.ds(r * body + j, 1), :]
                    act.activation(dst.rearrange("p e t -> p (e t)"), mm[:, j % 3, 0:T], ACT.Gelu) \
                        .then_inc(sem("hidden_taken"), 1)
                    cut_high(j + CUT, r)

                for part_ in range(TT):
                    with act.Fori(*((0, EARLY // body - 1) if part_ == 0 else (EARLY // body - 1, EARLY // body))) as r:
                        for j in range(body):
                            early(j, r)
                    act.wait_ge(sem("best_shifted"), TT * L + part_ + 1)
                    S.did(act.activation(expo[:, part_], shifted[:, part_], ACT.Exp), "best_exp")
                for c in range(TT):
                    n = OUT0[f"peer{L}_turn"] + c
                    evacuate(n, routeT[:, :, c * P:(c + 1) * P], width=384)
                n0 = OUT0[f"peer{L}_place"]
                def place(r, j):
                    act.wait_ge(sem("outs"), r * 4 + (n0 + j + 1))
                    dst = placed[:, EARLY:KEYS, bass.ds(r * 16 + 4 * j, 4)].rearrange("p e t -> p t e")
                    src = mm[:, (n0 + j) % BANKS, :].rearrange("p (t e) -> p t e", t=4)
                    act.activation(dst, src[:, :, EARLY:KEYS], ACT.Copy).then_inc(sem("place_copied"), 1)

                with act.Fori(0, T // 16) as r:
                    for j in range(4):
                        place(r, j)
                with act.Fori(0, EARLY // body) as r:
                    for j in range(body):
                        cut_high(EARLY + j + CUT, r, ("tiles_used", r * body + (USED0[f"peer{L}_experts"] + j + 1)))

                def gelu(j, r):
                    act.wait_ge(sem("hidden_ready"), r * UNROLL + (KEYS * L + EARLY + j + 1))
                    act.wait_ge(sem("weighted"), r * UNROLL + (KEYS * L + EARLY + j - 3 + 1))
                    act.activation(mix[:, j % 3, :], mm[:, j % 3, 0:T], ACT.Gelu).then_inc(sem("hidden_taken"), 1)

                def two_highs(j, r):
                    for i in (2 * j + 1, 2 * j + 2):
                        if isinstance(r, int) and r * body + i >= 2 * (KEYS - EARLY):
                            continue
                        what, value = cut_free(q0 + 2 * EARLY + i + body - CUT)
                        if isinstance(r, int) and r == 0:
                            what, value = cut_free(q0 + 2 * EARLY + i - CUT)
                        elif isinstance(r, int):
                            what, value = cut_free(q0 + 2 * EARLY + r * body + i - CUT)
                        else:
                            value = r * UNROLL + (value - UNROLL)
                        cut_high(2 * EARLY + i, r, (what, value))

                for j in range(UNROLL):
                    gelu(j, 0)
                    if j == 0:
                        cut_high(2 * EARLY + 3, 0)
                    elif j == 1:
                        cut_high(2 * EARLY + 4, 0)
                    else:
                        two_highs(j, 0)
                last = (KEYS - EARLY) // UNROLL
                with act.Fori(1, last) as r:
                    for j in range(UNROLL):
                        gelu(j, r)
                        two_highs(j, r)
                for j in range(KEYS - EARLY - last * UNROLL):
                    gelu(j, last)
                    two_highs(j, last)
                cuts_made[0] = q0 + 2 * KEYS

            experts(0)

            ahead("fox_q", 0)
            squares(6)
            root(6)
            high_parts(6)
            for j in range(8):
                ahead("fox_q", j)
                evacuate(OUT0["fox_q"] + j, fq3[:, j, :])
            act.wait_ge(sem("fox_nz"), 1)
            S.did(act.activation(ffe, ffn_, ACT.Exp))
            S.settle()
            S.did(act.activation(ffl, ffe, ACT.Ln, bias=1.0), "fox_ln")
            for j in range(8):
                ahead("fox_k", j)
                evacuate(OUT0["fox_k"] + j, fk3[:, j, :])
            for j in range(8):
                ahead("fox_v", j // 2 * 2 + 1)
                evacuate(OUT0["fox_v"] + j, fv[:, j % 2, (j // 2) * T:(j // 2 + 1) * T])
            for j in range(8):
                ahead("fox_og", j)
                evacuate(OUT0["fox_og"] + j, fo[:, j, :], ACT.Sigmoid)
            for j in range(2):
                act.wait_ge(sem("fox_inverse"), j + 1)
                S.did(act.activation(fsq[:, j * 2048:(j + 1) * 2048], fsq[:, j * 2048:(j + 1) * 2048], ACT.Sqrt),
                      "fox_rstd")
            for i in range(FH + 2):
                if i < FH:
                    act.wait_ge(sem("fox_max"), i + 1)
                    if i >= 3:
                        out_ready(act, OUT0[f"fox_turn{i - 3}"])
                    b = i % 3
                    act.activation(fP[:, b, 0:P], fL[:, b, 0:P], ACT.Exp, bias=fnm[:, b, 0:1],
                                   accum_out=fsum[:, b, 0:1])
                    S.did(act.activation(fP[:, b, P:3 * P], fL[:, b, P:3 * P], ACT.Exp, bias=fnm[:, b, 1:2],
                                         accum_out=fsum[:, b, 1:2]), "fox_exp")
                if i >= 2:
                    hd = i - 2
                    if hd >= 3:
                        act.wait_ge(sem("fox_pv"), hd - 2)
                    evacuate(OUT0[f"fox_turn{hd}"], fPT[:, hd % 3, :], width=384)
            experts(1)

        @block.gpsimd
        def _(pool):
            def cut_low(rows, width, raw_slot, cut_slot):
                pool.tensor_tensor(low[0:rows, cut_slot, 0:width], ring[0:rows, raw_slot, 0:width],
                                   high[0:rows, cut_slot, 0:width].bitcast(F32), ALU.subtract) \
                    .then_inc(sem("low_done"), 1)

            def cut_one(name, i):
                q, n = CUT0[name] + i, TILE_AT[name, i]
                pool.wait_ge(sem("high_done"), q + 1)
                cut_low(*tile_shape(name, i), n % RAW, q % CUT)

            def second_onehots(L):
                for c in range(TT):
                    out_taken(pool, OUT0[f"peer{L}_turn"] + c)
                n0 = OUT0[f"peer{L}_place"]
                with pool.Fori(0, T // 16) as r:
                    for j in range(4):
                        pool.wait_ge(sem("outs"), r * 4 + (n0 + j - 2 + 1))
                        keys = routeT[:, 1, bass.ds(r * 16 + 4 * j, 4)]
                        pool.tensor_tensor(onehot[:, j % 2, 1, :, :], iota.unsqueeze(1).to_broadcast([P, 4, P]),
                                           keys.unsqueeze(2).to_broadcast([P, 4, P]), ALU.subtract) \
                            .then_inc(sem("key_distances"), 1)

            def add_mods():
                for n_ in range(EARLY_MODS * (KD - 1)):
                    g, k = n_ // (KD - 1), n_ % (KD - 1) + 1
                    pool.wait_ge(sem("mod_scaled"), KD * g + k + 1)
                    if k > 1:
                        pool.wait_ge(sem("mod_added"), n_)
                    sums_ = mod_sums[:, g % MOD_SUMS, :]
                    pool.tensor_tensor(sums_, sums_, scaled[:, n_ % SCALED, :], ALU.add).then_inc(sem("mod_added"), 1)

            for name, count, _, _, is_cut in STREAM:
                if name == "mod":
                    add_mods()
                if not is_cut:
                    continue
                if not name.endswith("experts"):
                    for i in range(count):
                        cut_one(name, i)
                    continue
                q0, t0, body = CUT0[name], TILE0[name], 2 * UNROLL

                def loop(first, last):
                    with pool.Fori(first, last) as r:
                        for i in range(body):
                            pool.wait_ge(sem("high_done"), r * body + (q0 + i + 1))
                            cut_low(P, SLOT, (t0 + i) % RAW, (q0 + i) % CUT)

                loop(0, EARLY // body)
                for i in range(EARLY, EARLY + CUT):
                    cut_one(name, i)
                second_onehots(int(name[4]))
                for i in range(EARLY + CUT, EARLY + body):
                    cut_one(name, i)
                loop(EARLY // body + 1, count // body)
                for i in range(count // body * body, count):
                    cut_one(name, i)

        @block.vector
        def _(dve):
            S = Steps(dve, sem, "dve_step")

            def tt(out_, a, b, op, name=None):
                S.did(dve.tensor_tensor(out_, a, b, op), name)

            def ts(out_, a, s1, s2, op0, op1=None, name=None):
                S.did(dve.tensor_scalar(out_, a, s1, s2, op0, *([op1] if op1 is not None else [])), name)

            def stt(out_, a, s, b, op0, op1, name=None, **kw):
                S.did(dve.scalar_tensor_tensor(out=out_, in0=a, scalar=s, in1=b, op0=op0, op1=op1, **kw), name)

            def bank(n, m=P, width=T):
                out_ready(dve, n)
                return mm[0:m, n % BANKS, 0:width]

            def norm(i, gain):
                n = OUT0[f"norm{i}"]
                src = bank(n)
                if i >= 1:
                    S.settle()
                ts(rstd[:, :], src, 1.0 / D, EPS, ALU.mult, ALU.add, taken(n))
                S.settle()
                S.did(dve.reciprocal(rstd[:, :], rstd[:, :]), "norm_inverse")
                dve.wait_ge(sem("norm_rstd"), i + 1)
                if i == 0:
                    dve.wait_ge(sem("vec_loaded"), 16)
                for k in range(KD):
                    dst, name = (x, "x_done" if k == KD - 1 else None) if i == 3 else (hf, "h_scaled")
                    stt(dst[:, k, :], x[:, k, :], gain[:, k:k + 1], rstd[:, :], ALU.mult, ALU.mult, name)
                if i == 3:
                    return
                for k in range(KD):
                    dve.wait_ge(sem("h_high"), KD * H_NORMS.index(i) + k + 1)
                    if k == 0:
                        S.settle()
                    hi_ = hs[:, 0, k, :].bitcast(F32)
                    if i <= 2:
                        tt(hs[:, 1, k, :], hf[:, k, :], hi_, ALU.subtract, "h_low")
                    else:
                        m = (i - 4) * 24 + k
                        stt(hs[:, 1, k, :], hf[:, k, :], mod[:, m:m + 1], hi_, ALU.add, ALU.subtract, "h_low")

            def cut_parts(high_, low_, src, name=None):
                S.settle()
                S.did(dve.tensor_copy(high_, src))
                S.settle()
                tt(low_, src, high_.bitcast(F32), ALU.subtract, name)

            S.did(dve.memset(cin[:, :, 0:3], 0.0), "pad_zero")
            norm(0, v("g_mix"))

            for j in range(12):
                out_taken(dve, OUT0["qkv"] + j)
                w = v("conv", 4 * j, 4 * j + 4)
                ts(cv[:, j, :], cin[:, j, 0:T], w[:, 0:1], None, ALU.mult)
                for s in range(1, 4):
                    S.settle()
                    stt(cv[:, j, :], cin[:, j, s:s + T], w[:, s:s + 1], cv[:, j, :], ALU.mult, ALU.add,
                        "conv_done" if s == 3 else None)

            n = OUT0["small"]
            src = bank(n, width=32).rearrange("p (c j) -> p c j", c=TT)
            tt(pre, src, v("gate_bias").unsqueeze(1).to_broadcast([P, TT, 16]), ALU.add, taken(n))
            S.settle()
            S.did(dve.tensor_copy(zz[:, :, 0:4], pre[:, :, 4:8]), "pre_ready")
            ts(zz[:, :, 4:8], pre[:, :, 12:16], -1.0, None, ALU.mult)
            S.settle()
            ts(nz, zz, -1.0, None, ALU.mult)
            S.settle()
            tt(nz, nz, zz, ALU.min, "nz_ready")
            ts(sp, zz, 0.0, None, ALU.max)
            dve.wait_ge(sem("ln_ready"), 1)
            S.settle()
            tt(sp, sp, ln, ALU.add)
            S.settle()
            ts(lgt, sp, -1.0, None, ALU.mult)
            S.settle()
            dve.wait_ge(sem("expa_ready"), 1)
            tt(lgt[:, :, 0:4], lgt[:, :, 0:4], expa.unsqueeze(1).to_broadcast([P, TT, 4]), ALU.mult, "log_decays")

            dve.wait_ge(sem("qkv_active"), 8)
            out_ready(dve, OUT0["norm0"])
            qk = cv[:, 0:8, :].rearrange("p j t -> p (j t)")
            tt(scratch[:, :], qk, qk, ALU.mult, "qk_squares")
            dve.wait_ge(sem("qk_sums"), 1)
            S.settle()
            ts(scratch[:, :], ms[:, :, :].rearrange("p b n -> p (b n)"), EPS, None, ALU.add, None, "qk_sums_taken")
            S.settle()
            S.did(dve.reciprocal(scratch[:, :], scratch[:, :]), "qk_inverse")
            dve.wait_ge(sem("cum_ready"), 1)
            S.did(dve.tensor_copy(cum, mm[:, 0, 0:16].rearrange("p (c j) -> p c j", c=TT)))
            S.did(dve.tensor_copy(gl, mm[:, 0, 16:20]), "cum_taken")
            S.settle()
            tt(gdif, gl, cum[:, 0, 0:4], ALU.subtract, "gdif_ready")
            ts(ngc, cum[:, :, 0:4], -1.0, None, ALU.mult)
            tt(imb, pre[:, :, 8:12], cum[:, :, 4:8], ALU.subtract)
            S.settle()
            for u in range(8):
                ts(diag[:, u, :], ident, ngc[:, u % 2, u // 2:u // 2 + 1], None, ALU.mult, None,
                   "diag_ready" if u == 7 else None)
            dve.wait_ge(sem("qk_rstd"), 1)
            stt(qk[:, 0:1024], qk[:, 0:1024], float(P) ** -0.5, scratch[:, 0:1024], ALU.mult, ALU.mult)
            tt(qk[:, 1024:2048], qk[:, 1024:2048], scratch[:, 1024:2048], ALU.mult, "qk_normal")
            dve.wait_ge(sem("rows_ready"), 1)
            dve.wait_ge(sem("masks_loaded"), 16)
            for u in range(8):
                r = ms[:, u // 4, (u % 4) * P:(u % 4 + 1) * P]
                g = cum[:, u % 2, u // 2:u // 2 + 1]
                stt(decay[:, u, :], r, g, cst("mask")[:, P:2 * P], ALU.add, ALU.add)
                stt(decayT[:, u, :], r, g, cst("maskT"), ALU.add, ALU.add, "decay_logs" if u == 7 else None)
            dve.wait_ge(sem("grow_ready"), 1)
            tt(grow, grow, cv[:, 0:4, P:T], ALU.mult, "rows_taken")
            dve.wait_ge(sem("decay_ready"), 2)
            dve.wait_ge(sem("kk_ready"), 1)
            dve.wait_ge(sem("beta_ready"), 1)
            for u in range(8):
                stt(M[:, u, :], mm[:, u // 4, (u % 4) * P:(u % 4 + 1) * P], beta[:, u % 2, u // 2:u // 2 + 1],
                    decay[:, u, :], ALU.mult, ALU.mult, "M_ready" if u == 7 else None)
            dve.wait_ge(sem("kq_ready"), 1)
            tt(attnT, ms[:, 2:4, :].rearrange("p b (j t) -> p (b j) t", j=4), decayT, ALU.mult, "attnT_ready")

            def level_mask(l):
                return cst("levelsT")[:, l * P:(l + 1) * P].unsqueeze(1).to_broadcast([P, 8, P])

            identb = ident.unsqueeze(1).to_broadcast([P, 8, P])
            S.settle()
            tt(Pm, M, cst("level0").unsqueeze(1).to_broadcast([P, 8, P]), ALU.mult)
            S.settle()
            tt(X, identb, Pm, ALU.subtract)
            dve.wait_ge(sem("M_turned"), 1)
            S.did(dve.tensor_copy(MT, mm[:, 0:2, :].rearrange("p b (j t) -> p (b j) t", j=4)))
            S.settle()
            tt(Ml[0], MT, level_mask(0), ALU.mult)
            tt(Ml[1], MT, level_mask(1), ALU.mult, "corner_ready")
            dve.wait_ge(sem("v_turned"), 1)
            for u in range(8):
                ts(vb[:, u, :], ms[:, u // 4, (u % 4) * P:(u % 4 + 1) * P], beta[:, u % 2, u // 2:u // 2 + 1], None,
                   ALU.mult)
            dve.wait_ge(sem("k_turned"), 1)
            dve.wait_ge(sem("column_decays"), 1)
            for i in range(4):
                ts(kdec[:, i, :], ms[:, 2, i * P:(i + 1) * P], ekd[:, i:i + 1], None, ALU.mult)
                ts(kbg[:, i, :], ms[:, 3, i * P:(i + 1) * P], beta[:, 1, i:i + 1], ecum[:, i:i + 1], ALU.mult,
                   ALU.mult, "tokens_ready" if i == 3 else None)
            S.settle()
            for u in range(2):
                tt(XT[:, 4 * u:4 * u + 4, :], ident.unsqueeze(1).to_broadcast([P, 4, P]), Ml[0][:, 4 * u:4 * u + 4, :],
                   ALU.subtract, "X_ready")
            for l in range(1, LEVELS):
                for u in range(2):
                    dve.wait_ge(sem("MX_ready"), 2 * (l - 1) + u + 1)
                    S.did(dve.tensor_copy(Pm[:, 4 * u:4 * u + 4, :], ms[:, u, :].rearrange("p (j t) -> p j t", j=4)),
                          "MX_taken")
                if l + 1 < LEVELS:
                    tt(Ml[(l + 1) % 2], MT, level_mask(l + 1), ALU.mult, "corner_ready")
                for u in range(2):
                    sl = slice(4 * u, 4 * u + 4)
                    dve.wait_ge(sem("XMX_ready"), 2 * (l - 1) + u + 1)
                    tt(X[:, sl, :], X[:, sl, :], ms[:, u, :].rearrange("p (j t) -> p j t", j=4), ALU.subtract)
                    tt(XT[:, sl, :], XT[:, sl, :], ms[:, 2 + u, :].rearrange("p (j t) -> p j t", j=4), ALU.subtract,
                       "X_ready")
            dve.wait_ge(sem("vn0_ready"), 1)
            S.did(dve.tensor_copy(vn[0], mm[:, 0, :].rearrange("p (j t) -> p j t", j=4)), "vn0_taken")
            dve.wait_ge(sem("w_ready"), 1)
            ts(nwT, mm[:, 1, :].rearrange("p (j t) -> p j t", j=4), -1.0, None, ALU.mult, None, "w_taken")
            dve.wait_ge(sem("state_ready"), 1)
            S.did(dve.tensor_copy(S1, mm[:, 2, :].rearrange("p (j t) -> p j t", j=4)), "state_taken")
            dve.wait_ge(sem("vn1_ready"), 1)
            S.did(dve.tensor_copy(vn[1], mm[:, 0, :].rearrange("p (j t) -> p j t", j=4)), "vn1_taken")
            for u in range(8):
                ts(diag2[:, u, :], ident, imb[:, u % 2, u // 2:u // 2 + 1], None, ALU.mult, None,
                   "diag2_ready" if u == 7 else None)

            def head_norm(which, o, gain, gate, done, cut_o):
                dve.wait_ge(sem("head_sums"), which + 1)
                inv = scratch[:, 1024:2048]
                ts(inv, ms[:, 2:4, :].rearrange("p b n -> p (b n)"), 1.0 / P, EPS, ALU.mult, ALU.add)
                S.settle()
                S.did(dve.reciprocal(inv, inv), "head_inverse")
                tt(gate, gate, o, ALU.mult, done)
                dve.wait_ge(sem("head_rstd"), which + 1)
                S.settle()
                for i in range(4):
                    stt(o[:, i, :], gate[:, i, :], gain[i], inv[:, i * T:(i + 1) * T], ALU.mult, ALU.mult)
                cut_parts(cut_o[:, 0], cut_o[:, 1], o, done or "ob_done")

            head_norm(0, oa, [v("gdn_norm")] * 4, gz, "oa_done", oas)

            dve.wait_ge(sem("ml_rows_ready"), 1)
            for i in range(4):
                r = mm[:, 1 + i // 2, (i % 2) * T:(i % 2 + 1) * T]
                stt(Dlog[:, i, 0:P], r[:, 0:P], cum[:, 0, 4 + i:5 + i], cst("mask")[:, P:2 * P], ALU.add, ALU.add)
                stt(Dlog[:, i, P:3 * P], r, cum[:, 1, 4 + i:5 + i], cst("mask"), ALU.add, ALU.add,
                    "ml_rows_taken" if i == 3 else None)
            S.settle()
            S.did(dve.tensor_reduce(mx[:, 0, :], Dlog[:, :, 0:P], AX.X, ALU.max))
            S.did(dve.tensor_reduce(mx[:, 1, :], Dlog[:, :, P:3 * P], AX.X, ALU.max))
            S.settle()
            tt(mx, mx, cum[:, :, 4:8], ALU.max)
            S.settle()
            ts(nm, mx, -1.0, None, ALU.mult, None, "ml_nm")
            dve.wait_ge(sem("ml_weights"), 1)
            dve.wait_ge(sem("ml_qk_ready"), 1)
            for i in range(4):
                stt(Em[:, i, 0:P], ms[:, i, 0:P], 64.0 ** -0.5, Em[:, i, 0:P], ALU.mult, ALU.mult,
                    accum_out=den[:, 0, i:i + 1])
                stt(Em[:, i, P:3 * P], ms[:, i, P:3 * P], 64.0 ** -0.5, Em[:, i, P:3 * P], ALU.mult, ALU.mult,
                    accum_out=den[:, 1, i:i + 1])
            S.settle()
            ts(nden, den, -1.0, None, ALU.mult)
            S.settle()
            tt(nden, nden, den, ALU.max)
            S.settle()
            tt(nden, nden, flo, ALU.max)
            S.settle()
            S.did(dve.reciprocal(rden, nden))
            S.settle()
            for i in range(4):
                ts(Em[:, i, 0:P], Em[:, i, 0:P], rden[:, 0, i:i + 1], None, ALU.mult)
                ts(Em[:, i, P:3 * P], Em[:, i, P:3 * P], rden[:, 1, i:i + 1], None, ALU.mult, None,
                   "ml_scores" if i == 3 else None)
            head_norm(1, ob, [v("ml_norm", i, i + 1) for i in range(4)], mo, None, obs)

            def finish_mods(first, last, sums_, name):
                a_, b_ = 24 * first, 24 * last
                tt(mod[:, a_:b_], sums_, v("mod_b", a_, b_), ALU.add, name)
                S.settle()
                gains = modg[:, KD * first:KD * last]
                ts(gains.rearrange("p (i s) -> p i s", s=KD),
                   mod[:, a_:b_].rearrange("p (i s) -> p i s", s=24)[:, :, 8:16], 1.0, None, ALU.add)
                S.settle()
                tt(gains, gains, v("norms2", KD * first, KD * last), ALU.mult)

            dve.wait_ge(sem("mods_summed"), EARLY_MODS)
            finish_mods(0, MODS - 1, mm[:, 3, 0:24 * (MODS - 1)], "mods_taken")

            for j in range(8):
                n = OUT0["branch_a"] + j
                tt(gates[:, j, :], bank(n), gates[:, j, :], ALU.mult, taken(n))
            for j in range(8):
                n = OUT0["branch_b"] + j
                tt(gates[:, 8 + j, :], bank(n), gates[:, 8 + j, :], ALU.mult, taken(n))
                S.settle()
                tt(gates[:, j, :], gates[:, j, :], gates[:, 8 + j, :], ALU.add)
                cut_parts(mixs[:, 0, j, :], mixs[:, 1, j, :], gates[:, j, :], "mixed")

            def residual(stage, gate=None):
                for j in range(KD):
                    n = OUT0[stage] + j
                    src = bank(n)
                    if gate is None:
                        tt(x[:, j, :], src, x[:, j, :], ALU.add, taken(n))
                    else:
                        stt(x[:, j, :], src, gate[:, j:j + 1], x[:, j, :], ALU.mult, ALU.add, taken(n))
                S.settle()
                S.did(dve.memset(tiny[:, 511:512], 0.0), "x_done")

            residual("w_out")
            norm(1, v("g_ffn"))
            def add_last_mod(i):
                n = TILE_AT["last_mod", i]
                tile_ready(dve, n)
                sums_, k = last_sums[:, i // KD, :], i % KD
                if k == 0:
                    ts(sums_, ring[:, n % RAW, :], csilu[:, 0:1], None, ALU.mult, None, "mod_tiles_added")
                else:
                    S.settle()
                    stt(sums_, ring[:, n % RAW, :], csilu[:, k:k + 1], sums_, ALU.mult, ALU.add, "mod_tiles_added")

            for j in range(FFG):
                add_last_mod(j)
                out_taken(dve, OUT0["ffn_up"] + 2 * j)
                n = OUT0["ffn_up"] + 2 * j + 1
                src = bank(n)
                tt(ffact[:, j % 2, :], src, up[:, j % 2, :], ALU.mult, taken(n))
                cut_parts(ffs_[:, 0, j, :], ffs_[:, 1, j, :], ffact[:, j % 2, :], "ffact_cut")
            for i in range(FFG, 24):
                add_last_mod(i)
            residual("ffn_down")
            norm(2, v("g_ple"))
            dve.wait_ge(sem("last_mod_summed"), 1)
            finish_mods(MODS - 1, MODS, ms[:, 0, 0:24], "last_mod_taken")
            for j in range(KD):
                n = OUT0["ple"] + j
                out_taken(dve, OUT0["ple_gate"] + j)
                src = bank(n)
                tt(pleg[:, j, :], src, pleg[:, j, :], ALU.mult, taken(n))
            S.settle()
            tt(x[:, :, :], x[:, :, :], pleg, ALU.add, "x_done")
            norm(3, v("g_final"))

            c0, c1, c2, c3, c4, c5 = (lruc[:, i, :] for i in range(6))
            ts(c4, v("lam"), -1.0, None, ALU.mult)
            S.settle()
            tt(c0, c4, v("lam"), ALU.min, "nlam_ready")
            ts(c4, c4, 0.0, None, ALU.max)
            dve.wait_ge(sem("lam_exp"), 1)
            S.settle()
            ts(c2, c1, 2.0, None, ALU.add)
            S.settle()
            S.did(dve.reciprocal(c2, c2))
            S.settle()
            tt(c1, c1, c2, ALU.mult)
            S.settle()
            tt(c2, c1, c1, ALU.mult)
            S.settle()
            ts(c3, c2, 2.0 / 17, 2.0 / 15, ALU.mult, ALU.add)
            for d in (13, 11, 9, 7, 5, 3, 1):
                S.settle()
                tt(c3, c3, c2, ALU.mult)
                S.settle()
                ts(c3, c3, 2.0 / d, None, ALU.add)
            S.settle()
            tt(c3, c3, c1, ALU.mult)
            S.settle()
            tt(c3, c3, c4, ALU.add)
            S.settle()
            ts(c5, c3, 4.0, None, ALU.mult, None, "lru_rate")
            norm(4, modg[:, 0:8])
            S.did(dve.memset(lx[0:BLK, :, 0:3], 0.0), "lru_pad_zero")
            def lru_coefficients(j):
                dve.wait_ge(sem("lru_tanh"), j + 1)
                out_taken(dve, lru_out_of("ri", j))
                r_, i_, a_ = lr[0:BLK, j, :], li[0:BLK, j, :], lc[0:BLK, j, :]
                ts(r_, lt[0:BLK, j, :], 1.0, None, ALU.add, None, "lru_t_read")
                S.settle()
                S.did(dve.reciprocal(r_, r_))
                tt(i_, i_, a_, ALU.mult)
                S.settle()
                stt(i_, r_, 2.0, i_, ALU.mult, ALU.mult)
                ts(a_, r_, 2.0, -1.0, ALU.mult, ALU.add)

            for j in range(NBLK + 2):
                if j < NBLK:
                    out_taken(dve, lru_out_of("x", j))
                    w = v("lru_conv", 4 * j, 4 * j + 4, BLK)
                    ts(lc[0:BLK, j, :], lx[0:BLK, j, 0:T], w[:, 0:1], v("lru_conv_b", j, j + 1, BLK), ALU.mult, ALU.add)
                    for s in range(1, 4):
                        S.settle()
                        stt(lc[0:BLK, j, :], lx[0:BLK, j, s:s + T], w[:, s:s + 1], lc[0:BLK, j, :], ALU.mult, ALU.add,
                            "lru_conv" if s == 3 else None)
                if j >= 2:
                    lru_coefficients(j - 2)
            for j in range(NBLK + 1):
                if j < NBLK:
                    if j % 4 == 0:
                        dve.wait_ge(sem("lru_root"), j // 4 + 1)
                    S.settle()
                    tt(li[0:BLK, j, :], li[0:BLK, j, :], lt[0:BLK, j, :], ALU.mult)
                    S.settle()
                    S.did(dve.tensor_tensor_scan(lr[0:BLK, j, :], lc[0:BLK, j, :], li[0:BLK, j, :], 0.0, ALU.mult,
                                                 ALU.add))
                    S.settle()
                    tt(lt[0:BLK, j, :], lr[0:BLK, j, :], lg[0:BLK, j, :], ALU.mult, "lru_product")
                if j:
                    dve.wait_ge(sem("lru_high"), j)
                    tt(ys[0:BLK, 1, j - 1, :], lt[0:BLK, j - 1, :], ys[0:BLK, 0, j - 1, :].bitcast(F32), ALU.subtract,
                       "lru_y")
            residual("lru_out", mod[:, 16:24])

            def experts(L):
                i = 1 + 2 * L
                norm(5 + 2 * L, modg[:, 8 * i:8 * i + 8])
                for c in range(TT):
                    route_tile(L, c)
                for c in range(TT):
                    slot_weights(L, c)
                for c in range(TT):
                    out_taken(dve, OUT0[f"peer{L}_turn"] + c)
                n0 = OUT0[f"peer{L}_place"]

                def onehots(r, j):
                    dve.wait_ge(sem("outs"), r * 4 + (n0 + j - 2 + 1))
                    for k in range(4):
                        t = r * 16 + (4 * j + k)
                        dve.tensor_scalar(onehot[:, j % 2, 0, k, :], iota, routeT[:, 0, bass.ds(t, 1)],
                                          routeT[:, 2, bass.ds(t, 1)], ALU.is_equal, ALU.mult)
                    d = onehot[:, j % 2, 1, :, :]
                    dve.wait_ge(sem("key_distances"), r * 4 + (T // 4 * L + j + 1))
                    dve.tensor_scalar(d, d, 0.0, None, ALU.is_equal).then_inc(sem("onehots"), 1)

                def weigh_early(r, j):
                    dve.wait_ge(sem("place_copied"), r * 4 + (T // 4 * L + j + 1))
                    units = placed[:, 0:EARLY, bass.ds(r * 16 + 4 * j, 4)].rearrange("p e t -> p t e")
                    weights = mm[:, (n0 + j) % BANKS, :].rearrange("p (t e) -> p t e", t=4)[:, :, 0:EARLY]
                    dve.tensor_tensor(units, weights, units, ALU.mult).then_inc(sem(taken(n0 + j)[0]), 1)

                dve.wait_ge(sem("hidden_taken"), KEYS * L + EARLY)
                for j in range(4):
                    onehots(0, j)
                    if j >= 2:
                        weigh_early(0, j - 2)
                with dve.Fori(1, T // 16) as r:
                    for j in range(4):
                        onehots(r, j)
                        weigh_early(r, j - 2)
                for j in (2, 3):
                    weigh_early(T // 16 - 1, j)

                def cut_weighted(j, src, r, s_):
                    dve.wait_ge(sem("tiles_used"), r * UNROLL + (USED0[f"peer{L}_experts"] + s_ - 3 + 1))
                    dve.tensor_copy(wts[:, j % 3, 0, :], src).then_inc(sem("weighted_high"), 1)
                    dve.wait_ge(sem("weighted_high"), r * UNROLL + (KEYS * L + s_ + 1))
                    dve.tensor_tensor(wts[:, j % 3, 1, :], src, wts[:, j % 3, 0, :].bitcast(F32),
                                      ALU.subtract).then_inc(sem("weighted"), 1)

                def units(s_, r):
                    return placed[:, bass.ds(r * UNROLL + s_, 1), :].rearrange("p e t -> p (e t)")

                def weigh(j, r):
                    dve.wait_ge(sem("hidden_taken"), r * UNROLL + (KEYS * L + EARLY + j + 1))
                    dve.tensor_tensor(mix[:, j % 3, :], mix[:, j % 3, :], units(EARLY + j, r), ALU.mult) \
                        .then_inc(sem("hidden_weighted"), 1)
                    dve.wait_ge(sem("hidden_weighted"), r * UNROLL + ((KEYS - EARLY) * L + j + 1))
                    cut_weighted(j, mix[:, j % 3, :], r, EARLY + j)

                for j in range(BANKS):
                    out_taken(dve, n0 + T // 4 - 4 + j)
                with dve.Fori(0, EARLY // UNROLL) as r:
                    for j in range(UNROLL):
                        cut_weighted(j, units(j, r), r, j)
                last = (KEYS - EARLY) // UNROLL
                with dve.Fori(0, last) as r:
                    for j in range(UNROLL):
                        weigh(j, r)
                for j in range(KEYS - EARLY - last * UNROLL):
                    weigh(j, last)
                dve.wait_ge(sem("tiles_used"), USED0[f"peer{L}_experts"] + KEYS)
                for m in range(KD):
                    g = mod[:, 24 * i + 16 + m:24 * i + 17 + m]
                    stt(x[:, m, :], ms[:, m // 2, (m % 2) * T:(m % 2 + 1) * T], g, x[:, m, :], ALU.mult, ALU.add,
                        "x_done" if m == KD - 1 else None)

            def route_tile(L, c):
                for g in range(4):
                    out_taken(dve, OUT0[f"peer{L}_scores"] + 4 * c + g)
                if c or L:
                    S.settle()

                def best16(vals, idx, src, spare, count):
                    for rnd in range(2):
                        s = src if rnd == 0 else spare
                        lo, hi = 8 * rnd, 8 * rnd + 8
                        for j in range(count):
                            S.did(dve.max(vals(j)[:, lo:hi], s(j)))
                        S.settle()
                        for j in range(count):
                            S.did(dve.max_index(idx(j)[:, lo:hi], vals(j)[:, lo:hi], s(j)))
                        if rnd == 0:
                            for j in range(count):
                                S.did(dve.match_replace(spare(j), vals(j)[:, 0:8], src(j), LOWEST))
                            S.settle()
                    S.settle()

                best16(lambda j: top[:, j // 2, j % 2, :], lambda j: topi[:, j // 2, j % 2, :],
                       lambda j: es[:, c, j, :], lambda j: es2[:, j, :], 16)
                S.did(dve.tensor_copy(topf_flat, topi_flat))
                cand4 = cand.rearrange("p j (a b) -> p j a b", a=16)
                for j in range(PH):
                    tt(cand4[:, j], top[:, j, 0, :].unsqueeze(2).to_broadcast([P, 16, 16]),
                       top[:, j, 1, :].unsqueeze(1).to_broadcast([P, 16, 16]), ALU.add)
                S.settle()
                besti3 = besti.rearrange("p (j k) -> p j k", j=PH)
                best16(lambda j: best[:, j, :], lambda j: besti3[:, j, :],
                       lambda j: cand[:, j, :], lambda j: cand2[:, j, :], PH)
                ts(part[:, 0, :], besti, 4, None, ALU.logical_shift_right)
                ts(part[:, 1, :], besti, 15, None, ALU.bitwise_and)
                tt(shifted[:, c], best, best[:, :, 0:1].to_broadcast([P, PH, 16]), ALU.subtract, "best_shifted")
                S.settle()
                S.did(dve.tensor_copy(partf, part))
                S.settle()
                for s in range(2):
                    hot3 = hot.rearrange("p (q a) -> p q a", a=16)
                    tt(hot3, partf[:, s, :].unsqueeze(2).to_broadcast([P, P, 16]),
                       iota[:, 0:16].unsqueeze(1).to_broadcast([P, P, 16]), ALU.is_equal)
                    S.settle()
                    hot4 = hot.rearrange("p (j k a) -> p j k a", j=PH, k=16)
                    prod = hot2.rearrange("p (j k a) -> p j k a", j=PH, k=16)
                    for j in range(PH):
                        tt(prod[:, j], hot4[:, j], topf[:, j, s, :].unsqueeze(1).to_broadcast([P, 16, 16]), ALU.mult)
                    S.settle()
                    S.did(dve.tensor_reduce(route[:, c, s, :], hot2.rearrange("p (q a) -> p q a", a=16), AX.X,
                                            ALU.add))

            def slot_weights(L, c):
                dve.wait_ge(sem("best_exp"), TT * L + c + 1)
                S.settle()
                S.did(dve.tensor_reduce(sums, expo[:, c], AX.X, ALU.add))
                S.settle()
                S.did(dve.reciprocal(rsums, sums))
                S.settle()
                tt(route[:, c, 2, :].rearrange("p (j k) -> p j k", j=PH), expo[:, c],
                   rsums.unsqueeze(2).to_broadcast([P, PH, 16]), ALU.mult, "routed")

            experts(0)

            norm(6, modg[:, 16:24])
            n = OUT0["fox_small"]
            src = bank(n, width=32).rearrange("p (c j) -> p c j", c=TT)
            tt(ffz, src, v("fox_fb").unsqueeze(1).to_broadcast([P, TT, 16]), ALU.add, taken(n))
            S.settle()
            ts(ffs, ffz, -1.0, None, ALU.mult)
            S.settle()
            tt(ffn_, ffs, ffz, ALU.min, "fox_nz")
            ts(ffs, ffs, 0.0, None, ALU.max)
            dve.wait_ge(sem("fox_ln"), 1)
            S.settle()
            tt(ffs, ffs, ffl, ALU.add)
            S.settle()
            S.did(dve.memset(tiny[:, 509:510], 0.0), "fox_logf")
            n = OUT0["fox_cum"]
            S.did(dve.tensor_copy(fcum, bank(n, width=32).rearrange("p (c j) -> p c j", c=TT)), taken(n))
            S.settle()
            for hd in range(FH):
                for c in range(TT):
                    ts(fd[:, hd, c, :], ident, fcum[:, c, hd:hd + 1], None, ALU.mult, None,
                       "fox_diag" if hd == FH - 1 and c == TT - 1 else None)
            S.settle()
            ts(fcum, fcum, -1.0, None, ALU.mult)
            ts(fqg, v("fox_qg"), FE ** -0.5, None, ALU.mult)
            for s, f in enumerate((fq, fk)):
                for j in range(KD):
                    out_taken(dve, OUT0["fox_k" if s else "fox_q"] + j)
                tt(fsq[:, s * 2048:(s + 1) * 2048], f, f, ALU.mult, "fox_sq")
            for s, f in enumerate((fq, fk)):
                sq = fsq[:, s * 2048:(s + 1) * 2048]
                out_ready(dve, OUT0["fox_squares"] + 4 * s + 3)
                S.settle()
                for j in range(4):
                    n = OUT0["fox_squares"] + 4 * s + j
                    ts(sq[:, j * 512:(j + 1) * 512], bank(n, width=512), 1.0 / FE, EPS, ALU.mult, ALU.add, taken(n))
                S.settle()
                S.did(dve.reciprocal(sq, sq), "fox_inverse")
            for s, f in enumerate((fq, fk)):
                dve.wait_ge(sem("fox_rstd"), s + 1)
                stt(f, f, fqg if s == 0 else v("fox_kg"), fsq[:, s * 2048:(s + 1) * 2048], ALU.mult, ALU.mult,
                    "fox_normal")
            for i in range(FH + 4):
                if i < FH:
                    b = i % 3
                    n = OUT0[f"fox_scores{i}"]
                    src = bank(n, width=384)
                    if i >= 3:
                        dve.wait_ge(sem("fox_exp"), i - 2)
                    stt(fL[:, b, 0:P], src[:, 0:P], fcum[:, 0, i:i + 1], cst("mask")[:, P:2 * P], ALU.add, ALU.add)
                    stt(fL[:, b, P:3 * P], src[:, P:3 * P], fcum[:, 1, i:i + 1], cst("mask"), ALU.add, ALU.add, taken(n))
                    S.settle()
                    S.did(dve.tensor_reduce(fmx[:, b, 0:1], fL[:, b, 0:P], AX.X, ALU.max))
                    S.did(dve.tensor_reduce(fmx[:, b, 1:2], fL[:, b, P:3 * P], AX.X, ALU.max))
                    S.settle()
                    ts(fnm[:, b, :], fmx[:, b, :], -1.0, None, ALU.mult, None, "fox_max")
                if 1 <= i <= FH:
                    b = (i - 1) % 3
                    dve.wait_ge(sem("fox_exp"), i)
                    S.did(dve.reciprocal(frs[:, b, :], fsum[:, b, :]))
                    S.settle()
                    ts(fP[:, b, 0:P], fP[:, b, 0:P], frs[:, b, 0:1], None, ALU.mult)
                    ts(fP[:, b, P:3 * P], fP[:, b, P:3 * P], frs[:, b, 1:2], None, ALU.mult, None, "fox_probs")
                if i >= 5 and i % 2 == 1:
                    a = (i - 5) // 2
                    dve.wait_ge(sem("fox_pv"), 2 * a + 2)
                    tt(fy[:, a % 2, :], ms[:, a % 4, 0:T], fo[:, a, :], ALU.mult)
                    cut_parts(fys[:, 0, a, :], fys[:, 1, a, :], fy[:, a % 2, :], "fox_y")
            residual("fox_out", mod[:, 24 * 2 + 16:24 * 2 + 24])
            experts(1)


def host_constants():
    c = np.zeros((P, CONSTW), np.float32)
    i, j = np.arange(P)[:, None], np.arange(P)[None, :]

    def put(name, a):
        c[:, CONST0[name][0]:CONST0[name][1]] = a

    put("ident", i == j)
    put("upper", i <= j)
    put("ones", 1.0)
    put("heads", i // 64 == j // 64)
    put("iota", j + 0 * i)
    put("mask", np.concatenate([np.zeros((P, P)), np.where(j > i, -BIG, 0.0)], 1))
    put("maskT", np.where(j < i, BIG, 0.0))
    levels = []
    for l in range(LEVELS):
        b = 1 << l
        levels.append((i // (2 * b) == j // (2 * b)) & (i % (2 * b) >= b) & (j % (2 * b) < b))
    put("level0", levels[0])
    put("levelsT", np.concatenate([m.T for m in levels], 1))
    return c


def columns(w, groups=KD):
    k, n = w.shape
    wide = SLOT // groups
    return w.reshape(k // P // groups, groups, P, n // wide, wide).transpose(3, 0, 2, 1, 4).reshape(-1, P, SLOT)


def kernel(**inputs):
    import concourse.bacc as bacc
    from concourse.bass_utils import run_bass_kernel_spmd

    a = {k: np.asarray(val) for k, val in inputs.items()}
    w_in = a["w_in"][0]
    at = np.cumsum([0, 512, 512, 512, 512, 4, 4, 256, 256, 512, 512, 4, 4, 1024, 1024])
    gq, gk, gv, gz, gb, ga, mq, mk, mv, mo, mi, mf, ta, tb = (w_in[:, s:e] for s, e in zip(at[:-1], at[1:]))

    s = {}
    s["qkv"] = columns(np.concatenate([gq, gk, gv], 1))
    s["gz"] = columns(gz)
    s["mqk"] = columns(np.concatenate([mq, mk], 1))
    s["mv"] = columns(mv, 4)
    s["mo"] = columns(mo)
    s["gates"] = columns(np.concatenate([ta, tb], 1))
    mods = ["l0_mix", "l0_ffn", "l1_mix", "l1_ffn"]
    mod_tiles = np.concatenate([a[f"{m}_mod_w_2"].reshape(KD, P, 3, D).transpose(2, 0, 1, 3).reshape(3 * KD, P, D)
                                for m in mods], 0)
    s["mod"], s["last_mod"] = mod_tiles[:24 * (MODS - 1)], mod_tiles[24 * (MODS - 1):]
    s["branch_a"] = columns(a["w_branch_a"][0], 4)
    s["branch_b"] = columns(a["w_branch_b"][0], 4)
    s["w_out"] = columns(a["w_out"][0])
    both = np.stack([a["w1"][0].reshape(D, FFG, P), a["w3"][0].reshape(D, FFG, P)], 2).reshape(D, FFG * 256)
    s["ffn_up"] = columns(both)
    s["ffn_down"] = a["w2"][0].reshape(FFG, P, KD, P).transpose(2, 1, 0, 3).reshape(KD, P, FF)
    s["ple_gate"] = columns(a["w_ple_gate"][0])
    s["ple"] = columns(a["w_ple"][0], 2)
    s["lru_in"] = a["l0_lru_in_w_2"].reshape(KD, P, 2, NBLK, BLK).transpose(3, 2, 1, 0, 4).reshape(2 * NBLK, P, -1)
    lo = np.zeros((KD, 2, 96, 8, P), np.float32)
    lo[:, :, 0:BLK] = a["l0_lru_out_w_2"].reshape(2, 8, BLK, KD, P).transpose(3, 0, 2, 1, 4)
    s["lru_out"] = lo.reshape(2 * KD, 96, SLOT)
    fox = a["l1_fox_in_w_2"]
    s["fox_q"] = columns(fox[:, 0:D])
    s["fox_k"] = columns(fox[:, D:2 * D])
    s["fox_v"] = columns(fox[:, 2 * D:3 * D], 4)
    s["fox_og"] = columns(fox[:, 3 * D + FH:])
    s["fox_out"] = columns(a["l1_fox_out_w_2"])
    for L in range(2):
        s[f"peer{L}_q"] = columns(a[f"l{L}_peer_q_w_2"])
        keys = np.stack([a[f"l{L}_peer_subkey1_2"], a[f"l{L}_peer_subkey2_2"]], 1)
        s[f"peer{L}_keys"] = keys.reshape(2, PH // 2, 2, KEYS, P).transpose(0, 4, 1, 2, 3).reshape(2, P, SLOT)
        u = a[f"l{L}_peer_u_2"].reshape(KEYS, KEYS, KD, P).transpose(1, 3, 2, 0).reshape(KEYS, P, D)
        vv = a[f"l{L}_peer_v_2"].reshape(KEYS, KEYS, D).transpose(1, 0, 2)
        kinds = [expert_tile(i) for i in range(2 * KEYS)]
        s[f"peer{L}_experts"] = np.stack([(u if kind == "u" else vv)[step] for kind, step in kinds])

    def per_channel(w):
        return w.reshape(-1, P).T

    def blocks88(w):
        o = np.zeros((P, NBLK), np.float32)
        o[0:BLK] = w.reshape(NBLK, BLK).T
        return o

    vecs = np.zeros((P, VECW), np.float32)

    def put(name, w):
        vecs[:, VEC0[name][0]:VEC0[name][1]] = w

    put("g_mix", per_channel(a["g_mix"]))
    put("g_ffn", per_channel(a["g_ffn"]))
    put("g_ple", per_channel(a["g_ple"]))
    put("g_final", per_channel(a["g_final"]))
    put("gdn_norm", a["gdn_norm"][0][:, None])
    put("ml_norm", a["ml_norm"][0].T)
    put("conv", a["conv_w"][0].reshape(4, 12, P).transpose(2, 1, 0).reshape(P, 48))
    put("norms2", np.concatenate([per_channel(a[f"{m}_norm_g_2"]) for m in mods], 1))
    put("mod_b", np.concatenate([per_channel(a[f"{m}_mod_b_2"]) for m in mods], 1))
    put("c", per_channel(a["c_2"]))
    zero4 = np.zeros(4, np.float32)
    put("gate_bias", np.concatenate([zero4, a["dt_bias"][0], a["ml_i_bias"][0], a["ml_f_bias"][0]])[None, :])
    put("a_log", a["a_log"][0][None, :])
    lcw = np.zeros((P, NBLK, 4), np.float32)
    lcw[0:BLK] = a["l0_lru_conv_w_2"].reshape(4, NBLK, BLK).transpose(2, 1, 0)
    put("lru_conv", lcw.reshape(P, 64))
    put("lru_conv_b", blocks88(a["l0_lru_conv_b_2"]))
    put("ra_b", blocks88(a["l0_lru_ra_b_2"]))
    put("ri_b", blocks88(a["l0_lru_ri_b_2"]))
    put("lam", blocks88(a["l0_lru_lambda_2"]))
    put("fox_fb", a["l1_fox_f_b_2"][None, :])
    put("fox_qg", np.concatenate([a["l1_fox_q_norm_g_2"]] * 2)[:, None])
    put("fox_kg", np.concatenate([a["l1_fox_k_norm_g_2"]] * 2)[:, None])

    lgw = np.zeros((96, NBLK, 2, BLK), np.float32)
    lgw[0:BLK, :, 0] = a["l0_lru_ra_w_2"].transpose(1, 0, 2)
    lgw[0:BLK, :, 1] = a["l0_lru_ri_w_2"].transpose(1, 0, 2)

    arrays = {f"w_{name}": w for name, w in s.items()}
    arrays["xT"] = a["x"][0].T.reshape(KD, P, T).transpose(1, 0, 2)
    arrays["pT"] = a["p"][0, 0].T.reshape(2, P, T).transpose(1, 0, 2)
    arrays["consts"] = host_constants()
    arrays["vecs"] = vecs
    arrays["small_w"] = np.concatenate([gb, ga, mi, mf], 1).reshape(KD, P, 16).transpose(1, 0, 2)
    arrays["fox_f_w"] = fox[:, 3 * D:3 * D + FH].reshape(KD, P, 16).transpose(1, 0, 2)
    arrays["lru_gate_w"] = lgw
    arrays = {k: np.ascontiguousarray(w) for k, w in arrays.items()}

    nc = bacc.Bacc("TRN2", target_bir_lowering=False, num_devices=1, dynamic_dma_scratch_size=1024)
    dram = {k: nc.dram_tensor(k, list(w.shape), F32, kind="ExternalInput").ap() for k, w in arrays.items()}
    out = nc.dram_tensor("out", [P, KD, T], F32, kind="ExternalOutput").ap()
    build(nc, {name: dram[f"w_{name}"] for name in s}, *(dram[k] for k in (
        "xT", "pT", "consts", "vecs", "small_w", "fox_f_w", "lru_gate_w")), out)
    r = run_bass_kernel_spmd(nc, [arrays], core_ids=[0])
    y = r.results[0]["out"]
    return y.transpose(2, 1, 0).reshape(1, T, D)
```
